# Optimizing a Trainium2 kernel written in Bass

```python
import jax
import jax.numpy as jnp
from jax import lax
import numpy as np

D_MODEL = 1024
BATCH = 1
SEQ = 512
DEPTH = 2

CTX_LEN = 256
GRID_W = 64
NORM_EPS = 1e-6
ROPE_BASE = 10000.0
NEG_INF = -1e30
F32 = jnp.float32

M_HEADS = 4
M_HEAD_DIM = 128
M_WIDTH = M_HEADS * M_HEAD_DIM
M_CONV = 3
M_CHUNK = 64
M_FORGET_BIAS_LO = 3.0
M_FORGET_BIAS_HI = 6.0

A_HEADS = 8
A_KV_HEADS = 2
A_GROUP = A_HEADS // A_KV_HEADS
A_HEAD_DIM = 64
A_WIDTH = A_HEADS * A_HEAD_DIM
A_KV_WIDTH = A_KV_HEADS * A_HEAD_DIM
A_WINDOW = 128
A_BLOCK = 128

R_HEADS = 4
R_QK_DIM = 128
R_V_DIM = 256
R_QK_WIDTH = R_HEADS * R_QK_DIM
R_V_WIDTH = R_HEADS * R_V_DIM
R_CHUNK = 128

FFN_DIM = 2816
FFN_CONV = 3

IN_SPLITS = (M_WIDTH, M_WIDTH, M_WIDTH, M_WIDTH, 4 * M_HEADS,
             A_WIDTH, A_KV_WIDTH, A_KV_WIDTH,
             R_QK_WIDTH, R_QK_WIDTH, R_V_WIDTH, R_V_WIDTH,
             D_MODEL, D_MODEL, D_MODEL)
IN_COLS = sum(IN_SPLITS)

kernel_name = 'hybrid_mlstm_swa_retention_dit_block'

def _split_cols(w):
    offs = []
    acc = 0
    for s in IN_SPLITS[:-1]:
        acc += s
        offs.append(acc)
    return jnp.split(w, offs, axis=-1)

def _rmsnorm(x, w):
    xf = x.astype(F32)
    y = xf * lax.rsqrt(jnp.mean(xf * xf, axis=-1, keepdims=True) + NORM_EPS)
    return (y * w.astype(F32)).astype(x.dtype)

def _head_norm(y, w, n_heads, dt):
    shp = y.shape
    yf = y.astype(F32).reshape(shp[:-1] + (n_heads, shp[-1] // n_heads))
    mu = jnp.mean(yf, axis=-1, keepdims=True)
    var = jnp.mean(jnp.square(yf - mu), axis=-1, keepdims=True)
    yf = ((yf - mu) * lax.rsqrt(var + NORM_EPS)).reshape(shp)
    return (yf * w.astype(F32)).astype(dt)

def _modulation(cvec, w, b, n):
    return jnp.split(jax.nn.silu(cvec) @ w + b, n, axis=-1)

def _dwconv(x, w):
    K = w.shape[0]
    T = x.shape[1]
    r = K // 2
    xp = jnp.pad(x, ((0, 0), (r, r), (0, 0)))
    out = xp[:, 0:T] * w[0]
    for j in range(1, K):
        out = out + xp[:, j:j + T] * w[j]
    return out

def _rope_rotate(x, pos):
    half = x.shape[-1] // 2
    inv = ROPE_BASE ** (-jnp.arange(half, dtype=F32) / half)
    ang = pos.astype(F32)[:, None] * inv[None, :]
    cos = jnp.cos(ang)[None, :, None, :]
    sin = jnp.sin(ang)[None, :, None, :]
    xf = x.astype(F32)
    x1, x2 = xf[..., :half], xf[..., half:]
    return jnp.concatenate([x1 * cos - x2 * sin, x1 * sin + x2 * cos], axis=-1).astype(x.dtype)

def _axial_rope(x, row, col):
    half = x.shape[-1] // 2
    return jnp.concatenate([_rope_rotate(x[..., :half], row), _rope_rotate(x[..., half:], col)], axis=-1)

def _to_heads(t, n_heads):
    B, T, W = t.shape
    return t.reshape(B, T, n_heads, W // n_heads).transpose(0, 2, 1, 3)

def _from_heads(t):
    B, H, T, d = t.shape
    return t.transpose(0, 2, 1, 3).reshape(B, T, H * d)

def _flip(t):
    return jnp.flip(t, axis=2)

def _flip_opt(t):
    return None if t is None else _flip(t)

def _window_attention(q, k, v, kc, vc, sink):
    B, S, Hkv, G, hd = q.shape
    L = kc.shape[1]
    nb = S // A_BLOCK
    span = 3 * A_BLOCK
    scale = hd ** -0.5
    pad = ((0, 0), (A_BLOCK, A_BLOCK), (0, 0), (0, 0))
    kp = jnp.pad(k, pad).reshape(B, nb + 2, A_BLOCK, Hkv, hd)
    vp = jnp.pad(v, pad).reshape(B, nb + 2, A_BLOCK, Hkv, hd)
    kw = jnp.concatenate([kp[:, :nb], kp[:, 1:nb + 1], kp[:, 2:]], axis=2)
    vw = jnp.concatenate([vp[:, :nb], vp[:, 1:nb + 1], vp[:, 2:]], axis=2)
    qb = q.reshape(B, nb, A_BLOCK, Hkv, G, hd)
    blk = jnp.arange(nb)[:, None, None]
    qi = blk * A_BLOCK + jnp.arange(A_BLOCK)[None, :, None]
    kj = (blk - 1) * A_BLOCK + jnp.arange(span)[None, None, :]
    mask = (jnp.abs(qi - kj) <= A_WINDOW) & (kj >= 0) & (kj < S)
    sink_col = jnp.broadcast_to(sink[None, :, :, None, None], (B, Hkv, G, A_BLOCK, 1))

    def block(args):
        qx, kx, vx, mx = args
        s_loc = jnp.einsum('bqhgd,bkhd->bhgqk', qx, kx).astype(F32) * scale
        s_loc = jnp.where(mx[None, None, None], s_loc, NEG_INF)
        s_ctx = jnp.einsum('bqhgd,bchd->bhgqc', qx, kc).astype(F32) * scale
        p = jax.nn.softmax(jnp.concatenate([s_loc, s_ctx, sink_col], axis=-1), axis=-1).astype(vx.dtype)
        return (jnp.einsum('bhgqk,bkhd->bqhgd', p[..., :span], vx)
                + jnp.einsum('bhgqc,bchd->bqhgd', p[..., span:span + L], vc))

    out = lax.map(block, (jnp.moveaxis(qb, 1, 0), jnp.moveaxis(kw, 1, 0), jnp.moveaxis(vw, 1, 0), mask))
    return jnp.moveaxis(out, 0, 1).reshape(B, S, Hkv * G * hd)

def _context_attention(qc, kc, vc, sink):
    B, L, Hkv, G, hd = qc.shape
    s = jnp.einsum('bqhgd,bkhd->bhgqk', qc, kc).astype(F32) * (hd ** -0.5)
    sink_col = jnp.broadcast_to(sink[None, :, :, None, None], (B, Hkv, G, L, 1))
    p = jax.nn.softmax(jnp.concatenate([s, sink_col], axis=-1), axis=-1)[..., :L].astype(vc.dtype)
    return jnp.einsum('bhgqk,bkhd->bqhgd', p, vc).reshape(B, L, Hkv * G * hd)

def _mlstm_states(k, v, log_i, log_f, state0):
    B, H, T, dk = k.shape
    dv = v.shape[-1]
    N = T // M_CHUNK
    kc = k.reshape(B, H, N, M_CHUNK, dk)
    vc = v.reshape(B, H, N, M_CHUNK, dv)
    b = jnp.cumsum(log_f.reshape(B, H, N, M_CHUNK), axis=-1)
    g = b[..., -1]
    a = g[..., None] - b + log_i.reshape(B, H, N, M_CHUNK)

    def step(carry, xs):
        C, n, m = carry
        kx, vx, ax, gx = xs
        m_new = jnp.maximum(gx + m, jnp.max(ax, axis=-1))
        w = jnp.exp(ax - m_new[..., None])
        decay = jnp.exp(gx + m - m_new)
        C_new = decay[..., None, None] * C + jnp.einsum('bhlv,bhlk->bhvk', vx * w[..., None], kx)
        n_new = decay[..., None] * n + jnp.einsum('bhl,bhlk->bhk', w, kx)
        return (C_new, n_new, m_new), (C, n, m)

    xs = (jnp.moveaxis(kc, 2, 0), jnp.moveaxis(vc, 2, 0), jnp.moveaxis(a, 2, 0), jnp.moveaxis(g, 2, 0))
    final, starts = lax.scan(step, state0, xs)
    return starts, final, b

def _mlstm_outputs(q, k, v, log_i, b, starts):
    B, H, T, dk = q.shape
    dv = v.shape[-1]
    N = T // M_CHUNK
    C, n, m = [jnp.moveaxis(s_, 0, 2) for s_ in starts]
    qc = q.reshape(B, H, N, M_CHUNK, dk)
    kc = k.reshape(B, H, N, M_CHUNK, dk)
    vc = v.reshape(B, H, N, M_CHUNK, dv)
    ic = log_i.reshape(B, H, N, M_CHUNK)
    lower = jnp.tril(jnp.ones((M_CHUNK, M_CHUNK), dtype=bool))
    d_log = jnp.where(lower, b[..., :, None] - b[..., None, :] + ic[..., None, :], -jnp.inf)
    inter_log = b + m[..., None]
    m_j = jnp.maximum(inter_log, jnp.max(d_log, axis=-1))
    inter_w = jnp.exp(inter_log - m_j)
    s = jnp.einsum('bhnjd,bhnrd->bhnjr', qc, kc) * jnp.exp(d_log - m_j[..., None])
    num = (inter_w[..., None] * jnp.einsum('bhnvk,bhnjk->bhnjv', C, qc)
           + jnp.einsum('bhnjr,bhnrv->bhnjv', s, vc))
    den = inter_w * jnp.einsum('bhnk,bhnjk->bhnj', n, qc) + jnp.sum(s, axis=-1)
    h = num / jnp.maximum(jnp.abs(den), jnp.exp(-m_j))[..., None]
    return h.reshape(B, H, T, dv)

def _mlstm_dir(qc, kc, vc, ic, fc, qx, kx, vx, ix, fx):
    B, H, _, dk = kx.shape
    dv = vx.shape[-1]
    zero = (jnp.zeros((B, H, dv, dk), F32), jnp.zeros((B, H, dk), F32), jnp.zeros((B, H), F32))
    st_c, fin_c, b_c = _mlstm_states(kc, vc, ic, fc, zero)
    st_x, _, b_x = _mlstm_states(kx, vx, ix, fx, fin_c)
    hx = _mlstm_outputs(qx, kx, vx, ix, b_x, st_x)
    hc = None if qc is None else _mlstm_outputs(qc, kc, vc, ic, b_c, st_c)
    return hx, hc

def _mlstm_bidir(qc, kc, vc, gc, qx, kx, vx, gx):
    icf, fcf, icb, fcb = gc
    ixf, fxf, ixb, fxb = gx
    hx_f, hc_f = _mlstm_dir(qc, kc, vc, icf, fcf, qx, kx, vx, ixf, fxf)
    hx_b, hc_b = _mlstm_dir(_flip_opt(qc), _flip(kc), _flip(vc), _flip(icb), _flip(fcb),
                            _flip(qx), _flip(kx), _flip(vx), _flip(ixb), _flip(fxb))
    hx = _from_heads(hx_f + _flip(hx_b))
    hc = None if qc is None else _from_heads(hc_f + _flip(hc_b))
    return hx, hc

def _ret_states(k, v, log_g, state0):
    B, H, T, dk = k.shape
    dv = v.shape[-1]
    N = T // R_CHUNK
    kc = k.reshape(B, H, N, R_CHUNK, dk)
    vc = v.reshape(B, H, N, R_CHUNK, dv)
    pos = jnp.arange(R_CHUNK, dtype=F32)
    w = jnp.exp(log_g[:, None] * (R_CHUNK - 1.0 - pos)[None, :])
    chunk_decay = jnp.exp(log_g * R_CHUNK)

    def step(R, xs):
        kx, vx = xs
        R_new = (chunk_decay[None, :, None, None] * R
                 + jnp.einsum('bhlk,bhlv->bhkv', kx * w[None, :, :, None], vx))
        return R_new, R

    final, starts = lax.scan(step, state0, (jnp.moveaxis(kc, 2, 0), jnp.moveaxis(vc, 2, 0)))
    return starts, final

def _ret_outputs(q, k, v, log_g, starts):
    B, H, T, dk = q.shape
    dv = v.shape[-1]
    N = T // R_CHUNK
    qc = q.reshape(B, H, N, R_CHUNK, dk)
    kc = k.reshape(B, H, N, R_CHUNK, dk)
    vc = v.reshape(B, H, N, R_CHUNK, dv)
    R = jnp.moveaxis(starts, 0, 2)
    pos = jnp.arange(R_CHUNK, dtype=F32)
    diff = pos[:, None] - pos[None, :]
    decay = jnp.where(diff >= 0, jnp.exp(log_g[:, None, None] * jnp.maximum(diff, 0.0)), 0.0)
    s = jnp.einsum('bhnjd,bhnrd->bhnjr', qc, kc) * decay[None, :, None]
    inter = jnp.exp(log_g[:, None] * (pos + 1.0)[None, :])
    out = (jnp.einsum('bhnjr,bhnrv->bhnjv', s, vc)
           + inter[None, :, None, :, None] * jnp.einsum('bhnjk,bhnkv->bhnjv', qc, R))
    return out.reshape(B, H, T, dv)

def _ret_dir(qc, kc, vc, qx, kx, vx, log_g):
    B, H, _, dk = kx.shape
    dv = vx.shape[-1]
    st_c, fin_c = _ret_states(kc, vc, log_g, jnp.zeros((B, H, dk, dv), F32))
    st_x, _ = _ret_states(kx, vx, log_g, fin_c)
    hx = _ret_outputs(qx, kx, vx, log_g, st_x)
    hc = None if qc is None else _ret_outputs(qc, kc, vc, log_g, st_c)
    return hx, hc

def _ret_bidir(qc, kc, vc, qx, kx, vx, log_g):
    hx_f, hc_f = _ret_dir(qc, kc, vc, qx, kx, vx, log_g[0])
    hx_b, hc_b = _ret_dir(_flip_opt(qc), _flip(kc), _flip(vc), _flip(qx), _flip(kx), _flip(vx), log_g[1])
    hx = _from_heads(hx_f + _flip(hx_b))
    hc = None if qc is None else _from_heads(hc_f + _flip(hc_b))
    return hx, hc

def _token_mixer(h, hc, row, col, w_in, m_gate_bias, m_conv_w, m_norm_w, a_sink, ret_logit, ret_norm_w,
                 w_br_m, w_br_a, w_br_r, w_out, need_ctx):
    dt = h.dtype
    B, S, _ = h.shape
    L = hc.shape[1]
    (w_mq, w_mk, w_mv, w_mo, w_mg, w_aq, w_ak, w_av,
     w_rq, w_rk, w_rv, w_rg, w_gm, w_ga, w_gr) = _split_cols(w_in)
    conv_q, conv_k = m_conv_w[:, :M_WIDTH], m_conv_w[:, M_WIDTH:]

    def m_q(t):
        return _to_heads(jax.nn.silu(_dwconv(t @ w_mq, conv_q)), M_HEADS).astype(F32)

    def m_k(t):
        return _to_heads(jax.nn.silu(_dwconv(t @ w_mk, conv_k)), M_HEADS).astype(F32) * (M_HEAD_DIM ** -0.5)

    def m_v(t):
        return _to_heads(t @ w_mv, M_HEADS).astype(F32)

    def m_gates(t):
        Bt, Tt, _ = t.shape
        g = (t @ w_mg + m_gate_bias).astype(F32).reshape(Bt, Tt, 4, M_HEADS).transpose(2, 0, 3, 1)
        return (g[0], jax.nn.log_sigmoid(g[1]), g[2], jax.nn.log_sigmoid(g[3]))

    hm_x, hm_c = _mlstm_bidir(m_q(hc) if need_ctx else None, m_k(hc), m_v(hc), m_gates(hc),
                              m_q(h), m_k(h), m_v(h), m_gates(h))

    sink = a_sink.astype(F32).reshape(A_KV_HEADS, A_GROUP)
    q = _axial_rope((h @ w_aq).reshape(B, S, A_HEADS, A_HEAD_DIM), row, col)
    q = q.reshape(B, S, A_KV_HEADS, A_GROUP, A_HEAD_DIM)
    k = _axial_rope((h @ w_ak).reshape(B, S, A_KV_HEADS, A_HEAD_DIM), row, col)
    v = (h @ w_av).reshape(B, S, A_KV_HEADS, A_HEAD_DIM)
    kc = (hc @ w_ak).reshape(B, L, A_KV_HEADS, A_HEAD_DIM)
    vc = (hc @ w_av).reshape(B, L, A_KV_HEADS, A_HEAD_DIM)
    ya = _window_attention(q, k, v, kc, vc, sink)

    log_g = jax.nn.log_sigmoid(ret_logit.astype(F32))
    pos_c = jnp.arange(L)
    pos_x = L + jnp.arange(S)

    def r_qk(t, w, pos, scale):
        Bt, Tt, _ = t.shape
        r = _rope_rotate((t @ w).reshape(Bt, Tt, R_HEADS, R_QK_DIM), pos)
        return r.transpose(0, 2, 1, 3).astype(F32) * scale

    def r_v(t):
        return _to_heads(t @ w_rv, R_HEADS).astype(F32)

    k_scale = R_QK_DIM ** -0.5
    hr_x, hr_c = _ret_bidir(r_qk(hc, w_rq, pos_c, 1.0) if need_ctx else None, r_qk(hc, w_rk, pos_c, k_scale),
                            r_v(hc), r_qk(h, w_rq, pos_x, 1.0), r_qk(h, w_rk, pos_x, k_scale), r_v(h), log_g)

    def mlstm_out(t, hm):
        return jax.nn.sigmoid(t @ w_mo) * _head_norm(hm, m_norm_w, M_HEADS, dt)

    def ret_out(t, hr):
        return jax.nn.silu(t @ w_rg) * _head_norm(hr, ret_norm_w, R_HEADS, dt)

    def merge(t, ym_, ya_, yr_):
        return (jax.nn.sigmoid(t @ w_gm) * (ym_ @ w_br_m)
                + jax.nn.sigmoid(t @ w_ga) * (ya_ @ w_br_a)
                + jax.nn.sigmoid(t @ w_gr) * (yr_ @ w_br_r)) @ w_out

    y = merge(h, mlstm_out(h, hm_x), ya, ret_out(h, hr_x))
    if need_ctx:
        qcx = (hc @ w_aq).reshape(B, L, A_KV_HEADS, A_GROUP, A_HEAD_DIM)
        ya_c = _context_attention(qcx, kc, vc, sink)
        yc = merge(hc, mlstm_out(hc, hm_c), ya_c, ret_out(hc, hr_c))
    else:
        yc = None
    return y, yc

def _conv_ffn(h, w_up, conv_w, conv_b, w_down):
    a, b = jnp.split(h @ w_up, 2, axis=-1)
    return (jax.nn.silu(_dwconv(a, conv_w) + conv_b) * b) @ w_down

def setup_inputs(seed: int = 0) -> dict:
    key = jax.random.key(seed)
    ks = jax.random.split(key, 24)
    D = D_MODEL

    def nrm(k, shape, scale):
        return jax.random.normal(k, shape, F32) * scale

    lin = jnp.linspace(M_FORGET_BIAS_LO, M_FORGET_BIAS_HI, M_HEADS, dtype=F32)
    zer = jnp.zeros((M_HEADS,), F32)
    gate_base = jnp.concatenate([zer, lin, zer, lin])
    ret_base = jnp.log(2.0 ** (5.0 + jnp.arange(R_HEADS, dtype=F32)) - 1.0)
    return {
        'x': nrm(ks[0], (BATCH, SEQ, D), 1.0),
        'c': nrm(ks[1], (BATCH, D), 1.0),
        'ctx': nrm(ks[2], (BATCH, CTX_LEN, D), 1.0),
        'c_ctx': nrm(ks[3], (D,), 1.0),
        'mod_w': nrm(ks[4], (DEPTH, D, 6 * D), 0.5 * D ** -0.5),
        'mod_b': nrm(ks[5], (DEPTH, 6 * D), 0.02),
        'norm1_w': 1.0 + nrm(ks[6], (DEPTH, D), 0.02),
        'norm2_w': 1.0 + nrm(ks[7], (DEPTH, D), 0.02),
        'w_in': nrm(ks[8], (DEPTH, D, IN_COLS), D ** -0.5),
        'm_gate_bias': gate_base[None, :] + nrm(ks[9], (DEPTH, 4 * M_HEADS), 0.1),
        'm_conv_w': nrm(ks[10], (DEPTH, M_CONV, 2 * M_WIDTH), M_CONV ** -0.5),
        'm_norm_w': 1.0 + nrm(ks[11], (DEPTH, M_WIDTH), 0.02),
        'a_sink': nrm(ks[12], (DEPTH, A_HEADS), 0.5),
        'ret_logit': ret_base[None, None, :] + nrm(ks[13], (DEPTH, 2, R_HEADS), 0.1),
        'ret_norm_w': 1.0 + nrm(ks[14], (DEPTH, R_V_WIDTH), 0.02),
        'w_br_m': nrm(ks[15], (DEPTH, M_WIDTH, D), M_WIDTH ** -0.5),
        'w_br_a': nrm(ks[16], (DEPTH, A_WIDTH, D), A_WIDTH ** -0.5),
        'w_br_r': nrm(ks[17], (DEPTH, R_V_WIDTH, D), R_V_WIDTH ** -0.5),
        'w_out': nrm(ks[18], (DEPTH, D, D), D ** -0.5),
        'ffn_up': nrm(ks[19], (DEPTH, D, 2 * FFN_DIM), D ** -0.5),
        'ffn_conv_w': nrm(ks[20], (DEPTH, FFN_CONV, FFN_DIM), FFN_CONV ** -0.5),
        'ffn_conv_b': nrm(ks[21], (DEPTH, FFN_DIM), 0.02),
        'ffn_down': nrm(ks[22], (DEPTH, FFN_DIM, D), FFN_DIM ** -0.5),
        'final_norm_w': 1.0 + nrm(ks[23], (D,), 0.02),
    }

def reference(x, c, ctx, c_ctx, mod_w, mod_b, norm1_w, norm2_w, w_in, m_gate_bias, m_conv_w, m_norm_w,
              a_sink, ret_logit, ret_norm_w, w_br_m, w_br_a, w_br_r, w_out, ffn_up, ffn_conv_w, ffn_conv_b,
              ffn_down, final_norm_w):
    S = x.shape[1]
    rows = S // GRID_W
    row = jnp.repeat(jnp.arange(rows), GRID_W)
    col = jnp.tile(jnp.arange(GRID_W), rows)
    cx = ctx
    for l in range(DEPTH):
        last = l == DEPTH - 1
        sh1, sc1, g1, sh2, sc2, g2 = [t[:, None, :] for t in _modulation(c, mod_w[l], mod_b[l], 6)]
        if last:
            csh1, csc1 = _modulation(c_ctx, mod_w[l][:, :2 * D_MODEL], mod_b[l][:2 * D_MODEL], 2)
        else:
            csh1, csc1, cg1, csh2, csc2, cg2 = _modulation(c_ctx, mod_w[l], mod_b[l], 6)
        h = _rmsnorm(x, norm1_w[l]) * (1.0 + sc1) + sh1
        hc = _rmsnorm(cx, norm1_w[l]) * (1.0 + csc1) + csh1
        y, yc = _token_mixer(h, hc, row, col, w_in[l], m_gate_bias[l], m_conv_w[l], m_norm_w[l], a_sink[l],
                             ret_logit[l], ret_norm_w[l], w_br_m[l], w_br_a[l], w_br_r[l], w_out[l],
                             not last)
        x = x + g1 * y
        h2 = _rmsnorm(x, norm2_w[l]) * (1.0 + sc2) + sh2
        x = x + g2 * _conv_ffn(h2, ffn_up[l], ffn_conv_w[l], ffn_conv_b[l], ffn_down[l])
        if not last:
            cx = cx + cg1 * yc
            hc2 = _rmsnorm(cx, norm2_w[l]) * (1.0 + csc2) + csh2
            cx = cx + cg2 * _conv_ffn(hc2, ffn_up[l], ffn_conv_w[l], ffn_conv_b[l], ffn_down[l])
    return _rmsnorm(x, final_norm_w)


_drawn_inputs = setup_inputs


def setup_inputs(seed=0):
    import zlib

    import numpy as np

    out = dict(_drawn_inputs(seed))
    spreads = {}
    factors = {'norm1_w': 8.0,
     'norm2_w': 6.404,
     'm_norm_w': 64.0,
     'a_sink': 8.0,
     'ret_norm_w': 8.0,
     'ffn_conv_b': 8.0,
     'final_norm_w': 8.339,
     'm_conv_w': 2.761}
    for name, (base, spread) in spreads.items():
        noise = np.random.default_rng([zlib.crc32(name.encode()), seed]).standard_normal(out[name].shape)
        drawn = base * np.exp(spread * noise) if base else spread * noise
        out[name] = jnp.asarray(drawn.astype(out[name].dtype))
    for name, factor in factors.items():
        out[name] = (out[name] * factor).astype(out[name].dtype)
    return out
```

```python
from contextlib import ExitStack

import numpy as np
import concourse.bass as bass
from concourse import mybir

F32, F32R = mybir.dt.float32, mybir.dt.float32r
ALU, ACT, AX = mybir.AluOpType, mybir.ActivationFunctionType, mybir.AxisListType

P = 128
D, SEQ, CTX, DEPTH, GRID_W = 1024, 512, 256, 2, 64
KD = D // P
TILES, CT = (SEQ + CTX) // P, CTX // P
TOK = SEQ + CTX
MH, AH, AKV, RH, RV = 4, 8, 2, 4, 256
AD = 64
FFN = 2816
FT = FFN // P
GROUP = 4
URING = 6
EPS = 1e-6
NEG = -1e30
COLS = 256
SLOT = KD * COLS
PADDED = TOK + 4
BACK = [1, 0, 5, 4, 3, 2]
M_SCALE = 0.25 * P ** -0.5
R_SCALE = P ** -0.5
IN_OFF = dict(mq=0, mk=512, mv=1024, mo=1536, mg=2048, aq=2064, ak=2576, av=2704, rq=2832, rk=3344,
              rv=3856, rg=4880, gm=5904, ga=6928, gr=7952)


def at_tile(t):
    return 1 + P * t + (2 if t >= CT else 0)


def constants():
    r, j = np.meshgrid(np.arange(P), np.arange(P), indexing="ij")
    rot = np.zeros((P, P), np.float32)
    for m in range(P):
        if m % 32 < 16:
            rot[m + 16, m] = -1.0
        else:
            rot[m - 16, m] = 1.0
    window = np.concatenate([np.where(j >= r, 0.0, NEG), np.zeros((P, P)), np.where(j <= r, 0.0, NEG)], 1)
    parts = dict(
        ident=np.eye(P), upto=(r <= j), since=(r >= j), ones=np.ones((P, P)),
        hide_f=np.where(r <= j, 0.0, NEG), hide_b=np.where(r >= j, 0.0, NEG), window=window,
        ahead=np.maximum(j - r, 0), behind=np.maximum(r - j, 0), row_f=j + 1, row_b=P - j,
        col_f=127 - r[:, :1], col_b=r[:, :1], rot=rot, flip=np.eye(P)[::-1],
        neg_half=np.full((P, 1), -0.5), one=np.ones((P, 1)), cd=np.full((P, 1), float(P)))
    place, cols = {}, []
    n = 0
    for k, v in parts.items():
        place[k] = (n, n + v.shape[1])
        cols.append(v.astype(np.float32))
        n += v.shape[1]
    f = np.float32
    inv16 = (f(10000.0) ** (-np.arange(16, dtype=f) / f(16))).astype(f)
    t = np.arange(SEQ)
    ang = np.zeros((P, SEQ), f)
    for m in range(P):
        pos = (t // GRID_W) if m % 64 < 32 else (t % GRID_W)
        ang[m] = pos.astype(f) * inv16[m % 16]
    rope_a = np.stack([np.cos(ang), np.sin(ang)], 1).astype(f)
    inv64 = (f(10000.0) ** (-np.arange(64, dtype=f) / f(64))).astype(f)
    ang = np.arange(TOK).astype(f)[None, :] * inv64[np.arange(P) % 64][:, None]
    sign = np.where(np.arange(P) < 64, -1.0, 1.0)[:, None]
    rope_r = np.stack([np.cos(ang), np.sin(ang) * sign], 1).astype(f)
    return np.concatenate(cols, 1), place, rope_a, rope_r


def param_places():
    sizes = [("mod_b", 48), ("norm1", 8), ("norm2", 8), ("conv_q", 12), ("conv_k", 12), ("m_norm", 4),
             ("r_norm", 8), ("f_conv", 3 * FT), ("f_bias", FT), ("sink", AH), ("ret", 2 * RH), ("gate", 16)]
    place, n = {}, 0
    for k, s in sizes:
        place[k] = (n, s)
        n += s
    return place, n


def make_plan():
    plan, stream, bank, split = [], [], [0], [0]

    def slot(l, blocks, kt=KD, splits=True):
        s = dict(n=len(stream), l=l, blocks=blocks, kt=kt, cols=sum(b[1] for b in blocks[2]), sp=None)
        if splits:
            s["sp"] = split[0]
            split[0] += 1
        stream.append(s)
        return s

    def step(kind, slot=None, banks=0, **k):
        if not k.get("ctx", True):
            banks = {"mqk": 3, "rqk": 3, "aq": 2, "up": 2, "mvo": 3, "rowgate": 1}.get(kind, 2)
        k.update(kind=kind, slot=slot, bank=bank[0])
        bank[0] += banks
        plan.append(k)

    def seqs(ctx):
        return ((0, 0, CTX), (1, CTX, SEQ)) if ctx else ((1, CTX, SEQ),)

    def pairs(ctx):
        return (0, 1, 2) if ctx else (1, 2)

    def cols(name, l, c0, n=COLS, kt=KD, row=0, splits=True):
        return slot(l, (name, row, [(c0, n)]), kt, splits)

    def vectors(l, which):
        for n in ((0, 1, 2, 3, 4, 5, 6, 7) if which == 0 else (12, 13, 14, 15, 16, 17, 18, 19)):
            step("vector", cols("mod_w", l, n * COLS, splits=False), 1, l=l, n=n)
        step("affine", l=l, which=which)

    def rows(l, which, ctx):
        for n in range(4):
            c0 = (2 if which == 0 else 5) * D + n * COLS
            step("rowgate", cols("mod_w", l, c0, splits=False), 1, l=l, which=which, n=n, ctx=ctx, c0=c0)

    gen = 0
    step("setup")
    for l in range(DEPTH):
        ctx = l < DEPTH - 1
        if l == 0:
            vectors(0, 0)
            step("region", name="norm")
            for t in range(TILES):
                step("norm", l=0, use="first", t=t, gen=gen)
        h = gen
        step("region", name="mlstm")
        o = IN_OFF
        step("mgates", slot(l, ("w_in", 0, [(o["mg"], 16)])), 3, l=l, gen=h)
        for hd in range(MH):
            step("mqk", slot(l, ("w_in", 0, [(o["mq"] + hd * P, P), (o["mk"] + hd * P, P)])), 4, l=l, gen=h,
                 hd=hd, ctx=ctx)
            step("mvo", slot(l, ("w_in", 0, [(o["mv"] + hd * P, P), (o["mo"] + hd * P, P)])), 3, l=l, gen=h,
                 hd=hd, ctx=ctx)
            for t in range(TILES):
                step("mktok", l=l, hd=hd, t=t)
            for s in range(TILES - 1):
                step("mback", l=l, hd=hd, s=s)
            for t in range(TILES):
                step("mtile", l=l, hd=hd, t=t, out=ctx or t >= CT)
        step("region", name="branch")
        branch(step, cols, l, ctx, "m", h, pairs)
        step("region", name="attn")
        for g in range(2):
            blocks = [(o["aq"] + (2 * g + i + 4 * half) * AD, AD) for i in range(2) for half in range(2)]
            step("aq", slot(l, ("w_in", 0, blocks)), 4, l=l, gen=h, g=g, ctx=ctx)
        step("akv", slot(l, ("w_in", 0, [(o["ak"], P), (o["av"], P)])), 5, l=l, gen=h)
        for t in range(0 if ctx else CT, TILES):
            for hd in range(AH):
                step("ahead", l=l, t=t, hd=hd)
            step("aout", l=l, t=t)
        step("region", name="branch")
        branch(step, cols, l, ctx, "a", h, pairs)
        step("region", name="ret")
        for hd in range(RH):
            step("rqk", slot(l, ("w_in", 0, [(o["rq"] + hd * P, P), (o["rk"] + hd * P, P)])), 4, l=l, gen=h,
                 hd=hd, ctx=ctx)
            step("rv", cols("w_in", l, o["rv"] + hd * RV), 3, l=l, gen=h, hd=hd)
            step("rg", cols("w_in", l, o["rg"] + hd * RV), 3, l=l, gen=h, hd=hd, ctx=ctx)
            for t in range(TILES):
                step("rktok", l=l, hd=hd, t=t)
            for s in range(TILES - 1):
                step("rback", l=l, hd=hd, s=s)
            for t in range(TILES):
                step("rtile", l=l, hd=hd, t=t, out=ctx or t >= CT)
        step("region", name="branch")
        branch(step, cols, l, ctx, "r", h, pairs)
        step("region", name="norm")
        first = 0 if ctx else CT
        gen += 1
        for t in range(first, TILES):
            step("turn", l=l, t=t, gen=gen)
        for n in range(4):
            step("wout", cols("w_out", l, n * COLS), 3, l=l, gen=gen, n=n, ctx=ctx)
        vectors(l, 1)
        rows(l, 0, ctx)
        gen += 1
        for t in range(first, TILES):
            step("norm", l=l, use="mid", t=t, gen=gen)
        rows(l, 1, ctx)
        step("region", name="mlp")
        if ctx:
            vectors(l + 1, 0)
        down = 0
        for u in range(FT):
            step("up", slot(l, ("ffn_up", 0, [(u * P, P), (FFN + u * P, P)])), 4, l=l, gen=gen, u=u, ctx=ctx)
            if u >= GROUP and u % GROUP == 0 or u == FT - 1:
                while down * GROUP < FT and (down + 1) * GROUP <= u or (u == FT - 1 and down * GROUP < FT):
                    kt = min(GROUP, FT - down * GROUP)
                    for half in range(2):
                        step("down", slot(l, ("ffn_down", down * GROUP * P, [(half * 512, 512)]), kt),
                             TILES - first, l=l, g=down, half=half, kt=kt, first=first)
                    down += 1
        last = l == DEPTH - 1
        step("region", name="final" if last else "norm")
        gen += 1
        for t in range(first, TILES):
            step("norm", l=l, use="last" if last else "end", t=t, gen=gen)
    order, done = [], 0
    for st in plan:
        if st["slot"] is not None:
            while done < min(st["slot"]["n"] + 2, len(stream)):
                if stream[done]["sp"] is not None:
                    order.append(dict(kind="split", slot=stream[done]))
                done += 1
        order.append(st)
    annotate(order)
    return order, stream


MIXING = ("norm", "turn", "mgates", "aq", "akv", "mktok", "mback", "mtile", "ahead", "aout", "rktok",
          "rback", "rtile")


def annotate(order):
    last, norms, head_end, downs, stored = {}, [], {}, {}, {}
    for i, st in enumerate(order):
        kind = st["kind"]
        st["i"] = i
        st["prev"] = last.get("mixing")
        st["region"] = last.get("region")
        st["h_slot"] = last.get("h")
        st["prev_branch"] = last.get("branch")
        st["last_norm"] = last.get("norm")
        if kind in MIXING:
            last["mixing"] = i
        if kind in ("region", "branch", "norm"):
            last[kind] = i
        if st.get("gen") is not None and st["slot"] is not None:
            last["h"] = st["slot"]["n"]
        if kind[0] in "mr" and "hd" in st:
            st["prev_head"] = head_end.get((kind[0], st["l"], st["hd"] - 1))
            if kind in ("mtile", "rtile"):
                head_end[kind[0], st["l"], st["hd"]] = i
        if kind == "ahead":
            last["ahead"] = st["buf"] = 1 - last.get("ahead", 1)
        if kind == "down":
            for u in range(st["g"] * GROUP, st["g"] * GROUP + st["kt"]):
                downs[st["l"], u] = st["slot"]["n"]
        if kind == "up":
            st["ring_free"] = downs.get((st["l"], st["u"] - URING))
        if kind == "norm":
            st["id"] = len(norms)
            st["buf"] = len(norms) % 2
            st["before"] = norms[-1] if norms else None
            st["before2"] = norms[-2] if len(norms) > 1 else None
            st["back"] = stored.get(st["t"])
            if st["use"] in ("mid", "end"):
                stored[st["t"]] = st["id"]
            norms.append(st)
        if kind == "region":
            st["stores"] = [n["id"] for n in norms[-2:] if n["use"] in ("mid", "end")]


def branch(step, cols, l, ctx, which, h, pairs):
    name = {"m": "w_br_m", "a": "w_br_a", "r": "w_br_r"}[which]
    gate = {"m": "gm", "a": "ga", "r": "gr"}[which]
    kt = 8 if which == "r" else 4
    for n in range(4):
        step("gate", cols("w_in", l, IN_OFF[gate] + n * COLS), 3, l=l, gen=h, br=which, n=n, ctx=ctx)
        step("branch", cols(name, l, n * COLS, kt=kt, splits=False), 3, l=l, br=which, n=n, ctx=ctx, kt=kt)


class Events:

    def __init__(self, known, sems):
        self.known, self.sems, self.count, self.now = known, sems, {}, {}

    def mark(self, sem, *key, by=1):
        self.count[sem] = self.count.get(sem, 0) + by
        self.now.setdefault(key, {})[sem] = self.count[sem]
        return self.sems(sem), by

    def at(self, *key):
        if self.known is None:
            return self.sems("dry_run"), 1
        (sem, value), = self.known[key].items()
        return self.sems(sem), value

    def last(self, sem):
        return self.sems(sem), self.count.get(sem, 0)


def backbone(nc, ins, out, known, stop=None):
    consts_np, CP, _, _ = constants()
    PP, NPAR = param_places()
    PLAN, STREAM = make_plan()
    if stop is not None:
        PLAN = PLAN[:stop]
        used = {id(s["slot"]) for s in PLAN if s["slot"] is not None}
        STREAM = [s for s in STREAM if id(s) in used]
    seqs = {True: ((0, 0, CTX), (1, CTX, SEQ)), False: ((1, CTX, SEQ),)}

    with ExitStack() as ctx:
        semaphores = {}

        def semaphore(name):
            if name not in semaphores:
                semaphores[name] = ctx.enter_context(nc.semaphore(name))
            return semaphores[name]

        ev = Events(known, semaphore)

        def sb(name, shape, dt=F32):
            return ctx.enter_context(nc.sbuf_tensor(name, shape, dt))

        psg = ctx.enter_context(nc.psum_tensor("psum_products", [P, 4, 512], F32))
        psm = ctx.enter_context(nc.psum_tensor("psum_mixers", [P, 4, 512], F32))
        hh = sb("h_head", [P, KD, TOK], F32R)
        hl = sb("h_rest", [P, KD, TOK], F32R)
        acc = sb("acc", [P, TILES, D])
        raw = sb("raw", [P, 2, SLOT])
        wh = sb("w_head", [P, 2, SLOT], F32R)
        wl = sb("w_rest", [P, 2, SLOT], F32R)
        const = sb("const", [P, consts_np.shape[1]])
        par = sb("par", [P, DEPTH, NPAR])
        cvec = sb("cvec", [P, 3, KD, 2])
        vec = sb("vec", [P, 4 * KD, 2])
        aff = sb("aff", [P, 2, 2, KD, 2])
        small = sb("small", [P, 96])
        arena_size = 71 * 1024
        arena = sb("arena", [P, arena_size // 4])

        class Region:

            def __init__(self, start=0):
                self.off = start

            def __call__(self, name, shape, dt=F32):
                n = int(np.prod(shape[1:])) * 4
                t = nc.alloc_sbuf_tensor_at(name, shape, dt, offset=ARENA + self.off)
                self.off += -(-n // 32) * 32
                assert self.off <= arena_size, (name, self.off)
                return t

        ARENA = arena_offset(nc, arena)
        R = Region()
        gate_b = R("gate_b", [P, 2, D])
        stage = R("stage", [P, 2, D])
        bias_b = R("bias_b", [P, D])
        xs = R("xs", [P, D])
        hf = R("hf", [P, KD, P])
        R = Region(8 * 1024)
        uh = R("u_head", [P, URING, TOK], F32R)
        ul = R("u_rest", [P, URING, TOK], F32R)
        fa = R("f_a", [P, 2, PADDED])
        fc = R("f_c", [P, PADDED])
        ft = R("f_t", [P, TOK])
        fb = R("f_b", [P, TOK])
        fu = R("f_u", [P, TOK])
        R = Region()
        yT = R("yT", [P, 8, TOK])
        R = Region(12 * 1024)
        gm = R("gm", [P, 12, 48])
        g16 = R("g16", [P, TILES, 16])
        atr = R("atr", [P, 4, P])
        ma = R("m_a", [P, 2, PADDED])
        mc = R("m_c", [P, 2, PADDED])
        mt = R("m_t", [P, 2, PADDED])
        mqk = R("m_qk", [P, 2, PADDED])
        mktok = R("m_ktok", [P, TILES, P])
        mv = R("m_v", [P, TILES, P + 1])
        mo = R("m_o", [P, TILES, P])
        mcb = R("m_cb", [P, TILES, P + 1])
        mcf = R("m_cf", [P, 2, P + 1])
        mvw = R("m_vw", [P, 2, P + 1])
        msc = R("m_sc", [P, 4, P])
        mnd = R("m_nd", [P, 4, P + 1])
        my = R("m_y", [P, 3, P])
        R = Region(12 * 1024)
        ropea = R("rope_a", [P, 2, SEQ])
        aq = R("a_q", [P, 4, TOK])
        ak = R("a_k", [P, TOK])
        av = R("a_v", [P, TILES, P])
        atmp = R("a_tmp", [P, SEQ])
        asb = R("a_s", [P, 2, 640])
        apt = R("a_pt", [P, 2, 640])
        ay = R("a_y", [P, 2, 512])
        R = Region(24 * 1024)
        roper = R("rope_r", [P, 2, TOK])
        rqk = R("r_qk", [P, 2, TOK])
        rtmp = R("r_tmp", [P, TOK])
        rktok = R("r_ktok", [P, TILES, P])
        rv = R("r_v", [P, TILES, RV])
        rg = R("r_g", [P, TILES, RV])
        rt = R("r_t", [P, RV])
        rb = R("r_b", [P, TILES, RV])
        rf = R("r_f", [P, 2, RV])
        rvw = R("r_vw", [P, 2, RV])
        rs = R("r_s", [P, 3, P])
        rd = R("r_d", [P, 3, P])
        ry = R("r_y", [P, 2, RV])
        R = Region(24 * 1024)
        tg = R("tg", [P, TILES, COLS])
        bt = R("bt", [P, 2, 512])

        def c(name):
            a, b = CP[name]
            return const[:, a:b]

        def pr(l, name, i=0, n=1):
            return par[:, l, PP[name][0] + i:PP[name][0] + i + n]

        res = nc.dram_tensor("residual", (TILES, P, D), F32, kind="Internal").ap()

        def raw_of(s):
            return raw[:, s["n"] % 2, 0:s["kt"] * s["cols"]].rearrange("p (k c) -> p k c", k=s["kt"])

        def halves(s):
            n = s["kt"] * s["cols"]
            a = wh[:, s["sp"] % 2, 0:n].rearrange("p (k c) -> p k c", k=s["kt"])
            b = wl[:, s["sp"] % 2, 0:n].rearrange("p (k c) -> p k c", k=s["kt"])
            return a, b

        def banks_a(st):
            out_, n = [], st["bank"]
            for ct in range(2):
                if st["kind"] == "akv" and ct == 1:
                    continue
                both = st.get("ctx", True) or st["kind"] in ("mqk", "rqk") and ct == 1
                for q in seqs[both]:
                    out_.append((n, ct, q))
                    n += 1
            return out_

        def banks_b(st):
            n = st["bank"] + (2 if st["kind"] == "akv" else 0)
            both = st.get("ctx", True) or st["kind"] == "mvo"
            return [(n + i, (2 * p_, 2 * p_ + 1)) for i, p_ in enumerate((0, 1, 2) if both else (1, 2))]

        block = ctx.enter_context(nc.Block())

        def walk(name):
            for i, st in enumerate(PLAN):
                yield i, st
                ev.now[name + "_step", i] = {name: ev.count.get(name, 0)}

        def phase_end(eng, i):
            for name in ("pe", "act", "dve", "pool"):
                eng.wait_ge(*ev.at(name + "_step", i - 1))
            for n in PLAN[i]["stores"]:
                eng.wait_ge(*ev.at("stored", n))

        @block.sync
        def _(sp):
            sp.dma_start(const[:], ins["consts"]).then_inc(*ev.mark("const_in", "const", by=16))
            sp.dma_start(par[:], ins["params"]).then_inc(*ev.mark("par_in", "par", by=16))
            sp.dma_start(cvec[:, 0], ins["cvec"]).then_inc(*ev.mark("cvec_in", "cvec", by=16))
            loaded = 0
            offs = np.cumsum([0] + [s["kt"] * s["cols"] * P for s in STREAM])
            order = {id(s): i for i, s in enumerate(STREAM)}

            def load(i):
                s = STREAM[i]
                if i >= 2:
                    sp.wait_ge(*ev.at("raw_free", STREAM[i - 2]["n"]))
                n = s["kt"] * s["cols"]
                src = ins["stream"][int(offs[i]):int(offs[i]) + n * P].rearrange("(p c) -> p c", p=P)
                sp.dma_start(raw[:, s["n"] % 2, 0:n], src).then_inc(
                    *ev.mark(f"raw{s['n'] % 2}_in", "raw", s["n"], by=16))

            for i, st in enumerate(PLAN):
                kind = st["kind"]
                s = st["slot"]
                if s is not None:
                    while loaded < min(order[id(s)] + (1 if kind == "split" else 2), len(STREAM)):
                        load(loaded)
                        loaded += 1
                if kind == "region":
                    if st["name"] == "attn":
                        phase_end(sp, i)
                        sp.dma_start(ropea[:], ins["rope_a"]).then_inc(*ev.mark("rope_in", "rope", i, by=16))
                    if st["name"] == "ret":
                        phase_end(sp, i)
                        sp.dma_start(roper[:], ins["rope_r"]).then_inc(*ev.mark("rope_in", "rope", i, by=16))
                    if st["name"] in ("norm", "final"):
                        phase_end(sp, i)
                    if st["name"] == "final":
                        sp.dma_start(bias_b[:], ins["final_w"].broadcast_to((P, D))).then_inc(
                            *ev.mark("fnorm_in", "fnorm", by=16))
                if kind == "rowgate" and st["n"] == 0:
                    if st["which"]:
                        sp.wait_ge(*ev.at("bias_free", st["l"], 0))
                    a = st["c0"]
                    b_ = ins["mod_b"][st["l"]:st["l"] + 1, a:a + D].broadcast_to((P, D))
                    sp.dma_start(bias_b[:], b_).then_inc(
                        *ev.mark("bias_in", "bias", st["l"], st["which"], by=16))
                if kind == "norm":
                    l, t, use = st["l"], st["t"], st["use"]
                    if st["before2"] is not None:
                        b2 = st["before2"]
                        if b2["use"] != "last":
                            sp.wait_ge(*ev.at("xs", b2["id"]))
                        if b2["use"] != "first":
                            sp.wait_ge(*ev.at("stored", b2["id"]))
                    if use == "first":
                        src = ins["ctx"][0, t * P:(t + 1) * P, :] if t < CT else \
                            ins["x"][0, (t - CT) * P:(t - CT + 1) * P, :]
                    elif l == 0 and use == "mid":
                        src = ins["ctx"][0, t * P:(t + 1) * P, :] if t < CT else \
                            ins["x"][0, (t - CT) * P:(t - CT + 1) * P, :]
                    else:
                        sp.wait_ge(*ev.at("stored", st["back"]))
                        src = res[t]
                    sp.dma_start(stage[:, st["buf"]], src).then_inc(
                        *ev.mark(f"stage{st['buf']}_in", "stage", st["id"], by=16))

        def akeys(t):
            return ([*range(max(CT, t - 1), min(TILES, t + 2))] if t >= CT else []) + [0, 1]

        @block.tensor
        def _(pe):
            def mm(o, a, b, start=True, stop=True):
                return nc.tensor.matmul(o, a, b, start=start, stop=stop)

            def three(o, wa, ha, kts, w_first):
                last = None
                for i, k in enumerate(kts):
                    for j, (a, b) in enumerate(((0, 0), (1, 0), (0, 1))):
                        w, h = wa[a](k), ha[b](k)
                        x, y = (w, h) if w_first else (h, w)
                        last = mm(o, x, y, i == 0 and j == 0, i == len(kts) - 1 and j == 2)
                return last

            def free_bank(n):
                if n >= 4:
                    pe.wait_ge(*ev.at("bank_free", n - 4))

            def part_a(st):
                w = halves(st["slot"])
                for n, ct, (q, t0, size) in banks_a(st):
                    free_bank(n)
                    for t in range(t0 // P, (t0 + size) // P):
                        pe.wait_ge(*ev.at("h", st["gen"], t))
                    wa = [lambda k, x=x: x[:, k, ct * P:(ct + 1) * P] for x in w]
                    ha = [lambda k, x=x: x[:, k, t0:t0 + size] for x in (hh, hl)]
                    three(psg[:, n % 4, 0:size], wa, ha, range(KD), True).then_inc(*ev.mark("pe", "bank", n))

            def part_b(st, c0, cn):
                w = halves(st["slot"])
                for n, tt in banks_b(st):
                    free_bank(n)
                    for i, t in enumerate(tt):
                        pe.wait_ge(*ev.at("h", st["gen"], t))
                        wa = [lambda k, x=x: x[:, k, c0:c0 + cn] for x in w]
                        ha = [lambda k, x=x: x[:, k, t * P:(t + 1) * P] for x in (hh, hl)]
                        last = three(psg[:, n % 4, i * 256:i * 256 + cn], wa, ha, range(KD), False)
                    last.then_inc(*ev.mark("pe", "bank", n))

            pe.wait_ge(*ev.at("const"))
            for i, st in walk("pe"):
                kind, s = st["kind"], st["slot"]
                l, hd, t = st.get("l"), st.get("hd"), st.get("t")
                if kind == "split":
                    continue
                if kind in MIXING:
                    if st["prev"] is not None:
                        pe.wait_ge(*ev.at("act_step", st["prev"]))
                        pe.wait_ge(*ev.at("dve_step", st["prev"]))
                        pe.wait_ge(*ev.at("pool_step", st["prev"]))
                if s is not None:
                    if s["sp"] is not None:
                        pe.wait_ge(*ev.at("rest", s["n"]))
                    else:
                        pe.wait_ge(*ev.at("raw", s["n"]))
                if kind == "vector":
                    pe.wait_ge(*ev.at("silu_c"))
                    free_bank(st["bank"])
                    w = raw_of(s)
                    for ct in range(2):
                        for k in range(KD):
                            last = mm(psg[:, st["bank"] % 4, 2 * ct:2 * ct + 2], w[:, k, ct * P:(ct + 1) * P],
                                      cvec[:, 2, k, :], k == 0, k == KD - 1)
                    last.then_inc(*ev.mark("pe", "bank", st["bank"]))
                elif kind == "rowgate":
                    free_bank(st["bank"])
                    w = raw_of(s)
                    for q in ((0, 1) if st["ctx"] else (1,)):
                        for k in range(KD):
                            last = mm(psg[:, st["bank"] % 4, q * 256:q * 256 + 256],
                                      cvec[:, 2, k, q:q + 1].broadcast_to((P, P)), w[:, k, :], k == 0, k == KD - 1)
                    last.then_inc(*ev.mark("pe", "bank", st["bank"]))
                elif kind == "norm":
                    if st["use"] == "last":
                        continue
                    for half in range(2):
                        pe.wait_ge(*ev.at("xs", st["id"]))
                        for k in range(4):
                            kk = half * 4 + k
                            last = nc.tensor.transpose(psm[:, half, k * P:(k + 1) * P], xs[:, kk * P:(kk + 1) * P],
                                                       c("ident"))
                        last.then_inc(*ev.mark("pe", "xT", st["id"], half))
                elif kind == "turn":
                    for half in range(2):
                        if st["prev_branch"] is not None:
                            pe.wait_ge(*ev.at("pool_step", st["prev_branch"]))
                            pe.wait_ge(*ev.at("dve_step", st["prev_branch"]))
                        for k in range(4):
                            kk = half * 4 + k
                            last = nc.tensor.transpose(psm[:, half + 2 * (t % 2), k * P:(k + 1) * P],
                                                       acc[:, t, kk * P:(kk + 1) * P], c("ident"))
                        last.then_inc(*ev.mark("pe", "turned", l, t, half))
                elif kind == "mgates":
                    part_b(st, 0, 16)
                    pe.wait_ge(*ev.at("logf", l))
                    mm(psm[:, 3, 0:24], c("upto"), gm[:, 2, 0:24])
                    mm(psm[:, 3, 24:48], c("since"), gm[:, 2, 24:48])
                    mm(psm[:, 3, 48:96], c("ones"), gm[:, 2, :]).then_inc(*ev.mark("pe", "sums", l))
                    pe.wait_ge(*ev.at("A", l))
                    mm(psm[0:24, 2, 0:P], gm[:, 4, 0:24], c("ident"))
                    mm(psm[0:24, 2, P:2 * P], gm[:, 4, 24:48], c("flip")).then_inc(*ev.mark("pe", "AT", l))
                    pe.wait_ge(*ev.at("scan", l))
                    mm(psm[:, 1, 0:24], atr[0:24, 2, :], c("ident")[0:24, 0:24])
                    mm(psm[:, 1, 24:48], atr[0:24, 3, :], c("ident")[0:24, 0:24]).then_inc(*ev.mark("pe", "LM", l))
                    pe.wait_ge(*ev.at("LMb", l))
                    mm(psm[:, 1, 48:72], c("flip"), gm[:, 5, 24:48]).then_inc(*ev.mark("pe", "LMf", l))
                elif kind in ("mqk", "rqk", "aq", "up"):
                    part_a(st)
                    if kind == "aq":
                        for ct in range(2):
                            pe.wait_ge(*ev.at("araw", l, st["g"], ct))
                            mm(psm[:, ct, 0:SEQ], c("rot"), aq[:, 2 * st["g"] + ct, CTX:TOK]).then_inc(
                                *ev.mark("pe", "arot", l, st["g"], ct))
                elif kind == "akv":
                    part_a(st)
                    part_b(st, P, P)
                    pe.wait_ge(*ev.at("araw", l, 2, 0))
                    mm(psm[:, 0, 0:SEQ], c("rot"), ak[:, CTX:TOK]).then_inc(*ev.mark("pe", "arot", l, 2, 0))
                elif kind in ("mvo", "rv", "rg", "gate", "wout"):
                    part_b(st, 0, COLS)
                elif kind == "branch":
                    w = raw_of(s)
                    for n, tt in banks_b(st):
                        free_bank(n)
                        for j, t_ in enumerate(tt):
                            pe.wait_ge(*ev.at("yT", l, st["br"], t_))
                            for k in range(st["kt"]):
                                last = mm(psg[:, n % 4, j * 256:j * 256 + 256], yT[:, k, t_ * P:(t_ + 1) * P],
                                          w[:, k, :], k == 0, k == st["kt"] - 1)
                        last.then_inc(*ev.mark("pe", "bank", n))
                elif kind == "down":
                    w = halves(s)
                    for j, t_ in enumerate(range(st["first"], TILES)):
                        n = st["bank"] + j
                        free_bank(n)
                        pe.wait_ge(*ev.at("u", l, st["g"] * GROUP + st["kt"] - 1))
                        wa = [lambda k, x=x: x[:, k, :] for x in w]
                        ha = [lambda k, x=x: x[:, (st["g"] * GROUP + k) % URING, t_ * P:(t_ + 1) * P]
                              for x in (uh, ul)]
                        three(psg[:, n % 4, :], wa, ha, range(st["kt"]), False).then_inc(
                            *ev.mark("pe", "bank", n))
                elif kind == "mktok":
                    pe.wait_ge(*ev.at("mqk", l, hd))
                    a = at_tile(t)
                    nc.tensor.transpose(psm[:, 3, (t % 4) * P:(t % 4 + 1) * P], mqk[:, 1, a:a + P],
                                        c("ident")).then_inc(*ev.mark("pe", "ktokT", l, hd, t))
                elif kind == "mback":
                    pe.wait_ge(*ev.at("mvw", l, hd, "b", st["s"]))
                    pe.wait_ge(*ev.at("mkt", l, hd, BACK[st["s"]]))
                    mm(psm[:, 2, 258:258 + P + 1], mktok[:, BACK[st["s"]], :], mvw[:, st["s"] % 2, :]).then_inc(
                        *ev.mark("pe", "mkv", l, hd, "b", st["s"]))
                elif kind == "mtile":
                    a = at_tile(t)
                    if t < TILES - 1:
                        pe.wait_ge(*ev.at("mvw", l, hd, "f", t))
                        mm(psm[:, 2, 258:258 + P + 1], mktok[:, t, :], mvw[:, t % 2, :]).then_inc(
                            *ev.mark("pe", "mkv", l, hd, "f", t))
                    if st["out"]:
                        pe.wait_ge(*ev.at("mcols", l))
                        mm(psm[:, 0, 0:P], mqk[:, 1, a:a + P], mqk[:, 0, a:a + P])
                        for d in range(2):
                            s_ = t if d == 0 else BACK.index(t)
                            col = d * 24 + s_ * 4 + hd
                            last = mm(psm[:, 0, (1 + d) * P:(2 + d) * P], gm[:, 9, col:col + 1].broadcast_to((P, P)),
                                      c("ident"))
                        last.then_inc(*ev.mark("pe", "mscore", l, hd, t))
                        pe.wait_ge(*ev.at("mC", l, hd, "f", t))
                        pe.wait_ge(*ev.at("mC", l, hd, "b", BACK.index(t)))
                        mm(psm[:, 2, 0:P + 1], mqk[:, 0, a:a + P], mcf[:, t % 2, :])
                        mm(psm[:, 2, P + 1:2 * (P + 1)], mqk[:, 0, a:a + P], mcb[:, BACK.index(t), :]).then_inc(
                            *ev.mark("pe", "minter", l, hd, t))
                        pe.wait_ge(*ev.at("mw", l, hd, t))
                        pe.wait_ge(*ev.at("mv", l, hd, t // 2))
                        mm(psm[:, 1, 0:P + 1], msc[:, 2, :], mv[:, t, :])
                        mm(psm[:, 1, P + 1:2 * (P + 1)], msc[:, 3, :], mv[:, t, :]).then_inc(
                            *ev.mark("pe", "mintra", l, hd, t))
                    if st["out"]:
                        pe.wait_ge(*ev.at("my", l, hd, t))
                        nc.tensor.transpose(psm[:, 3, 0:P], my[:, 2, :], c("ident")).then_inc(
                            *ev.mark("pe", "myT", l, hd, t))
                elif kind == "ahead":
                    i_, half = hd % 4, hd // 4
                    lo, hi = half * 64, half * 64 + 64
                    b0 = 0
                    pe.wait_ge(*ev.at("arope", l))
                    q_ = aq[lo:hi, i_, t * P:(t + 1) * P]
                    if t >= CT:
                        k0, k1 = max(CT, t - 1), min(TILES, t + 2)
                        mm(psm[:, b0, 0:(k1 - k0) * P], q_, ak[lo:hi, k0 * P:k1 * P])
                    mm(psm[:, b0 + 1, 0:CTX], q_, ak[lo:hi, 0:CTX]).then_inc(*ev.mark("pe", "ascore", l, t, hd))
                    keys = akeys(t)
                    pe.wait_ge(*ev.at("ap", l, t, hd))
                    for j, kt_ in enumerate(keys):
                        bk, cc = (2, j * P) if j < 4 else (3, 0)
                        last = nc.tensor.transpose(psm[:, bk, cc:cc + P], asb[:, st["buf"], j * P:(j + 1) * P],
                                                   c("ident"))
                    last.then_inc(*ev.mark("pe", "apT", l, t, hd))
                    pe.wait_ge(*ev.at("apt", l, t, hd))
                    for j, kt_ in enumerate(keys):
                        last = mm(psm[:, 3, 128:192], apt[:, st["buf"], j * P:(j + 1) * P],
                                  av[:, kt_, lo:hi], j == 0, j == len(keys) - 1)
                    last.then_inc(*ev.mark("pe", "apv", l, t, hd))
                elif kind == "aout":
                    pe.wait_ge(*ev.at("ay", l, t, AH - 1))
                    for j in range(4):
                        last = nc.tensor.transpose(psm[:, 1, j * P:(j + 1) * P], ay[:, t % 2, j * P:(j + 1) * P],
                                                   c("ident"))
                    last.then_inc(*ev.mark("pe", "ayT", l, t))
                elif kind == "rktok":
                    pe.wait_ge(*ev.at("rqk", l, hd))
                    nc.tensor.transpose(psm[:, 3, (t % 4) * P:(t % 4 + 1) * P], rqk[:, 1, t * P:(t + 1) * P],
                                        c("ident")).then_inc(*ev.mark("pe", "rktokT", l, hd, t))
                elif kind == "rback":
                    pe.wait_ge(*ev.at("rvw", l, hd, "b", st["s"]))
                    pe.wait_ge(*ev.at("rkt", l, hd, BACK[st["s"]]))
                    mm(psm[:, 2, 0:RV], rktok[:, BACK[st["s"]], :], rvw[:, st["s"] % 2, :]).then_inc(
                        *ev.mark("pe", "rkv", l, hd, "b", st["s"]))
                elif kind == "rtile":
                    if st["out"]:
                        mm(psm[:, 0, 0:P], rqk[:, 1, t * P:(t + 1) * P], rqk[:, 0, t * P:(t + 1) * P]).then_inc(
                            *ev.mark("pe", "rscore", l, hd, t))
                        pe.wait_ge(*ev.at("rR", l, hd, "f", t))
                        pe.wait_ge(*ev.at("rR", l, hd, "b", BACK.index(t)))
                        pe.wait_ge(*ev.at("rs", l, hd, t))
                        pe.wait_ge(*ev.at("rq", l, hd, t))
                        mm(psm[:, 1, 0:RV], rs[:, 0, :], rv[:, t, :], True, False)
                        mm(psm[:, 1, 0:RV], rs[:, 1, :], rf[:, t % 2, :], False, False)
                        mm(psm[:, 1, 0:RV], rs[:, 2, :], rb[:, BACK.index(t), :], False, True).then_inc(
                            *ev.mark("pe", "rout", l, hd, t))
                    if t < TILES - 1:
                        pe.wait_ge(*ev.at("rvw", l, hd, "f", t))
                        mm(psm[:, 2, 0:RV], rktok[:, t, :], rvw[:, t % 2, :]).then_inc(
                            *ev.mark("pe", "rkv", l, hd, "f", t))
                    if st["out"]:
                        pe.wait_ge(*ev.at("ry", l, hd, t))
                        for j in range(2):
                            last = nc.tensor.transpose(psm[:, 3, j * P:(j + 1) * P], ry[:, 1, j * P:(j + 1) * P],
                                                       c("ident"))
                        last.then_inc(*ev.mark("pe", "ryT", l, hd, t))
                if s is not None:
                    ev.now[("w_free", s["n"])] = {"pe": ev.count["pe"]}
                    if s["sp"] is not None:
                        ev.now[("w_free_sp", s["sp"])] = {"pe": ev.count["pe"]}
                    if s["sp"] is None:
                        ev.now[("raw_free", s["n"])] = {"pe": ev.count["pe"]}

        @block.scalar
        def _(act):
            act.wait_ge(*ev.at("cvec"))
            nc.scalar.activation(cvec[:, 1], cvec[:, 0], ACT.Tanh, scale=0.5).then_inc(*ev.mark("act", "tanh_c"))
            act.wait_ge(*ev.at("par"))
            act.wait_ge(*ev.at("const"))
            for i, st in walk("act"):
                kind, s = st["kind"], st["slot"]
                l, hd, t = st.get("l"), st.get("hd"), st.get("t")
                if kind == "region":
                    phase_end(act, i)
                if kind == "split":
                    n = s["kt"] * s["cols"]
                    act.wait_ge(*ev.at("raw", s["n"]))
                    if s["sp"] >= 2:
                        act.wait_ge(*ev.at("w_free_sp", s["sp"] - 2))
                    nc.scalar.activation(wh[:, s["sp"] % 2, 0:n], raw[:, s["n"] % 2, 0:n], ACT.Copy).then_inc(*ev.mark("act", "head", s["n"]))
                elif kind == "norm":
                    act.wait_ge(*ev.at(*(("stage", st["id"]) if st["use"] == "first" else ("rsum", st["id"]))))
                    if st["before"] is not None and st["before"]["use"] != "last":
                        act.wait_ge(*ev.at("xT", st["before"]["id"], 1))
                    nc.scalar.activation(xs[:], stage[:, st["buf"]], ACT.Square, accum_out=small[:, 0:1]).then_inc(*ev.mark("act", "ss", st["id"]))
                    if st["use"] in ("mid", "end"):
                        act.dma_start(res[t], stage[:, st["buf"]]).then_inc(
                            *ev.mark(f"store{st['buf']}", "stored", st["id"], by=16))
                    if st["use"] == "last":
                        act.wait_ge(*ev.at("outrow", st["id"]))
                        act.dma_start(out[0, (t - CT) * P:(t - CT + 1) * P, :], stage[:, st["buf"]]).then_inc(
                            *ev.mark(f"out{st['buf']}", "stored", st["id"], by=16))
                        continue
                    act.wait_ge(*ev.at("rstd", st["id"]))
                    act.wait_ge(*ev.last("act"))
                    nc.scalar.activation(xs[:], stage[:, st["buf"]], ACT.Copy, scale=small[:, 2:3]).then_inc(*ev.mark("act", "xs", st["id"]))
                    if st["h_slot"] is not None:
                        act.wait_ge(*ev.at("w_free", st["h_slot"]))
                    act.wait_ge(*ev.at("hf", st["id"]))
                    ts = slice(t * P, (t + 1) * P)
                    nc.scalar.activation(hh[:, :, ts], hf[:], ACT.Copy).then_inc(*ev.mark("act", "hh", st["id"]))
                elif kind == "turn":
                    for half in range(2):
                        act.wait_ge(*ev.at("turned", l, t, half))
                        if half == 0:
                            act.wait_ge(*ev.at("w_free", st["h_slot"]))
                        nc.scalar.activation(hh[:, half * 4:half * 4 + 4, t * P:(t + 1) * P], psm[:, half + 2 * (t % 2), :].rearrange("p (k c) -> p k c", k=4), ACT.Copy).then_inc(*ev.mark("act", "turn_hh", l, t, half))
                elif kind == "mgates":
                    act.wait_ge(*ev.at("Fx", l))
                    nc.scalar.activation(gm[:, 1, :], gm[:, 0, :], ACT.Abs).then_inc(*ev.mark("act", "absf", l))
                    act.wait_ge(*ev.last("act"))
                    nc.scalar.activation(gm[:, 3, :], gm[:, 1, :], ACT.Exp, scale=-1.0).then_inc(*ev.mark("act", "expf", l))
                    act.wait_ge(*ev.last("act"))
                    nc.scalar.activation(gm[:, 1, :], gm[:, 3, :], ACT.Ln, bias=c("one")).then_inc(*ev.mark("act", "lnf", l))
                    act.wait_ge(*ev.at("mlogs", l))
                    nc.scalar.activation(gm[:, 6:9, :], gm[:, 6:9, :], ACT.Exp).then_inc(*ev.mark("act", "mexp1", l))
                    nc.scalar.activation(gm[:, 10, :], gm[:, 10, :], ACT.Exp).then_inc(*ev.mark("act", "mexp", l))
                elif kind == "mqk":
                    if hd:
                        act.wait_ge(*ev.at("mt", l, hd - 1))
                    for n, ct, (q, t0, size) in banks_a(st):
                        act.wait_ge(*ev.at("bank", n))
                        a = at_tile(t0 // P)
                        nc.scalar.activation(ma[:, ct, a:a + size], psg[:, n % 4, 0:size], ACT.Copy).then_inc(*ev.mark("act", "bank_free", n))
                        ev.now[("ma", l, hd, ct)] = {"act": ev.count["act"]}
                    for ct in range(2):
                        r0 = 1 if (st["ctx"] or ct == 1) else at_tile(CT)
                        act.wait_ge(*ev.at("conv", l, hd, ct))
                        nc.scalar.activation(mt[:, ct, r0:PADDED - 1], mc[:, ct, r0:PADDED - 1], ACT.Tanh, scale=0.5).then_inc(*ev.mark("act", "mt_", l, hd, ct))
                elif kind == "mvo":
                    for n, tt in banks_b(st):
                        act.wait_ge(*ev.at("bank", n))
                        if st["prev_head"] is not None:
                            act.wait_ge(*ev.at("pe_step", st["prev_head"]))
                            act.wait_ge(*ev.at("dve_step", st["prev_head"]))
                            act.wait_ge(*ev.at("pool_step", st["prev_head"]))
                        ps = psg[:, n % 4, :].rearrange("p (j c) -> p j c", j=2)
                        nc.scalar.activation(mv[:, tt[0]:tt[0] + 2, 0:P], ps[:, :, 0:P], ACT.Copy).then_inc(*ev.mark("act", "mv", l, hd, tt[0] // 2))
                        nc.scalar.activation(mo[:, tt[0]:tt[0] + 2, :], ps[:, :, P:2 * P], ACT.Tanh, scale=0.5).then_inc(*ev.mark("act", "bank_free", n))
                        ev.now[("mo", l, hd)] = {"act": ev.count["act"]}
                elif kind in ("mktok", "rktok"):
                    r_ = kind[0]
                    dst = mktok if r_ == "m" else rktok
                    act.wait_ge(*ev.at(r_ + "ktokT" if r_ == "r" else "ktokT", l, hd, t))
                    if st["prev_head"] is not None:
                        act.wait_ge(*ev.at("pe_step", st["prev_head"]))
                    nc.scalar.activation(dst[:, t, :], psm[:, 3, (t % 4) * P:(t % 4 + 1) * P], ACT.Copy).then_inc(*ev.mark("act", r_ + "kt", l, hd, t))
                elif kind == "mtile" and st["out"]:
                    act.wait_ge(*ev.at("marg", l, hd, t))
                    nc.scalar.activation(msc[:, 0:2, :], msc[:, 0:2, :], ACT.Exp).then_inc(*ev.mark("act", "mexpw", l, hd, t))
                    act.wait_ge(*ev.at("mintra", l, hd, t))
                    nc.scalar.activation(mnd[:, 0:2, :], psm[:, 1, 0:2 * (P + 1)].rearrange("p (d c) -> p d c", d=2), ACT.Copy).then_inc(*ev.mark("act", "mintra_sb", l, hd, t))
                    act.wait_ge(*ev.at("myT", l, hd, t))
                    nc.scalar.activation(yT[:, hd, t * P:(t + 1) * P], psm[:, 3, 0:P], ACT.Copy, scale=pr(l, "m_norm", hd)).then_inc(*ev.mark("act", "yT", l, "m", t))
                    ev.now[("yTm", l, hd, t)] = {"act": ev.count["act"]}
                elif kind in ("gate",):
                    for n, tt in banks_b(st):
                        act.wait_ge(*ev.at("bank", n))
                        if st["prev_branch"] is not None:
                            act.wait_ge(*ev.at("dve_step", st["prev_branch"]))
                        ps = psg[:, n % 4, :].rearrange("p (j c) -> p j c", j=2)
                        nc.scalar.activation(tg[:, tt[0]:tt[0] + 2, :], ps, ACT.Tanh, scale=0.5).then_inc(*ev.mark("act", "bank_free", n))
                        ev.now[("tg", l, st["br"], st["n"], tt[0])] = {"act": ev.count["act"]}
                elif kind in ("aq", "akv"):
                    for n, ct, (q, t0, size) in banks_a(st):
                        act.wait_ge(*ev.at("bank", n))
                        dst = ak[:, t0:t0 + size] if kind == "akv" else aq[:, 2 * st["g"] + ct, t0:t0 + size]
                        nc.scalar.activation(dst, psg[:, n % 4, 0:size], ACT.Copy).then_inc(*ev.mark("act", "bank_free", n))
                        ev.now[("araw", l, st.get("g", 2), ct)] = {"act": ev.count["act"]}
                    if kind == "akv":
                        for n, tt in banks_b(st):
                            act.wait_ge(*ev.at("bank", n))
                            ps = psg[:, n % 4, :].rearrange("p (j c) -> p j c", j=2)
                            nc.scalar.activation(av[:, tt[0]:tt[0] + 2, :], ps[:, :, 0:P], ACT.Copy).then_inc(*ev.mark("act", "bank_free", n))
                            ev.now[("av", l)] = {"act": ev.count["act"]}
                elif kind == "ahead":
                    nk = len(akeys(t)) * P
                    b = st["buf"]
                    s0 = 8 + 8 * b
                    act.wait_ge(*ev.at("anm", l, t, hd))
                    nc.scalar.activation(asb[:, b, 0:nk], asb[:, b, 0:nk], ACT.Exp, bias=small[:, s0 + 1:s0 + 2], accum_out=small[:, s0 + 2:s0 + 3]).then_inc(*ev.mark("act", "ap_", l, t, hd))
                    nc.scalar.activation(small[:, s0 + 3:s0 + 4], pr(l, "sink", hd), ACT.Exp, bias=small[:, s0 + 1:s0 + 2]).then_inc(*ev.mark("act", "ap", l, t, hd))
                    act.wait_ge(*ev.at("apT", l, t, hd))
                    n1 = min(nk, 512)
                    nc.scalar.activation(apt[:, b, 0:n1], psm[:, 2, 0:n1], ACT.Copy).then_inc(*ev.mark("act", "apt", l, t, hd))
                    if nk > 512:
                        nc.scalar.activation(apt[:, b, 512:640], psm[:, 3, 0:P], ACT.Copy).then_inc(*ev.mark("act", "apt", l, t, hd))
                elif kind == "aout":
                    act.wait_ge(*ev.at("ayT", l, t))
                    nc.scalar.activation(yT[:, 0:4, t * P:(t + 1) * P], psm[:, 1, :].rearrange("p (k c) -> p k c", k=4), ACT.Copy).then_inc(*ev.mark("act", "yT", l, "a", t))
                elif kind == "rqk":
                    if hd == 0:
                        x = small[:, 48:56]
                        nc.scalar.activation(x, pr(l, "ret", 0, 8), ACT.Abs).then_inc(*ev.mark("act", "r", l))
                        act.wait_ge(*ev.last("act"))
                        nc.scalar.activation(x, x, ACT.Exp, scale=-1.0).then_inc(*ev.mark("act", "r", l))
                        act.wait_ge(*ev.last("act"))
                        nc.scalar.activation(x, x, ACT.Ln, bias=c("one")).then_inc(*ev.mark("act", "rabs", l))
                    for ct in (0, 1):
                        for n, ct_, (q, t0, size) in banks_a(st):
                            if ct_ != ct:
                                continue
                            act.wait_ge(*ev.at("bank", n))
                            if ct or hd:
                                act.wait_ge(*ev.at("rtmp_done", l, hd if ct else hd - 1, 1 - ct))
                            nc.scalar.activation(rtmp[0:64, t0:t0 + size], psg[64:128, n % 4, 0:size], ACT.Copy).then_inc(*ev.mark("act", "rsw", l, hd, ct, q))
                            nc.scalar.activation(rtmp[64:128, t0:t0 + size], psg[0:64, n % 4, 0:size], ACT.Copy).then_inc(*ev.mark("act", "rsw", l, hd, ct, q))
                    act.wait_ge(*ev.at("logg", l))
                    if st["prev_head"] is not None:
                        act.wait_ge(*ev.at("dve_step", st["prev_head"]))
                        act.wait_ge(*ev.at("pool_step", st["prev_head"]))
                    for d in range(2):
                        g = small[:, 40 + d * 4 + hd:41 + d * 4 + hd]
                        nc.scalar.activation(rd[:, d, :], c("ahead" if d == 0 else "behind"), ACT.Exp, scale=g).then_inc(*ev.mark("act", "rdec", l, hd))
                    act.wait_ge(*ev.at("rdecD", l, hd))
                    for d in range(2):
                        g = small[:, 40 + d * 4 + hd:41 + d * 4 + hd]
                        nc.scalar.activation(rd[:, 1 + d, :], c("row_f" if d == 0 else "row_b"), ACT.Exp, scale=g).then_inc(*ev.mark("act", "rrow", l, hd))
                        nc.scalar.activation(small[:, 56 + d:57 + d], c("col_f" if d == 0 else "col_b"), ACT.Exp, scale=g).then_inc(*ev.mark("act", "rcol", l, hd))
                        nc.scalar.activation(small[:, 58 + d:59 + d], c("cd"), ACT.Exp, scale=g).then_inc(*ev.mark("act", "rcd", l, hd))
                elif kind == "rv":
                    for n, tt in banks_b(st):
                        act.wait_ge(*ev.at("bank", n))
                        if st["prev_head"] is not None:
                            act.wait_ge(*ev.at("pe_step", st["prev_head"]))
                            act.wait_ge(*ev.at("pool_step", st["prev_head"]))
                        ps = psg[:, n % 4, :].rearrange("p (j c) -> p j c", j=2)
                        nc.scalar.activation(rv[:, tt[0]:tt[0] + 2, :], ps, ACT.Copy).then_inc(*ev.mark("act", "bank_free", n))
                        ev.now[("rv_sb", l, hd)] = {"act": ev.count["act"]}
                elif kind == "rg":
                    for n, tt in banks_b(st):
                        act.wait_ge(*ev.at("bank", n))
                        if st["prev_head"] is not None:
                            act.wait_ge(*ev.at("dve_step", st["prev_head"]))
                        ps = psg[:, n % 4, :].rearrange("p (j c) -> p j c", j=2)
                        nc.scalar.activation(rg[:, tt[0]:tt[0] + 2, :], ps, ACT.Tanh, scale=0.5).then_inc(*ev.mark("act", "rgt", l, hd, tt[0]))
                elif kind == "rtile" and st["out"]:
                    act.wait_ge(*ev.at("ryT", l, hd, t))
                    for j in range(2):
                        nc.scalar.activation(yT[:, 2 * hd + j, t * P:(t + 1) * P], psm[:, 3, j * P:(j + 1) * P], ACT.Copy, scale=pr(l, "r_norm", 2 * hd + j)).then_inc(*ev.mark("act", "yT", l, "r", t))
                    ev.now[("yTr", l, hd, t)] = {"act": ev.count["act"]}
                elif kind == "up":
                    u, b = st["u"], st["u"] % 2
                    r0 = 1 if st["ctx"] else at_tile(CT)
                    if u >= 2:
                        act.wait_ge(*ev.at("fa_free", l, u - 2))
                    for n, ct, (q, t0, size) in banks_a(st):
                        act.wait_ge(*ev.at("bank", n))
                        if ct == 0:
                            a = at_tile(t0 // P)
                            nc.scalar.activation(fa[:, b, a:a + size], psg[:, n % 4, 0:size], ACT.Copy).then_inc(*ev.mark("act", "bank_free", n))
                            ev.now[("fa", l, u)] = {"act": ev.count["act"]}
                        else:
                            if u:
                                act.wait_ge(*ev.at("u_", l, u - 1))
                            nc.scalar.activation(fb[:, t0:t0 + size], psg[:, n % 4, 0:size], ACT.Copy, scale=0.5).then_inc(*ev.mark("act", "bank_free", n))
                            ev.now[("fb", l, u)] = {"act": ev.count["act"]}
                    act.wait_ge(*ev.at("fc", l, u))
                    if u:
                        act.wait_ge(*ev.at("u_", l, u - 1))
                    for q, t0, size in seqs[st["ctx"]]:
                        a = at_tile(t0 // P)
                        nc.scalar.activation(ft[:, t0:t0 + size], fc[:, a:a + size], ACT.Tanh, scale=0.5).then_inc(*ev.mark("act", "ft", l, u))
                    act.wait_ge(*ev.at("u_", l, u))
                    if st["ring_free"] is not None:
                        act.wait_ge(*ev.at("w_free", st["ring_free"]))
                    t0 = 0 if st["ctx"] else CTX
                    nc.scalar.activation(uh[:, u % URING, t0:TOK], fu[:, t0:TOK], ACT.Copy).then_inc(*ev.mark("act", "uh", l, u))
            for k in ("store0", "store1", "out0", "out1"):
                if ev.count.get(k, 0):
                    act.wait_ge(semaphore(k), ev.count[k])

        def head_norm(dve, x, r_, l, hd, t):
            dve.bn_stats(small[:, 28:34], x).then_inc(*ev.mark("dve", "hn"))
            dve.wait_ge(*ev.last("dve"))
            dve.bn_aggr(small[:, 36:38], small[:, 28:34]).then_inc(*ev.mark("dve", "hn"))
            dve.wait_ge(*ev.last("dve"))
            dve.tensor_scalar(small[:, 38:39], small[:, 37:38], EPS, None, ALU.add).then_inc(*ev.mark("dve", r_ + "var", l, hd, t))
            dve.wait_ge(*ev.at(r_ + "rstd", l, hd, t))

        @block.vector
        def _(dve):
            V = nc.vector

            dve.wait_ge(*ev.at("cvec"))
            dve.wait_ge(*ev.at("const"))
            dve.wait_ge(*ev.at("par"))
            dve.wait_ge(*ev.at("tanh_c"))
            V.scalar_tensor_tensor(out=cvec[:, 1], in0=cvec[:, 1], scalar=1.0, in1=cvec[:, 0], op0=ALU.add,
                                      op1=ALU.mult).then_inc(*ev.mark("dve", "c1"))
            dve.wait_ge(*ev.last("dve"))
            V.tensor_scalar(cvec[:, 2], cvec[:, 1], 0.5, None, ALU.mult).then_inc(*ev.mark("dve", "silu_c"))
            for i, st in walk("dve"):
                kind, s = st["kind"], st["slot"]
                l, hd, t = st.get("l"), st.get("hd"), st.get("t")
                if kind == "region":
                    phase_end(dve, i)
                    if st["name"] == "mlstm":
                        for b in range(2):
                            for z in (0, at_tile(CT) - 2, at_tile(CT) - 1, PADDED - 1):
                                V.memset(ma[:, b, z:z + 1], 0.0).then_inc(*ev.mark("dve", "pads", i))
                        V.memset(mv[:, :, P:P + 1], 1.0).then_inc(*ev.mark("dve", "pads", i))
                if kind == "vector":
                    n = st["bank"]
                    dve.wait_ge(*ev.at("bank", n))
                    m = st["n"] * 2
                    slot_ = (m // 8 if m < 16 else m // 8 - 1) % 4
                    o_ = vec[:, slot_ * 8 + m % 8:slot_ * 8 + m % 8 + 2, :]
                    V.tensor_tensor(o_, psg[:, n % 4, 0:4].rearrange("p (a b) -> p a b", a=2),
                                       pr(l, "mod_b", m, 2).rearrange("p (a b) -> p a b", b=1).broadcast_to((P, 2, 2)),
                                       ALU.add).then_inc(*ev.mark("dve", "bank_free", n))
                elif kind == "affine":
                    w = st["which"]
                    dve.wait_ge(*ev.last("dve"))
                    if st["last_norm"] is not None:
                        dve.wait_ge(*ev.at("act_step", st["last_norm"]))
                    nw = pr(l, "norm1" if w == 0 else "norm2", 0, 8)
                    nwb = nw.rearrange("p (a b) -> p a b", b=1).broadcast_to((P, KD, 2))
                    V.scalar_tensor_tensor(out=aff[:, w, 0], in0=vec[:, (2 * w + 1) * 8:(2 * w + 2) * 8, :],
                                              scalar=1.0, in1=nwb, op0=ALU.add, op1=ALU.mult).then_inc(*ev.mark("dve", "affine", l, w))
                    V.tensor_copy(aff[:, w, 1], vec[:, 2 * w * 8:(2 * w + 1) * 8, :]).then_inc(*ev.mark("dve", "affine", l, w))
                elif kind == "rowgate":
                    n = st["bank"]
                    dve.wait_ge(*ev.at("bank", n))
                    dve.wait_ge(*ev.at("bias", l, st["which"]))
                    dve.wait_ge(*ev.last("dve"))
                    for q in ((0, 1) if st["ctx"] else (1,)):
                        cs = slice(st["n"] * COLS, (st["n"] + 1) * COLS)
                        V.tensor_tensor(gate_b[:, q, cs], psg[:, n % 4, q * 256:q * 256 + 256], bias_b[:, cs],
                                           ALU.add).then_inc(*ev.mark("dve", "bank_free", n))
                    if st["which"] == 0:
                        dve.wait_ge(*ev.last("dve"))
                        for q in ((0, 1) if st["ctx"] else (1,)):
                            V.tensor_scalar(gate_b[:, q, cs], gate_b[:, q, cs], 0.5, None, ALU.mult).then_inc(*ev.mark("dve", "gb"))
                    ev.now[("bias_free", l, st["which"])] = {"dve": ev.count["dve"]}
                elif kind == "norm":
                    q = 1 if t >= CT else 0
                    sg = stage[:, st["buf"]]
                    dve.wait_ge(*ev.at("stage", st["id"]))
                    if st["use"] != "first":
                        dve.wait_ge(*ev.last("dve"))
                        V.tensor_tensor(acc[:, t, :], acc[:, t, :], gate_b[:, q, :], ALU.mult).then_inc(*ev.mark("dve", "na"))
                        dve.wait_ge(*ev.last("dve"))
                        V.tensor_tensor(sg, sg, acc[:, t, :], ALU.add).then_inc(*ev.mark("dve", "rsum", st["id"]))
                    dve.wait_ge(*ev.at("ss", st["id"]))
                    V.tensor_scalar(small[:, 1:2], small[:, 0:1], 1.0 / D, EPS, ALU.mult, ALU.add).then_inc(*ev.mark("dve", "ms", st["id"]))
                    w = 0 if st["use"] in ("first", "end") else 1
                    if st["use"] == "last":
                        dve.wait_ge(*ev.at("rstd", st["id"]))
                        dve.wait_ge(*ev.at("fnorm"))
                        V.scalar_tensor_tensor(out=sg, in0=sg, scalar=small[:, 2:3], in1=bias_b[:],
                                                  op0=ALU.mult, op1=ALU.mult).then_inc(*ev.mark("dve", "outrow", st["id"]))
                        continue
                    if st["before"] is not None:
                        dve.wait_ge(*ev.at("h", st["before"]["gen"], st["before"]["t"]))
                    for half in range(2):
                        dve.wait_ge(*ev.at("xT", st["id"], half))
                        for k in range(4):
                            kk = half * 4 + k
                            V.tensor_scalar(hf[:, kk, :], psm[:, half, k * P:(k + 1) * P],
                                               aff[:, w, 0, kk, q:q + 1], aff[:, w, 1, kk, q:q + 1], ALU.mult,
                                               ALU.add).then_inc(*ev.mark("dve", "hf", st["id"]))
                elif kind == "turn":
                    ts = slice(t * P, (t + 1) * P)
                    for half in range(2):
                        dve.wait_ge(*ev.at("turn_hh", l, t, half))
                        ks = slice(half * 4, half * 4 + 4)
                        V.tensor_tensor(hl[:, ks, ts],
                                           psm[:, half + 2 * (t % 2), :].rearrange("p (k c) -> p k c", k=4),
                                           hh[:, ks, ts].bitcast(F32), ALU.subtract).then_inc(*ev.mark("dve", "h", st["gen"], t))
                elif kind == "wout":
                    for n, tt in banks_b(st):
                        dve.wait_ge(*ev.at("bank", n))
                        dve.wait_ge(*ev.at("h", st["gen"], TILES - 1))
                        cs = slice(st["n"] * COLS, (st["n"] + 1) * COLS)
                        ps = psg[:, n % 4, :].rearrange("p (j c) -> p j c", j=2)
                        V.tensor_copy(acc[:, tt[0]:tt[0] + 2, cs], ps).then_inc(*ev.mark("dve", "bank_free", n))
                elif kind == "down":
                    for j, t_ in enumerate(range(st["first"], TILES)):
                        n = st["bank"] + j
                        dve.wait_ge(*ev.at("bank", n))
                        cs = slice(st["half"] * 512, st["half"] * 512 + 512)
                        if st["g"] == 0:
                            V.tensor_copy(acc[:, t_, cs], psg[:, n % 4, :]).then_inc(*ev.mark("dve", "bank_free", n))
                        else:
                            V.tensor_tensor(acc[:, t_, cs], acc[:, t_, cs], psg[:, n % 4, :], ALU.add).then_inc(*ev.mark("dve", "bank_free", n))
                elif kind == "up":
                    u, b = st["u"], st["u"] % 2
                    if u == 0:
                        for b_ in range(2):
                            for z in (0, at_tile(CT) - 2, at_tile(CT) - 1, PADDED - 1):
                                V.memset(fa[:, b_, z:z + 1], 0.0).then_inc(*ev.mark("dve", "fpads", l))
                    r0 = 1 if st["ctx"] else at_tile(CT)
                    r1 = PADDED - 1
                    dve.wait_ge(*ev.at("fa", l, u))
                    dve.wait_ge(*ev.last("dve"))
                    w = [pr(l, "f_conv", j * FT + u) for j in range(3)]
                    if u:
                        dve.wait_ge(*ev.at("ft", l, u - 1))
                    V.tensor_scalar(fc[:, r0:r1], fa[:, b, r0 - 1:r1 - 1], w[0], pr(l, "f_bias", u), ALU.mult,
                                       ALU.add).then_inc(*ev.mark("dve", "fc0"))
                    for j in (1, 2):
                        dve.wait_ge(*ev.last("dve"))
                        V.scalar_tensor_tensor(out=fc[:, r0:r1], in0=fa[:, b, r0 - 1 + j:r1 - 1 + j],
                                                  scalar=w[j], in1=fc[:, r0:r1], op0=ALU.mult, op1=ALU.add).then_inc(*ev.mark("dve", "fc", l, u))
                    ev.now[("fa_free", l, u)] = {"dve": ev.count["dve"]}
                    dve.wait_ge(*ev.at("ft", l, u))
                    if u:
                        dve.wait_ge(*ev.at("uh", l, u - 1))
                        dve.wait_ge(*ev.at("u", l, u - 1))
                    for q, t0, size in seqs[st["ctx"]]:
                        a = at_tile(t0 // P)
                        V.scalar_tensor_tensor(out=fu[:, t0:t0 + size], in0=ft[:, t0:t0 + size], scalar=1.0,
                                                  in1=fc[:, a:a + size], op0=ALU.add, op1=ALU.mult).then_inc(*ev.mark("dve", "fp"))
                    dve.wait_ge(*ev.at("fb", l, u))
                    dve.wait_ge(*ev.last("dve"))
                    t0 = 0 if st["ctx"] else CTX
                    V.tensor_tensor(fu[:, t0:], fu[:, t0:], fb[:, t0:], ALU.mult).then_inc(*ev.mark("dve", "u_", l, u))
                elif kind == "mgates":
                    for n, tt in banks_b(st):
                        dve.wait_ge(*ev.at("bank", n))
                        ps = psg[:, n % 4, :].rearrange("p (j c) -> p j c", j=2)[:, :, 0:16]
                        gb = pr(l, "gate", 0, 16).rearrange("p (a b) -> p a b", a=1).broadcast_to((P, 2, 16))
                        V.tensor_tensor(g16[:, tt[0]:tt[0] + 2, :], ps, gb, ALU.add).then_inc(*ev.mark("dve", "bank_free", n))
                    dve.wait_ge(*ev.last("dve"))
                    Fv = gm[:, 0, :].rearrange("p (d s h) -> p d s h", d=2, s=TILES)
                    Iv = gm[:, 11, :].rearrange("p (d s h) -> p d s h", d=2, s=TILES)
                    V.tensor_copy(Iv[:, 0], g16[:, :, 0:4]).then_inc(*ev.mark("dve", "gI"))
                    V.tensor_copy(Fv[:, 0], g16[:, :, 4:8]).then_inc(*ev.mark("dve", "gF"))
                    for s_, t_ in enumerate(BACK):
                        V.tensor_copy(Iv[:, 1, s_], g16[:, t_, 8:12]).then_inc(*ev.mark("dve", "gI"))
                        V.tensor_copy(Fv[:, 1, s_], g16[:, t_, 12:16]).then_inc(*ev.mark("dve", "Fx", l))
                    dve.wait_ge(*ev.at("lnf", l))
                    V.scalar_tensor_tensor(out=gm[:, 2, :], in0=gm[:, 0, :], scalar=0.0, in1=gm[:, 1, :],
                                              op0=ALU.min, op1=ALU.subtract).then_inc(*ev.mark("dve", "logf", l))
                    dve.wait_ge(*ev.at("sums", l))
                    V.tensor_tensor(gm[:, 4, :], gm[:, 11, :], psm[:, 3, 0:48], ALU.subtract).then_inc(*ev.mark("dve", "A", l))
                    dve.wait_ge(*ev.at("AT", l))
                    V.tensor_copy(atr[0:24, 0:2, :], psm[0:24, 2, 0:2 * P].rearrange("p (a b) -> p a b", a=2)).then_inc(*ev.mark("dve", "atr"))
                    dve.wait_ge(*ev.last("dve"))
                    for d in range(2):
                        V.tensor_tensor_scan(atr[0:24, 2 + d, :], atr[0:24, d, :], atr[0:24, d, :], NEG,
                                                ALU.max, ALU.max).then_inc(*ev.mark("dve", "scan", l))
                    dve.wait_ge(*ev.at("LM", l))
                    V.tensor_copy(gm[:, 5, :], psm[:, 1, 0:48]).then_inc(*ev.mark("dve", "LMb", l))
                    dve.wait_ge(*ev.at("LMf", l))
                    V.tensor_copy(gm[:, 5, 24:48], psm[:, 1, 48:72]).then_inc(*ev.mark("dve", "LM2"))
                    dve.wait_ge(*ev.at("cmax", l))
                    v = {k: gm[:, k, :].rearrange("p (d s h) -> p d s h", d=2, s=TILES) for k in (0, 1, 3)}
                    g_ = psm[:, 3, 48:96].rearrange("p (d s h) -> p d s h", d=2, s=TILES)
                    V.memset(v[3][:, :, 0, :], 0.0).then_inc(*ev.mark("dve", "ms0"))
                    for s_ in range(TILES):
                        dve.wait_ge(*ev.last("dve"))
                        V.tensor_tensor(v[1][:, :, s_, :], v[3][:, :, s_, :], v[0][:, :, s_, :], ALU.max).then_inc(*ev.mark("dve", "mm"))
                        if s_ < TILES - 1:
                            dve.wait_ge(*ev.last("dve"))
                            V.tensor_tensor(v[3][:, :, s_ + 1, :], v[1][:, :, s_, :], g_[:, :, s_, :], ALU.add).then_inc(*ev.mark("dve", "mm"))
                    dve.wait_ge(*ev.last("dve"))
                    V.tensor_tensor(gm[:, 5, :], gm[:, 3, :], gm[:, 5, :], ALU.max).then_inc(*ev.mark("dve", "M"))
                    dve.wait_ge(*ev.last("dve"))
                    V.tensor_tensor(gm[:, 6, :], gm[:, 4, :], gm[:, 1, :], ALU.subtract).then_inc(*ev.mark("dve", "e"))
                    V.tensor_tensor(gm[:, 7, :], gm[:, 3, :], gm[:, 1, :], ALU.subtract).then_inc(*ev.mark("dve", "e"))
                    V.tensor_tensor(gm[:, 8, :], gm[:, 3, :], gm[:, 5, :], ALU.subtract).then_inc(*ev.mark("dve", "e"))
                    V.tensor_scalar(gm[:, 9, :], gm[:, 5, :], -1.0, None, ALU.mult).then_inc(*ev.mark("dve", "negM", l))
                    dve.wait_ge(*ev.last("dve"))
                    V.tensor_tensor(gm[:, 10, :], gm[:, 9, :], psm[:, 3, 0:48], ALU.subtract).then_inc(*ev.mark("dve", "mlogs", l))
                    dve.wait_ge(*ev.at("mexp", l))
                    V.tensor_scalar(gm[:, 6, :], gm[:, 6, :], M_SCALE, None, ALU.mult).then_inc(*ev.mark("dve", "mcols", l))
                elif kind == "mqk":
                    for ct in range(2):
                        r0 = 1 if (st["ctx"] or ct == 1) else at_tile(CT)
                        r1 = PADDED - 1
                        dve.wait_ge(*ev.at("ma", l, hd, ct))
                        dve.wait_ge(*ev.last("dve"))
                        w = [pr(l, "conv_q" if ct == 0 else "conv_k", j * MH + hd) for j in range(3)]
                        V.tensor_scalar(mc[:, ct, r0:r1], ma[:, ct, r0 - 1:r1 - 1], w[0], None, ALU.mult).then_inc(*ev.mark("dve", "c"))
                        for j in (1, 2):
                            dve.wait_ge(*ev.last("dve"))
                            V.scalar_tensor_tensor(out=mc[:, ct, r0:r1], in0=ma[:, ct, r0 - 1 + j:r1 - 1 + j],
                                                      scalar=w[j], in1=mc[:, ct, r0:r1], op0=ALU.mult,
                                                      op1=ALU.add).then_inc(*ev.mark("dve", "conv", l, hd, ct))
                    for ct in range(2):
                        r0 = 1 if (st["ctx"] or ct == 1) else at_tile(CT)
                        dve.wait_ge(*ev.at("mt_", l, hd, ct))
                        if st["prev_head"] is not None:
                            dve.wait_ge(*ev.at("pe_step", st["prev_head"]))
                        V.scalar_tensor_tensor(out=mqk[:, ct, r0:r1], in0=mt[:, ct, r0:r1], scalar=1.0,
                                                  in1=mc[:, ct, r0:r1], op0=ALU.add, op1=ALU.mult).then_inc(*ev.mark("dve", "mqk", l, hd))
                    ev.now[("mt", l, hd)] = {"dve": ev.count["dve"]}
                elif kind == "mback":
                    s_ = st["s"]
                    if s_ == 0:
                        if st["prev_head"] is not None:
                            dve.wait_ge(*ev.at("pe_step", st["prev_head"]))
                        dve.wait_ge(*ev.last("dve"))
                        V.memset(mcb[:, 0, :], 0.0).then_inc(*ev.mark("dve", "z"))
                        V.memset(mcf[:, 0, :], 0.0).then_inc(*ev.mark("dve", "z"))
                        ev.now[("mC", l, hd, "f", 0)] = {"dve": ev.count["dve"]}
                        ev.now[("mC", l, hd, "b", 0)] = {"dve": ev.count["dve"]}
                        dve.wait_ge(*ev.last("dve"))
                    dve.wait_ge(*ev.at("mkv", l, hd, "b", s_))
                    col = 24 + s_ * 4 + hd
                    dve.wait_ge(*ev.last("dve"))
                    V.scalar_tensor_tensor(out=mcb[:, s_ + 1, :], in0=mcb[:, s_, :], scalar=gm[:, 7, col:col + 1],
                                              in1=psm[:, 2, 258:258 + P + 1], op0=ALU.mult, op1=ALU.add).then_inc(*ev.mark("dve", "mC", l, hd, "b", s_ + 1))
                elif kind == "mtile":
                    if st["out"]:
                        cf = t * 4 + hd
                        cb = 24 + BACK.index(t) * 4 + hd
                        dve.wait_ge(*ev.at("mscore", l, hd, t))
                        for d, col in ((0, cf), (1, cb)):
                            V.scalar_tensor_tensor(out=msc[:, d, :], in0=psm[:, 0, (1 + d) * P:(2 + d) * P],
                                                      scalar=gm[:, 4, col:col + 1],
                                                      in1=c("hide_f" if d == 0 else "hide_b"), op0=ALU.add,
                                                      op1=ALU.add).then_inc(*ev.mark("dve", "marg", l, hd, t))
                        dve.wait_ge(*ev.at("mexpw", l, hd, t))
                        for d in range(2):
                            V.scalar_tensor_tensor(out=msc[:, 2 + d, :], in0=psm[:, 0, 0:P], scalar=M_SCALE,
                                                      in1=msc[:, d, :], op0=ALU.mult, op1=ALU.mult).then_inc(*ev.mark("dve", "mw", l, hd, t))
                        dve.wait_ge(*ev.at("mintra_sb", l, hd, t))
                        dve.wait_ge(*ev.at("minter", l, hd, t))
                        for d, col in ((0, cf), (1, cb)):
                            V.scalar_tensor_tensor(out=mnd[:, 2 + d, :],
                                                      in0=psm[:, 2, d * (P + 1):(d + 1) * (P + 1)],
                                                      scalar=gm[:, 8, col:col + 1], in1=mnd[:, d, :],
                                                      op0=ALU.mult, op1=ALU.add).then_inc(*ev.mark("dve", "mnd", l, hd, t))
                        dve.wait_ge(*ev.last("dve"))
                        den = mnd[:, 2:4, P]
                        V.scalar_tensor_tensor(out=small[:, 24:26], in0=den, scalar=-1.0, in1=den,
                                                  op0=ALU.mult, op1=ALU.max).then_inc(*ev.mark("dve", "d"))
                        dve.wait_ge(*ev.last("dve"))
                        V.tensor_tensor(small[:, 24:25], small[:, 24:25], gm[:, 10, cf:cf + 1], ALU.max).then_inc(*ev.mark("dve", "d"))
                        V.tensor_tensor(small[:, 25:26], small[:, 25:26], gm[:, 10, cb:cb + 1], ALU.max).then_inc(*ev.mark("dve", "d"))
                        dve.wait_ge(*ev.last("dve"))
                        V.reciprocal(small[:, 26:28], small[:, 24:26]).then_inc(*ev.mark("dve", "d"))
                        dve.wait_ge(*ev.last("dve"))
                        V.tensor_scalar(my[:, 0, :], mnd[:, 2, 0:P], small[:, 26:27], None, ALU.mult).then_inc(*ev.mark("dve", "d"))
                        dve.wait_ge(*ev.last("dve"))
                        V.scalar_tensor_tensor(out=my[:, 1, :], in0=mnd[:, 3, 0:P], scalar=small[:, 27:28],
                                                  in1=my[:, 0, :], op0=ALU.mult, op1=ALU.add).then_inc(*ev.mark("dve", "d"))
                        dve.wait_ge(*ev.last("dve"))
                        head_norm(dve, my[:, 1, :], "m", l, hd, t)
                        V.tensor_scalar(my[:, 1, :], my[:, 1, :], small[:, 36:37], small[:, 39:40],
                                           ALU.subtract, ALU.mult).then_inc(*ev.mark("dve", "d"))
                        dve.wait_ge(*ev.last("dve"))
                        dve.wait_ge(*ev.at("mo", l, hd))
                        V.tensor_scalar(my[:, 0, :], mo[:, t, :], 1.0, 0.5, ALU.add, ALU.mult).then_inc(*ev.mark("dve", "d"))
                        dve.wait_ge(*ev.last("dve"))
                        V.tensor_tensor(my[:, 2, :], my[:, 1, :], my[:, 0, :], ALU.mult).then_inc(*ev.mark("dve", "my", l, hd, t))
                    if t < TILES - 1:
                        dve.wait_ge(*ev.at("minter" if st["out"] else "mkv", l, hd, *(() if st["out"] else ("f",)), t))
                        col = t * 4 + hd
                        dve.wait_ge(*ev.last("dve"))
                        V.scalar_tensor_tensor(out=mcf[:, (t + 1) % 2, :], in0=mcf[:, t % 2, :],
                                                  scalar=gm[:, 7, col:col + 1], in1=psm[:, 2, 258:258 + P + 1],
                                                  op0=ALU.mult, op1=ALU.add).then_inc(*ev.mark("dve", "mC", l, hd, "f", t + 1))
                elif kind == "branch":
                    first = st["br"] == "m"
                    cs = slice(st["n"] * COLS, (st["n"] + 1) * COLS)
                    for j, (n, tt) in enumerate(banks_b(st)):
                        dve.wait_ge(*ev.at("bank", n))
                        dve.wait_ge(*ev.at("tg", l, st["br"], st["n"], tt[0]))
                        ps = psg[:, n % 4, :].rearrange("p (j c) -> p j c", j=2)
                        dst = acc[:, tt[0]:tt[0] + 2, cs] if first else \
                            bt[:, n % 2, :].rearrange("p (j c) -> p j c", j=2)
                        if not first:
                            if st["prev_branch"] is not None:
                                dve.wait_ge(*ev.at("pool_step", st["prev_branch"]))
                            if j == 2:
                                dve.wait_ge(*ev.at("summed", n - 2))
                        V.scalar_tensor_tensor(out=dst, in0=tg[:, tt[0]:tt[0] + 2, :], scalar=1.0, in1=ps,
                                                  op0=ALU.add, op1=ALU.mult).then_inc(*ev.mark("dve", "bank_free", n))
                        ev.now[("gated", l, st["br"], st["n"], tt[0])] = {"dve": ev.count["dve"]}
                elif kind in ("aq", "akv"):
                    for ct in range(2 if kind == "aq" else 1):
                        g = st.get("g", 2)
                        x = aq[:, 2 * g + ct, CTX:TOK] if kind == "aq" else ak[:, CTX:TOK]
                        dve.wait_ge(*ev.at("arot", l, g, ct))
                        dve.wait_ge(*ev.at("rope", st["region"]))
                        dve.wait_ge(*ev.last("dve"))
                        V.tensor_tensor(atmp[:], psm[:, ct, 0:SEQ], ropea[:, 1, :], ALU.mult).then_inc(*ev.mark("dve", "amix_", l, g, ct))
                        V.tensor_tensor(x, x, ropea[:, 0, :], ALU.mult).then_inc(*ev.mark("dve", "x"))
                        dve.wait_ge(*ev.last("dve"))
                        V.tensor_tensor(x, x, atmp[:], ALU.add).then_inc(*ev.mark("dve", "arope", l))
                elif kind == "ahead":
                    b = st["buf"]
                    s0 = 8 + 8 * b
                    keys = akeys(t)
                    nw = len(keys) - 2
                    dve.wait_ge(*ev.at("ascore", l, t, hd))
                    if nw:
                        c0 = (max(CT, t - 1) - (t - 1)) * P
                        V.scalar_tensor_tensor(out=asb[:, b, 0:nw * P], in0=psm[:, 0, 0:nw * P],
                                                  scalar=AD ** -0.5, in1=c("window")[:, c0:c0 + nw * P],
                                                  op0=ALU.mult, op1=ALU.add).then_inc(*ev.mark("dve", "as"))
                    V.tensor_scalar(asb[:, b, nw * P:(nw + 2) * P], psm[:, 1, 0:CTX], AD ** -0.5, None,
                                       ALU.mult).then_inc(*ev.mark("dve", "as_", l, t, hd))
                    dve.wait_ge(*ev.last("dve"))
                    V.tensor_reduce(small[:, s0:s0 + 1], asb[:, b, 0:(nw + 2) * P], AX.X, ALU.max).then_inc(*ev.mark("dve", "am"))
                    dve.wait_ge(*ev.last("dve"))
                    V.tensor_scalar(small[:, s0 + 1:s0 + 2], small[:, s0:s0 + 1], pr(l, "sink", hd), -1.0,
                                       ALU.max, ALU.mult).then_inc(*ev.mark("dve", "anm", l, t, hd))
                    dve.wait_ge(*ev.at("ap", l, t, hd))
                    V.tensor_tensor(small[:, s0 + 4:s0 + 5], small[:, s0 + 2:s0 + 3], small[:, s0 + 3:s0 + 4],
                                       ALU.add).then_inc(*ev.mark("dve", "aden"))
                    dve.wait_ge(*ev.last("dve"))
                    V.reciprocal(small[:, s0 + 5:s0 + 6], small[:, s0 + 4:s0 + 5]).then_inc(*ev.mark("dve", "ard"))
                    dve.wait_ge(*ev.last("dve"))
                    dve.wait_ge(*ev.at("apv", l, t, hd))
                    V.tensor_scalar(ay[:, t % 2, hd * AD:(hd + 1) * AD], psm[:, 3, 128:192],
                                       small[:, s0 + 5:s0 + 6], None, ALU.mult).then_inc(*ev.mark("dve", "ay", l, t, hd))
                elif kind == "rqk":
                    if hd == 0:
                        dve.wait_ge(*ev.last("dve"))
                        x = small[:, 48:56]
                        dve.wait_ge(*ev.at("rabs", l))
                        V.scalar_tensor_tensor(out=small[:, 40:48], in0=pr(l, "ret", 0, 8), scalar=0.0,
                                                  in1=x, op0=ALU.min, op1=ALU.subtract).then_inc(*ev.mark("dve", "logg", l))
                    for ct in (0, 1):
                        for n, ct_, (q, t0, size) in banks_a(st):
                            if ct_ != ct:
                                continue
                            dve.wait_ge(*ev.at("bank", n))
                            dve.wait_ge(*ev.at("rope", st["region"]))
                            if st["prev_head"] is not None:
                                dve.wait_ge(*ev.at("pe_step", st["prev_head"]))
                                dve.wait_ge(*ev.at("pool_step", st["prev_head"]))
                            dve.wait_ge(*ev.at("rsw", l, hd, ct, q))
                            x = rqk[:, ct, t0:t0 + size]
                            V.tensor_tensor(x, psg[:, n % 4, 0:size], roper[:, 0, t0:t0 + size], ALU.mult).then_inc(*ev.mark("dve", "bank_free", n))
                            V.tensor_tensor(rtmp[:, t0:t0 + size], rtmp[:, t0:t0 + size],
                                               roper[:, 1, t0:t0 + size], ALU.mult).then_inc(*ev.mark("dve", "r"))
                            dve.wait_ge(*ev.last("dve"))
                            V.tensor_tensor(x, x, rtmp[:, t0:t0 + size], ALU.add).then_inc(*ev.mark("dve", "rqk", l, hd))
                        ev.now[("rtmp_done", l, hd, ct)] = {"dve": ev.count["dve"]}
                    dve.wait_ge(*ev.at("rdec", l, hd))
                    V.scalar_tensor_tensor(out=rd[:, 0, :], in0=rd[:, 0, :], scalar=R_SCALE, in1=c("upto"),
                                              op0=ALU.mult, op1=ALU.mult).then_inc(*ev.mark("dve", "r"))
                    V.scalar_tensor_tensor(out=rd[:, 1, :], in0=rd[:, 1, :], scalar=R_SCALE, in1=c("since"),
                                              op0=ALU.mult, op1=ALU.mult).then_inc(*ev.mark("dve", "r"))
                    dve.wait_ge(*ev.last("dve"))
                    V.tensor_tensor(rd[:, 0, :], rd[:, 0, :], rd[:, 1, :], ALU.add).then_inc(*ev.mark("dve", "rdecD", l, hd))
                    dve.wait_ge(*ev.at("rcd", l, hd))
                    V.tensor_scalar(small[:, 60:62], small[:, 56:58], R_SCALE, None, ALU.mult).then_inc(*ev.mark("dve", "rw", l, hd))
                elif kind == "rg":
                    for n, tt in banks_b(st):
                        dve.wait_ge(*ev.at("rgt", l, hd, tt[0]))
                        ps = psg[:, n % 4, :].rearrange("p (j c) -> p j c", j=2)
                        x = rg[:, tt[0]:tt[0] + 2, :]
                        V.scalar_tensor_tensor(out=x, in0=x, scalar=1.0, in1=ps, op0=ALU.add, op1=ALU.mult).then_inc(*ev.mark("dve", "bank_free", n))
                        ev.now[("rg_sb", l, hd)] = {"dve": ev.count["dve"]}
                elif kind == "rback":
                    s_ = st["s"]
                    if s_ == 0:
                        if st["prev_head"] is not None:
                            dve.wait_ge(*ev.at("pe_step", st["prev_head"]))
                        dve.wait_ge(*ev.last("dve"))
                        V.memset(rb[:, 0, :], 0.0).then_inc(*ev.mark("dve", "z"))
                        V.memset(rf[:, 0, :], 0.0).then_inc(*ev.mark("dve", "z"))
                        ev.now[("rR", l, hd, "f", 0)] = {"dve": ev.count["dve"]}
                        ev.now[("rR", l, hd, "b", 0)] = {"dve": ev.count["dve"]}
                    dve.wait_ge(*ev.at("rkv", l, hd, "b", s_))
                    dve.wait_ge(*ev.last("dve"))
                    V.scalar_tensor_tensor(out=rb[:, s_ + 1, :], in0=rb[:, s_, :], scalar=small[:, 59:60],
                                              in1=psm[:, 2, 0:RV], op0=ALU.mult, op1=ALU.add).then_inc(*ev.mark("dve", "rR", l, hd, "b", s_ + 1))
                elif kind == "rtile":
                    if st["out"]:
                        dve.wait_ge(*ev.at("rscore", l, hd, t))
                        V.tensor_tensor(rs[:, 0, :], psm[:, 0, 0:P], rd[:, 0, :], ALU.mult).then_inc(*ev.mark("dve", "rs", l, hd, t))
                        dve.wait_ge(*ev.at("rout", l, hd, t))
                        dve.wait_ge(*ev.last("dve"))
                        head_norm(dve, psm[:, 1, 0:RV], "r", l, hd, t)
                        V.tensor_scalar(ry[:, 0, :], psm[:, 1, 0:RV], small[:, 36:37], small[:, 39:40],
                                           ALU.subtract, ALU.mult).then_inc(*ev.mark("dve", "rnormed", l, hd, t))
                        dve.wait_ge(*ev.last("dve"))
                        dve.wait_ge(*ev.at("rg_sb", l, hd))
                        V.scalar_tensor_tensor(out=ry[:, 1, :], in0=ry[:, 0, :], scalar=0.5, in1=rg[:, t, :],
                                                  op0=ALU.mult, op1=ALU.mult).then_inc(*ev.mark("dve", "ry", l, hd, t))
                    if t < TILES - 1:
                        dve.wait_ge(*ev.at("rkv", l, hd, "f", t))
                        dve.wait_ge(*ev.last("dve"))
                        if st["out"]:
                            dve.wait_ge(*ev.at("rout", l, hd, t))
                        V.scalar_tensor_tensor(out=rf[:, (t + 1) % 2, :], in0=rf[:, t % 2, :],
                                                  scalar=small[:, 58:59], in1=psm[:, 2, 0:RV], op0=ALU.mult,
                                                  op1=ALU.add).then_inc(*ev.mark("dve", "rR", l, hd, "f", t + 1))

        @block.gpsimd
        def _(pool):
            G = nc.gpsimd

            pool.wait_ge(*ev.at("const"))
            for i, st in walk("pool"):
                kind, s = st["kind"], st["slot"]
                l, hd, t = st.get("l"), st.get("hd"), st.get("t")
                if kind == "region":
                    phase_end(pool, i)
                if kind == "split":
                    n = s["kt"] * s["cols"]
                    pool.wait_ge(*ev.at("head", s["n"]))
                    G.tensor_tensor(wl[:, s["sp"] % 2, 0:n], raw[:, s["n"] % 2, 0:n],
                                       wh[:, s["sp"] % 2, 0:n].bitcast(F32), ALU.subtract).then_inc(*ev.mark("pool", "rest", s["n"]))
                    ev.now[("raw_free", s["n"])] = {"pool": ev.count["pool"]}
                elif kind == "norm":
                    pool.wait_ge(*ev.at("ms", st["id"]))
                    G.tensor_tensor(small[:, 2:3], small[:, 1:2], c("neg_half"), ALU.pow).then_inc(*ev.mark("pool", "rstd", st["id"]))
                    if st["use"] != "last":
                        ts = slice(t * P, (t + 1) * P)
                        pool.wait_ge(*ev.at("hh", st["id"]))
                        G.tensor_tensor(hl[:, :, ts], hf[:], hh[:, :, ts].bitcast(F32), ALU.subtract).then_inc(*ev.mark("pool", "h", st["gen"], t))
                elif kind == "up":
                    u = st["u"]
                    pool.wait_ge(*ev.at("uh", l, u))
                    t0 = 0 if st["ctx"] else CTX
                    G.tensor_tensor(ul[:, u % URING, t0:TOK], fu[:, t0:TOK],
                                       uh[:, u % URING, t0:TOK].bitcast(F32), ALU.subtract).then_inc(*ev.mark("pool", "u", l, u))
                elif kind == "mgates":
                    pool.wait_ge(*ev.at("A", l))
                    G.partition_all_reduce(gm[:, 0, :], gm[:, 4, :], P, bass.bass_isa.ReduceOp.max).then_inc(*ev.mark("pool", "cmax", l))
                elif kind == "mback" or kind == "mtile" and t < TILES - 1:
                    d, s_ = ("b", st["s"]) if kind == "mback" else ("f", t)
                    t_ = BACK[s_] if d == "b" else t
                    col = (24 if d == "b" else 0) + s_ * 4 + hd
                    pool.wait_ge(*ev.at("mcols", l))
                    pool.wait_ge(*ev.at("mv", l, hd, t_ // 2))
                    pool.wait_ge(*ev.at("pads", st["region"]))
                    if s_ >= 2:
                        pool.wait_ge(*ev.at("mkv", l, hd, d, s_ - 2))
                    elif d == "f":
                        pool.wait_ge(*ev.at("mkv", l, hd, "b", TILES - 2))
                    elif hd:
                        pool.wait_ge(*ev.at("mkv", l, hd - 1, "f", TILES - 2))
                    G.tensor_scalar(mvw[:, s_ % 2, :], mv[:, t_, :], gm[:, 6, col:col + 1], None, ALU.mult).then_inc(*ev.mark("pool", "mvw", l, hd, d, s_))
                if kind in ("mtile", "rtile") and st["out"]:
                    r_ = kind[0]
                    if r_ == "r":
                        pool.wait_ge(*ev.at("rqk", l, hd))
                        pool.wait_ge(*ev.at("rrow", l, hd))
                        if st["prev"] is not None:
                            pool.wait_ge(*ev.at("pe_step", st["prev"]))
                        for d in range(2):
                            G.tensor_tensor(rs[:, 1 + d, :], rqk[:, 0, t * P:(t + 1) * P], rd[:, 1 + d, :],
                                               ALU.mult).then_inc(*ev.mark("pool", "rq", l, hd, t))
                if kind == "rback" or kind == "rtile" and t < TILES - 1:
                    d, s_ = ("b", st["s"]) if kind == "rback" else ("f", t)
                    t_ = BACK[s_] if d == "b" else t
                    pool.wait_ge(*ev.at("rw", l, hd))
                    pool.wait_ge(*ev.at("rv_sb", l, hd))
                    if s_ >= 2:
                        pool.wait_ge(*ev.at("rkv", l, hd, d, s_ - 2))
                    elif d == "f":
                        pool.wait_ge(*ev.at("rkv", l, hd, "b", TILES - 2))
                    elif hd:
                        pool.wait_ge(*ev.at("rkv", l, hd - 1, "f", TILES - 2))
                    cc = 61 if d == "b" else 60
                    G.tensor_scalar(rvw[:, s_ % 2, :], rv[:, t_, :], small[:, cc:cc + 1], None, ALU.mult).then_inc(*ev.mark("pool", "rvw", l, hd, d, s_))
                if kind in ("mtile", "rtile") and st["out"]:
                    r_ = kind[0]
                    pool.wait_ge(*ev.at(r_ + "var", l, hd, t))
                    G.tensor_tensor(small[:, 39:40], small[:, 38:39], c("neg_half"), ALU.pow).then_inc(*ev.mark("pool", r_ + "rstd", l, hd, t))
                if kind == "branch" and st["br"] != "m":
                    cs = slice(st["n"] * COLS, (st["n"] + 1) * COLS)
                    for n, tt in banks_b(st):
                        pool.wait_ge(*ev.at("gated", l, st["br"], st["n"], tt[0]))
                        x = acc[:, tt[0]:tt[0] + 2, cs]
                        G.tensor_tensor(x, x, bt[:, n % 2, :].rearrange("p (j c) -> p j c", j=2), ALU.add).then_inc(*ev.mark("pool", "summed", n))
        return ev.now


def arena_offset(nc, arena):
    return nc.sbuf_base - 71 * 1024


def build(bacc, args, shape, stop=None):
    known = None
    for _ in range(2):
        nc = bacc.Bacc("TRN2", target_bir_lowering=False, num_devices=1)
        ins = {k: nc.dram_tensor(f"in_{k}", v.shape, F32, kind="ExternalInput").ap() for k, v in args.items()}
        out = nc.dram_tensor("out", shape, F32, kind="ExternalOutput").ap()
        known = backbone(nc, ins, out, known, stop)
    return nc


def layout(inputs, stop=None):
    consts, _, rope_a, rope_r = constants()
    PP, NPAR = param_places()
    plan, stream = make_plan()
    if stop is not None:
        used = {id(s["slot"]) for s in plan[:stop] if s["slot"] is not None}
        stream = [s for s in stream if id(s) in used]
    g = {k: np.ascontiguousarray(v) for k, v in inputs.items()}
    flat = np.empty(sum(s["kt"] * s["cols"] * P for s in stream), np.float32)
    off = 0
    for s in stream:
        name, row, cols = s["blocks"]
        w = g[name][s["l"], row:row + s["kt"] * P]
        w = np.concatenate([w[:, a:a + n] for a, n in cols], 1)
        n = w.size
        flat[off:off + n] = w.reshape(s["kt"], P, -1).transpose(1, 0, 2).ravel()
        off += n
    par = np.empty((P, DEPTH, NPAR), np.float32)
    for l in range(DEPTH):
        tap = g["m_conv_w"][l]
        rows = {
            "mod_b": g["mod_b"][l], "norm1": g["norm1_w"][l], "norm2": g["norm2_w"][l],
            "conv_q": tap[:, :MH * P].ravel(), "conv_k": tap[:, MH * P:].ravel(), "m_norm": g["m_norm_w"][l],
            "r_norm": g["ret_norm_w"][l], "f_conv": g["ffn_conv_w"][l].ravel(), "f_bias": g["ffn_conv_b"][l]}
        for k, v in rows.items():
            a, n = PP[k]
            par[:, l, a:a + n] = v.reshape(n, P).T
        for k, v in (("sink", g["a_sink"][l]), ("ret", g["ret_logit"][l].ravel()), ("gate", g["m_gate_bias"][l])):
            a, n = PP[k]
            par[:, l, a:a + n] = v[None, :]
    cvec = np.stack([g["c_ctx"].reshape(KD, P), g["c"][0].reshape(KD, P)], 0).transpose(2, 1, 0)
    return {"stream": flat, "consts": consts, "params": par, "cvec": np.ascontiguousarray(cvec),
            "rope_a": rope_a, "rope_r": rope_r, "mod_b": g["mod_b"], "final_w": g["final_norm_w"][None, :],
            "x": g["x"], "ctx": g["ctx"]}


def kernel(**inputs):
    from concourse.bass_utils import run_bass_kernel_spmd as run
    import concourse.bacc as bacc
    args = layout(inputs)
    nc = build(bacc, args, inputs["x"].shape)
    r = run(nc, [{f"in_{k}": v for k, v in args.items()}], core_ids=[0])
    return r.results[0]["out"]
```

```python
from contextlib import ExitStack
from itertools import chain, islice

import numpy as np
import concourse.bass as bass
from concourse import mybir

F32, F32R = mybir.dt.float32, mybir.dt.float32r
ALU, ACT, AX = mybir.AluOpType, mybir.ActivationFunctionType, mybir.AxisListType

P = 128
D, SEQ, CTX, DEPTH, GRID_W = 1024, 512, 256, 2, 64
KD = D // P
TILES, CT = (SEQ + CTX) // P, CTX // P
TOK = SEQ + CTX
MH, AH, AKV, RH, RV = 4, 8, 2, 4, 256
AD = 64
FFN = 2816
FT = FFN // P
GROUP = 4
RING = 3
URING = 6
ARENA_BYTES = 74 * 1024
EPS = 1e-6
NEG = -1e30
COLS = 256
SLOT = KD * COLS
PADDED = TOK + 4
BACK = [1, 0, 5, 4, 3, 2]
M_SCALE = 0.25 * P ** -0.5
R_SCALE = P ** -0.5
IN_OFF = dict(mq=0, mk=512, mv=1024, mo=1536, mg=2048, aq=2064, ak=2576, av=2704, rq=2832, rk=3344,
              rv=3856, rg=4880, gm=5904, ga=6928, gr=7952)


def at_tile(t):
    return 1 + P * t + (2 if t >= CT else 0)


def constants():
    r, j = np.meshgrid(np.arange(P), np.arange(P), indexing="ij")
    rot = np.zeros((P, P), np.float32)
    for m in range(P):
        if m % 32 < 16:
            rot[m + 16, m] = -1.0
        else:
            rot[m - 16, m] = 1.0
    window = np.concatenate([np.where(j >= r, 0.0, NEG), np.zeros((P, P)), np.where(j <= r, 0.0, NEG)], 1)
    parts = dict(
        ident=np.eye(P), upto=(r <= j), since=(r >= j), ones=np.ones((P, P)),
        hide_f=np.where(r <= j, 0.0, NEG), hide_b=np.where(r >= j, 0.0, NEG), window=window,
        ahead=np.maximum(j - r, 0), behind=np.maximum(r - j, 0), row_f=j + 1, row_b=P - j,
        col_f=127 - r[:, :1], col_b=r[:, :1], rot=rot, flip=np.eye(P)[::-1],
        neg_half=np.full((P, 1), -0.5), one=np.ones((P, 1)), cd=np.full((P, 1), float(P)))
    place, cols = {}, []
    n = 0
    for k, v in parts.items():
        place[k] = (n, n + v.shape[1])
        cols.append(v.astype(np.float32))
        n += v.shape[1]
    f = np.float32
    inv16 = (f(10000.0) ** (-np.arange(16, dtype=f) / f(16))).astype(f)
    t = np.arange(SEQ)
    ang = np.zeros((P, SEQ), f)
    for m in range(P):
        pos = (t // GRID_W) if m % 64 < 32 else (t % GRID_W)
        ang[m] = pos.astype(f) * inv16[m % 16]
    rope_a = np.stack([np.cos(ang), np.sin(ang)], 1).astype(f)
    inv64 = (f(10000.0) ** (-np.arange(64, dtype=f) / f(64))).astype(f)
    ang = np.arange(TOK).astype(f)[None, :] * inv64[np.arange(P) % 64][:, None]
    sign = np.where(np.arange(P) < 64, -1.0, 1.0)[:, None]
    rope_r = np.stack([np.cos(ang), np.sin(ang) * sign], 1).astype(f)
    return np.concatenate(cols, 1), place, rope_a, rope_r


def param_places():
    sizes = [("mod_b", 48), ("norm1", 8), ("norm2", 8), ("conv_q", 12), ("conv_k", 12), ("m_norm", 4),
             ("r_norm", 8), ("f_conv", 3 * FT), ("f_bias", FT), ("sink", AH), ("ret", 2 * RH), ("gate", 16)]
    place, n = {}, 0
    for k, s in sizes:
        place[k] = (n, s)
        n += s
    return place, n


def make_plan():
    plan, stream, bank, split = [], [], [0], [0]

    def slot(l, blocks, kt=KD, splits=True):
        s = dict(n=len(stream), l=l, blocks=blocks, kt=kt, cols=sum(b[1] for b in blocks[2]), sp=None)
        if splits:
            s["sp"] = split[0]
            split[0] += 1
        stream.append(s)
        return s

    def step(kind, slot=None, banks=0, **k):
        if "piece" in k:
            if k["piece"] == 0:
                slot["bank"], banks = bank[0], 1
            k.update(kind=kind, slot=slot, bank=slot["bank"])
        else:
            if not k.get("ctx", True):
                banks = {"mqk": 3, "rqk": 3, "mvo": 3}.get(kind, 2)
            k.update(kind=kind, slot=slot, bank=bank[0])
        bank[0] += banks
        plan.append(k)

    def seqs(ctx):
        return ((0, 0, CTX), (1, CTX, SEQ)) if ctx else ((1, CTX, SEQ),)

    def pairs(ctx):
        return (0, 1, 2) if ctx else (1, 2)

    def cols(name, l, c0, n=COLS, kt=KD, row=0, splits=True):
        return slot(l, (name, row, [(c0, n)]), kt, splits)

    def modulation():
        for l in range(DEPTH):
            for n in range(6 * D // COLS):
                s = cols("mod_w", l, n * COLS, splits=False)
                for piece in range(5):
                    yield step("vector", s, l=l, n=n, piece=piece)

    spread = modulation()

    def vectors(count):
        for _ in islice(spread, 5 * count):
            pass

    def gate(l, which, n, h, ctx):
        c0 = IN_OFF[{"m": "gm", "a": "ga", "r": "gr"}[which]] + n * COLS
        s = cols("w_in", l, c0)
        for pair in pairs(ctx):
            for piece in range(4):
                yield step("gate", s, l=l, gen=h, br=which, n=n, ctx=ctx, pair=pair, piece=piece,
                           open=pair != pairs(ctx)[-1])

    def ticks(kind, count, fill=iter(()), pieces=0, **k):
        before = 0
        for i in range(count):
            step(kind, ticks=range(i, i + 1), **k)
            upto = round((i + 1) * pieces / count)
            for _ in islice(fill, upto - before):
                pass
            before = upto

    gen = 0
    step("setup")
    for l in range(DEPTH):
        ctx = l < DEPTH - 1
        tiles = list(range(0 if ctx else CT, TILES))
        if l == 0:
            vectors(2 * D // COLS)
            step("affine", l=0, which=0)
            step("region", name="norm")
            step("norms", l=0, use="first", tiles=list(range(TILES)), gen=gen)
        h = gen
        o = IN_OFF

        def aq_slot(g):
            return slot(l, ("w_in", 0, [(o["aq"] + (2 * g + i + 4 * half) * AD, AD)
                                        for i in range(2) for half in range(2)]))

        step("region", name="mlstm")
        step("mgates", slot(l, ("w_in", 0, [(o["mg"], 16)])), 2, l=l, gen=h)
        s = None
        for hd in range(MH):
            s = s or slot(l, ("w_in", 0, [(o["mq"] + hd * P, P), (o["mk"] + hd * P, P)]))
            step("mqk", s, 4, l=l, gen=h, hd=hd, ctx=ctx)
            if hd == 0:
                step("mgates2", l=l)
            step("mvo", slot(l, ("w_in", 0, [(o["mv"] + hd * P, P), (o["mo"] + hd * P, P)])), 3, l=l, gen=h,
                 hd=hd, ctx=ctx)
            if hd == 0:
                step("mgates3", l=l)
            fill = gate(l, "m", hd, h, ctx)
            ticks("mstates", 4, fill, 4, l=l, hd=hd, ctx=True)
            s = slot(l, ("w_in", 0, [(o["mq"] + (hd + 1) * P, P), (o["mk"] + (hd + 1) * P, P)])) \
                if hd + 1 < MH else cols("w_br_m", l, 0, kt=4)
            pieces = 4 * len(pairs(ctx)) + 1
            fill = chain(islice(spread, 5), fill)
            ticks("mtiles", len(tiles) + 5, fill, pieces, l=l, hd=hd, tiles=tiles)
        step("region", name="branch")
        step("ysplit", l=l, br="m", kt=4, tiles=tiles)
        for n in range(4):
            branch(step, cols, l, ctx, "m", n, None if n else s)
        step("region", name="attn")
        step("aq", aq_slot(0), 4, l=l, gen=h, g=0, ctx=ctx)
        step("akv", slot(l, ("w_in", 0, [(o["ak"], P), (o["av"], P)])), 5, l=l, gen=h)
        step("arot", l=l, g=0, first=True)
        step("aq", aq_slot(1), 4, l=l, gen=h, g=1, ctx=ctx)
        step("arot", l=l, g=2, first=False)
        step("arot", l=l, g=1, first=False)
        count = AH * len(tiles) + 2
        fill = chain(*[gate(l, "a", n, h, ctx) for n in range(3)])
        ticks("attend", AH * len(tiles) + 3, fill, 12 * len(pairs(ctx)), l=l,
              heads=[(t, hd) for t in tiles for hd in range(AH)])
        step("region", name="branch")
        step("ysplit", l=l, br="a", kt=4, tiles=tiles)
        step("gate", cols("w_in", l, o["ga"] + 3 * COLS), 3, l=l, gen=h, br="a", n=3, ctx=ctx)
        for n in range(4):
            branch(step, cols, l, ctx, "a", n)
        step("region", name="ret")
        s = slot(l, ("w_in", 0, [(o["rq"], P), (o["rk"], P)]))
        for hd in range(RH):
            step("rqk", s, 4, l=l, gen=h, hd=hd, ctx=ctx)
            step("rv", cols("w_in", l, o["rv"] + hd * RV), 3, l=l, gen=h, hd=hd)
            step("rg", cols("w_in", l, o["rg"] + hd * RV), 3, l=l, gen=h, hd=hd, ctx=ctx)
            s = slot(l, ("w_in", 0, [(o["rq"] + (hd + 1) * P, P), (o["rk"] + (hd + 1) * P, P)])) \
                if hd + 1 < RH else cols("w_in", l, o["gr"])
            ticks("rstates", 4, spread, 4, l=l, hd=hd)
            ticks("rtiles", len(tiles) + 4, spread, 11, l=l, hd=hd, tiles=tiles)
        step("region", name="branch")
        step("ysplit", l=l, br="r", kt=8, tiles=tiles)
        for n in range(4):
            step("gate", cols("w_in", l, o["gr"] + n * COLS) if n else s, 3, l=l, gen=h, br="r", n=n, ctx=ctx)
            branch(step, cols, l, ctx, "r", n)
        step("region", name="norm")
        first = 0 if ctx else CT
        gen += 1
        step("gates", None, 4, l=l, which=0, ctx=ctx)
        step("turns", l=l, tiles=tiles, gen=gen)
        for n in range(4):
            step("wout", cols("w_out", l, n * COLS), 3, l=l, gen=gen, n=n, ctx=ctx)
        step("affine", l=l, which=1)
        gen += 1
        step("norms", l=l, use="mid", tiles=tiles, gen=gen)
        step("gates", None, 4, l=l, which=1, ctx=ctx)
        step("region", name="mlp")
        down = 0
        for u in range(FT):
            step("up", slot(l, ("ffn_up", 0, [(u * P, P), (FFN + u * P, P)])), 4, l=l, gen=gen, u=u, ctx=ctx)
            if ctx and 1 <= u <= 2 * D // COLS:
                vectors(1)
            if u >= GROUP and u % GROUP == 0 or u == FT - 1:
                while down * GROUP < FT and (down + 1) * GROUP <= u or (u == FT - 1 and down * GROUP < FT):
                    kt = min(GROUP, FT - down * GROUP)
                    for half in range(2):
                        step("down", slot(l, ("ffn_down", down * GROUP * P, [(half * 512, 512)]), kt),
                             TILES - first, l=l, g=down, half=half, kt=kt, first=first)
                    down += 1
        last = l == DEPTH - 1
        step("region", name="final" if last else "norm")
        if not last:
            step("affine", l=l + 1, which=0)
        gen += 1
        step("norms", l=l, use="last" if last else "end", tiles=tiles, gen=gen)
    splits = [s for s in stream if s["sp"] is not None]
    order, done, used = [], 0, set()
    for st in plan:
        if st["kind"] == "norms" and st["use"] == "first":
            while done < 2:
                order.append(dict(kind="split", slot=splits[done]))
                done += 1
        if st["slot"] is not None:
            n, sp = st["slot"]["n"], st["slot"]["sp"]
            upto = done if sp is None else sp + 1
            if sp is not None and not st.get("open") and sp + 1 < len(splits):
                waiting = [s["n"] for s in stream[n:splits[sp + 1]["n"]] if s["sp"] is None and s["n"] not in used]
                upto += len(waiting) <= 1
            while done < upto:
                order.append(dict(kind="split", slot=splits[done]))
                done += 1
            if sp is None:
                used.add(n)
        order.append(st)
    annotate(order)
    return order, stream


MIXING = ("norms", "turns", "mgates", "mgates2", "mgates3", "arot", "mstates", "mtiles", "attend",
          "rstates", "rtiles")


def annotate(order):
    last, head_end, downs, norms = {}, {}, {}, []
    for i, st in enumerate(order):
        kind = st["kind"]
        st["i"] = i
        own_banks = kind == "arot" and not st["first"] or st.get("ticks", range(1)).start > 0
        st["prev"] = None if own_banks else last.get("mixing")
        st["region"] = last.get("region")
        st["h_slot"] = last.get("h")
        st["prev_branch"] = last.get("branch")
        if kind in MIXING:
            last["mixing"] = i
        if kind in ("region", "branch"):
            last[kind] = i
        if st.get("gen") is not None and st["slot"] is not None:
            last["h"] = st["slot"]["n"]
        if kind[0] in "mr" and "hd" in st:
            st["prev_head"] = head_end.get((kind[0], st["l"], st["hd"] - 1))
            if kind in ("mtiles", "rtiles"):
                head_end[kind[0], st["l"], st["hd"]] = i
        if kind == "down":
            for u in range(st["g"] * GROUP, st["g"] * GROUP + st["kt"]):
                downs[st["l"], u] = st["slot"]["n"]
        if kind == "up":
            st["ring_free"] = downs.get((st["l"], st["u"] - URING))
        if kind == "norms":
            st["back"] = {t: (n["i"], n["tiles"].index(t)) for n in norms for t in st["tiles"]}
            norms += [st] if st["use"] in ("mid", "end") else []
        if kind == "region":
            n = norms[-1] if norms else None
            st["stores"] = [(n["i"], len(n["tiles"]) - 3 + b) for b in range(3)] if n else []


def branch(step, cols, l, ctx, which, n, s=None):
    name = {"m": "w_br_m", "a": "w_br_a", "r": "w_br_r"}[which]
    kt = 8 if which == "r" else 4
    step("branch", s or cols(name, l, n * COLS, kt=kt), 3, l=l, br=which, n=n, ctx=ctx, kt=kt)


class Events:

    def __init__(self, known, sems):
        self.known, self.sems, self.count, self.now = known, sems, {}, {}

    def mark(self, sem, *key, by=1):
        self.count[sem] = self.count.get(sem, 0) + by
        self.now.setdefault(key, {})[sem] = self.count[sem]
        return self.sems(sem), by

    def at(self, *key):
        if self.known is None:
            return self.sems("dry_run"), 1
        (sem, value), = self.known[key].items()
        return self.sems(sem), value

    def last(self, sem):
        return self.sems(sem), self.count.get(sem, 0)


def backbone(nc, ins, out, known, stop=None):
    consts_np, CP, _, _ = constants()
    PP, NPAR = param_places()
    PLAN, STREAM = make_plan()
    if stop is not None:
        PLAN = PLAN[:stop]
        used = {id(s["slot"]) for s in PLAN if s["slot"] is not None}
        STREAM = [s for s in STREAM if id(s) in used]
    seqs = {True: ((0, 0, CTX), (1, CTX, SEQ)), False: ((1, CTX, SEQ),)}

    with ExitStack() as ctx:
        semaphores = {}

        def semaphore(name):
            if name not in semaphores:
                semaphores[name] = ctx.enter_context(nc.semaphore(name))
            return semaphores[name]

        ev = Events(known, semaphore)

        def sb(name, shape, dt=F32):
            return ctx.enter_context(nc.sbuf_tensor(name, shape, dt))

        psg = ctx.enter_context(nc.psum_tensor("psum_products", [P, RING, 512], F32))
        psm = ctx.enter_context(nc.psum_tensor("psum_mixers", [P, 8 - RING, 512], F32))
        hh = sb("h_head", [P, KD, TOK], F32R)
        hl = sb("h_rest", [P, KD, TOK], F32R)
        acc = sb("acc", [P, TILES, D])
        raw = sb("raw", [P, 2, SLOT])
        wh = sb("w_head", [P, 2, SLOT], F32R)
        wl = sb("w_rest", [P, 2, SLOT], F32R)
        const = sb("const", [P, consts_np.shape[1]])
        par = sb("par", [P, DEPTH, NPAR])
        cvec = sb("cvec", [P, 3, KD, 2])
        vrow = sb("vrow", [P, COLS])
        vec = sb("vec", [P, DEPTH, 6 * KD, 2])
        aff = sb("aff", [P, 2, 2, KD, 2])
        small = sb("small", [P, 128])
        arena_size = ARENA_BYTES
        arena = sb("arena", [P, arena_size // 4])

        class Region:

            def __init__(self, start=0):
                self.off = start

            def __call__(self, name, shape, dt=F32):
                n = int(np.prod(shape[1:])) * 4
                t = nc.alloc_sbuf_tensor_at(name, shape, dt, offset=ARENA + self.off)
                self.off += -(-n // 32) * 32
                assert self.off <= arena_size, (name, self.off)
                return t

        ARENA = arena_offset(nc, arena)
        R = Region()
        gate_b = R("gate_b", [P, 2, D])
        stage = R("stage", [P, 3, D])
        bias_b = R("bias_b", [P, D])
        xs = R("xs", [P, 2, D])
        hf = R("hf", [P, 2, KD, P])
        R = Region(8 * 1024)
        uh = R("u_head", [P, URING, TOK], F32R)
        ul = R("u_rest", [P, URING, TOK], F32R)
        fa = R("f_a", [P, 2, PADDED])
        fc = R("f_c", [P, PADDED])
        ft = R("f_t", [P, TOK])
        fb = R("f_b", [P, TOK])
        fu = R("f_u", [P, TOK])
        R = Region()
        yT = R("yT", [P, 8, TOK])
        yh = Region(34 * 1024)("y_head", [P, 8, TOK], F32R)
        yl = Region()("y_rest", [P, 8, TOK], F32R)
        R = Region(12 * 1024)
        gm = R("gm", [P, 12, 48])
        g16 = R("g16", [P, TILES, 16])
        atr = R("atr", [P, 4, P])
        ma = R("m_a", [P, 2, PADDED])
        mc = R("m_c", [P, 2, PADDED])
        mt = R("m_t", [P, 2, PADDED])
        mqk = R("m_qk", [P, 2, PADDED])
        here = R.off
        mktok = R("m_ktok", [P, TILES, P])
        grow = Region(here)("m_grow", [P, TOK])
        mv = R("m_v", [P, TILES, P + 1])
        mo = R("m_o", [P, TILES, P])
        mcb = R("m_cb", [P, TILES, P + 1])
        mcf = R("m_cf", [P, TILES, P + 1])
        mvw = R("m_vw", [P, 4, P + 1])
        msc = R("m_sc", [P, 2, 4, P])
        mnd = R("m_nd", [P, 2, 4, P + 1])
        my = R("m_y", [P, 2, 3, P])
        R = Region(12 * 1024)
        ropea = R("rope_a", [P, 2, SEQ])
        aq = R("a_q", [P, 4, TOK])
        ak = R("a_k", [P, TOK])
        av = R("a_v", [P, TILES, P])
        atmp = R("a_tmp", [P, SEQ])
        asb = R("a_s", [P, 4, 640])
        apt = R("a_pt", [P, 2, 640])
        ay = R("a_y", [P, 2, 512])
        tga = R("a_tg", [P, 3, TILES, COLS])
        R = Region(24 * 1024)
        roper = R("rope_r", [P, 2, TOK])
        rqk = R("r_qk", [P, 2, TOK])
        rktok = R("r_ktok", [P, TILES, P])
        rv = R("r_v", [P, TILES, RV])
        rg = R("r_g", [P, TILES, RV])
        rb = R("r_b", [P, TILES - 1, RV])
        rf = R("r_f", [P, TILES - 1, RV])
        rvw = R("r_vw", [P, 4, RV])
        rs = R("r_s", [P, 2, 3, P])
        rd = R("r_d", [P, 3, P])
        here = R.off
        ry = R("r_y", [P, 2, 2, RV])
        rtmp = Region(here)("r_tmp", [P, TOK])
        R = Region(24 * 1024)
        tg = R("tg", [P, TILES, COLS])
        bt = R("bt", [P, 2, 512])

        def c(name):
            a, b = CP[name]
            return const[:, a:b]

        def pr(l, name, i=0, n=1):
            return par[:, l, PP[name][0] + i:PP[name][0] + i + n]

        res = nc.dram_tensor("residual", (TILES, P, D), F32, kind="Internal").ap()

        def raw_of(s):
            return raw[:, s["n"] % 2, 0:s["kt"] * s["cols"]].rearrange("p (k c) -> p k c", k=s["kt"])

        def halves(s):
            n = s["kt"] * s["cols"]
            a = wh[:, s["sp"] % 2, 0:n].rearrange("p (k c) -> p k c", k=s["kt"])
            b = wl[:, s["sp"] % 2, 0:n].rearrange("p (k c) -> p k c", k=s["kt"])
            return a, b

        def banks_a(st):
            out_, n = [], st["bank"]
            for ct in range(2):
                if st["kind"] in ("akv", "mgates") and ct == 1:
                    continue
                both = st.get("ctx", True) or st["kind"] in ("mqk", "rqk") and ct == 1
                for q in seqs[both]:
                    out_.append((n, ct, q))
                    n += 1
            return out_

        def banks_b(st):
            n = st["bank"] + (2 if st["kind"] == "akv" else 0)
            if "pair" in st:
                return [(n, (2 * st["pair"], 2 * st["pair"] + 1))]
            both = st.get("ctx", True) or st["kind"] == "mvo"
            return [(n + i, (2 * p_, 2 * p_ + 1)) for i, p_ in enumerate((0, 1, 2) if both else (1, 2))]

        def gate_banks(st):
            which = [(q, half) for q in ((0, 1) if st["ctx"] else (1,)) for half in range(2)]
            return [(st["bank"] + i, q, half) for i, (q, half) in enumerate(which)]

        def gate_place(st, t):
            if st["br"] == "m":
                return acc[:, t:t + 2, st["n"] * COLS:(st["n"] + 1) * COLS]
            if st["br"] == "a" and st["n"] < 3:
                return tga[:, st["n"], t:t + 2, :]
            return tg[:, t:t + 2, :]

        def state_turns(st):
            return [j for j in range(2 * (TILES - 1)) if j // 4 + 1 in st["ticks"]]

        def weigh_values(eng, name, scaled, st, j):
            r_, l, hd = st["kind"][0], st["l"], st["hd"]
            d, s_ = j % 2, j // 2
            t = BACK[s_] if d else s_
            if j < 2:
                eng.wait_ge(*(ev.at("mcols", l) if r_ == "m" else ev.at("rw", l, hd)))
                eng.wait_ge(*(ev.at("mv", l, hd, 2) if r_ == "m" else ev.at("rv_sb", l, hd)))
                if r_ == "m":
                    eng.wait_ge(*ev.at("pads", st["region"]))
            if j >= 4:
                eng.wait_ge(*ev.at(r_ + "kv", l, hd, j - 4))
            elif st["prev_head"] is not None:
                eng.wait_ge(*ev.at("pe_step", st["prev_head"]))
            if r_ == "m":
                col = 24 * d + s_ * 4 + hd
                scaled(mvw[:, j % 4, :], mv[:, t, :], gm[:, 6, col:col + 1]).then_inc(
                    *ev.mark(name, "mvw", l, hd, j))
            else:
                scaled(rvw[:, j % 4, :], rv[:, t, :], small[:, 116 + d:117 + d]).then_inc(
                    *ev.mark(name, "rvw", l, hd, j))

        block = ctx.enter_context(nc.Block())

        def walk(name):
            for i, st in enumerate(PLAN):
                yield i, st
                ev.now[name + "_step", i] = {name: ev.count.get(name, 0)}

        def phase_end(eng, i):
            if PLAN[i]["region"] is None:
                return
            for name in ("pe", "act", "dve", "pool"):
                eng.wait_ge(*ev.at(name + "_step", i - 1))
            for n, k in PLAN[i]["stores"]:
                eng.wait_ge(*ev.at("stored", n, k))

        @block.sync
        def _(sp):
            sp.dma_start(const[:], ins["consts"]).then_inc(*ev.mark("const_in", "const", by=16))
            sp.dma_start(par[:], ins["params"]).then_inc(*ev.mark("par_in", "par", by=16))
            sp.dma_start(cvec[:, 0], ins["cvec"]).then_inc(*ev.mark("cvec_in", "cvec", by=16))
            loaded = 0
            offs = np.cumsum([0] + [s["kt"] * s["cols"] * P for s in STREAM])
            order = {id(s): i for i, s in enumerate(STREAM)}

            def load(i):
                s = STREAM[i]
                if i >= 2:
                    sp.wait_ge(*ev.at("raw_free", STREAM[i - 2]["n"]))
                n = s["kt"] * s["cols"]
                src = ins["stream"][int(offs[i]):int(offs[i]) + n * P].rearrange("(p c) -> p c", p=P)
                sp.dma_start(raw[:, s["n"] % 2, 0:n], src).then_inc(
                    *ev.mark(f"raw{s['n'] % 2}_in", "raw", s["n"], by=16))

            for i, st in enumerate(PLAN):
                kind = st["kind"]
                s = st["slot"]
                if s is not None:
                    while loaded < min(order[id(s)] + (1 if kind == "split" else 3), len(STREAM)):
                        load(loaded)
                        loaded += 1
                if kind == "region":
                    if st["name"] == "attn":
                        phase_end(sp, i)
                        sp.dma_start(ropea[:], ins["rope_a"]).then_inc(*ev.mark("rope_in", "rope", i, by=16))
                    if st["name"] == "ret":
                        phase_end(sp, i)
                        sp.dma_start(roper[:], ins["rope_r"]).then_inc(*ev.mark("rope_in", "rope", i, by=16))
                    if st["name"] in ("norm", "final"):
                        phase_end(sp, i)
                    if st["name"] == "final":
                        sp.dma_start(bias_b[:], ins["final_w"].broadcast_to((P, D))).then_inc(
                            *ev.mark("fnorm_in", "fnorm", by=16))
                if kind == "norms":
                    l, use = st["l"], st["use"]
                    for k, t in enumerate(st["tiles"]):
                        if k >= 3:
                            if use != "last":
                                sp.wait_ge(*ev.at("xs", i, k - 3))
                            if use != "first":
                                sp.wait_ge(*ev.at("stored", i, k - 3))
                        if t not in st["back"]:
                            src = ins["ctx"][0, t * P:(t + 1) * P, :] if t < CT else \
                                ins["x"][0, (t - CT) * P:(t - CT + 1) * P, :]
                        else:
                            sp.wait_ge(*ev.at("stored", *st["back"][t]))
                            src = res[t]
                        sp.dma_start(stage[:, k % 3], src).then_inc(
                            *ev.mark(f"stage{k % 3}_in", "stage", i, k, by=16))

        def akeys(t):
            return ([*range(max(CT, t - 1), min(TILES, t + 2))] if t >= CT else []) + [0, 1]

        @block.tensor
        def _(pe):
            def mm(o, a, b, start=True, stop=True):
                return nc.tensor.matmul(o, a, b, start=start, stop=stop)

            def three(o, wa, ha, kts, w_first, first=0, end=KD):
                last = None
                for k in kts:
                    for j, (a, b) in enumerate(((0, 0), (1, 0), (0, 1))):
                        w, h = wa[a](k), ha[b](k)
                        x, y = (w, h) if w_first else (h, w)
                        last = mm(o, x, y, k == first and j == 0, k == end - 1 and j == 2)
                return last

            def free_bank(n):
                if n >= RING:
                    pe.wait_ge(*ev.at("bank_free", n - RING))

            def part_a(st):
                w = halves(st["slot"])
                for n, ct, (q, t0, size) in banks_a(st):
                    free_bank(n)
                    for t in range(t0 // P, (t0 + size) // P):
                        pe.wait_ge(*ev.at("h", st["gen"], t))
                    wa = [lambda k, x=x: x[:, k, ct * P:(ct + 1) * P] for x in w]
                    ha = [lambda k, x=x: x[:, k, t0:t0 + size] for x in (hh, hl)]
                    three(psg[:, n % RING, 0:size], wa, ha, range(KD), True).then_inc(*ev.mark("pe", "bank", n))

            def part_b(st, c0, cn):
                w = halves(st["slot"])
                piece = st.get("piece")
                for n, tt in banks_b(st):
                    if not piece:
                        free_bank(n)
                    for i, t in enumerate(tt):
                        if piece is not None and i != piece // 2:
                            continue
                        kts = range(KD) if piece is None else range(4 * (piece % 2), 4 * (piece % 2) + 4)
                        pe.wait_ge(*ev.at("h", st["gen"], t))
                        wa = [lambda k, x=x: x[:, k, c0:c0 + cn] for x in w]
                        ha = [lambda k, x=x: x[:, k, t * P:(t + 1) * P] for x in (hh, hl)]
                        last = three(psg[:, n % RING, i * 256:i * 256 + cn], wa, ha, kts, False)
                    last.then_inc(*(ev.mark("pe", "bank", n) if piece in (None, 3) else ev.mark("pe", "piece")))

            pe.wait_ge(*ev.at("const"))
            for i, st in walk("pe"):
                kind, s = st["kind"], st["slot"]
                l, hd, t = st.get("l"), st.get("hd"), st.get("t")
                if kind == "split":
                    continue
                if kind in MIXING:
                    if st["prev"] is not None:
                        pe.wait_ge(*ev.at("act_step", st["prev"]))
                        pe.wait_ge(*ev.at("dve_step", st["prev"]))
                        pe.wait_ge(*ev.at("pool_step", st["prev"]))
                if s is not None:
                    if s["sp"] is not None:
                        pe.wait_ge(*ev.at("rest", s["n"]))
                    else:
                        pe.wait_ge(*ev.at("raw", s["n"]))
                if kind == "vector":
                    pe.wait_ge(*ev.at("silu_c"))
                    piece = st["piece"]
                    if piece == 0:
                        free_bank(st["bank"])
                    w = raw_of(s)
                    bank = psg[:, st["bank"] % RING, :]
                    if piece < 4:
                        for k in (2 * piece, 2 * piece + 1):
                            last = mm(bank[0:2, 0:COLS], cvec[:, 2, k, :], w[:, k, :], k == 0, k == KD - 1)
                        last.then_inc(*ev.mark("pe", "vrow", l, st["n"]))
                    else:
                        pe.wait_ge(*ev.at("vrow_sb", l, st["n"]))
                        for ct in range(2):
                            last = mm(bank[:, 2 * ct:2 * ct + 2], vrow[0:2, ct * P:(ct + 1) * P],
                                      c("ident")[0:2, 0:2])
                        last.then_inc(*ev.mark("pe", "bank", st["bank"]))
                elif kind == "gates":
                    pe.wait_ge(*ev.at("vec", l, 11 + 12 * st["which"]))
                    for n, q, half in gate_banks(st):
                        free_bank(n)
                        for j in range(4):
                            m = (2 + 3 * st["which"]) * KD + 4 * half + j
                            last = mm(psg[:, n % RING, j * P:(j + 1) * P],
                                      vec[:, l, m, q:q + 1].broadcast_to((P, P)), c("ident"))
                        last.then_inc(*ev.mark("pe", "bank", n))
                elif kind == "norms":
                    if st["use"] == "last":
                        continue
                    for k, t in enumerate(st["tiles"]):
                        pe.wait_ge(*ev.at("xs", i, k))
                        if k >= 2:
                            pe.wait_ge(*ev.at("hf", i, k - 2))
                        for half in range(2):
                            for kk in range(4 * half, 4 * half + 4):
                                last = nc.tensor.transpose(psm[:, 2 * (k % 2) + half, (kk % 4) * P:(kk % 4 + 1) * P],
                                                           xs[:, k % 2, kk * P:(kk + 1) * P], c("ident"))
                        last.then_inc(*ev.mark("pe", "xT", i, k))
                elif kind == "turns":
                    pe.wait_ge(*ev.at("pool_step", st["prev_branch"]))
                    pe.wait_ge(*ev.at("dve_step", st["prev_branch"]))
                    for k, t in enumerate(st["tiles"]):
                        if k >= 2:
                            pe.wait_ge(*ev.at("h", st["gen"], st["tiles"][k - 2]))
                        for half in range(2):
                            for kk in range(4 * half, 4 * half + 4):
                                last = nc.tensor.transpose(psm[:, half + 2 * (k % 2), (kk % 4) * P:(kk % 4 + 1) * P],
                                                           acc[:, t, kk * P:(kk + 1) * P], c("ident"))
                            last.then_inc(*ev.mark("pe", "turned", l, t, half))
                elif kind == "mgates":
                    w = halves(st["slot"])
                    for n, _, (q, t0, size) in banks_a(st):
                        free_bank(n)
                        for t in range(t0 // P, (t0 + size) // P):
                            pe.wait_ge(*ev.at("h", st["gen"], t))
                        wa = [lambda k, x=x: x[:, k, :] for x in w]
                        ha = [lambda k, x=x: x[:, k, t0:t0 + size] for x in (hh, hl)]
                        three(psg[0:16, n % RING, 0:size], wa, ha, range(KD), True).then_inc(*ev.mark("pe", "bank", n))
                    pe.wait_ge(*ev.at("grow", l))
                    for t in range(TILES):
                        last = mm(psm[:, 3, 16 * t:16 * t + 16], grow[0:16, t * P:(t + 1) * P], c("ident")[0:16, 0:16])
                    last.then_inc(*ev.mark("pe", "gturned", l))
                elif kind == "mgates2":
                    pe.wait_ge(*ev.at("logf", l))
                    mm(psm[:, 3, 0:24], c("upto"), gm[:, 2, 0:24])
                    mm(psm[:, 3, 24:48], c("since"), gm[:, 2, 24:48])
                    mm(psm[:, 3, 48:96], c("ones"), gm[:, 2, :]).then_inc(*ev.mark("pe", "sums", l))
                    pe.wait_ge(*ev.at("A", l))
                    mm(psm[0:24, 2, 0:P], gm[:, 4, 0:24], c("ident"))
                    mm(psm[0:24, 2, P:2 * P], gm[:, 4, 24:48], c("flip")).then_inc(*ev.mark("pe", "AT", l))
                elif kind == "mgates3":
                    pe.wait_ge(*ev.at("scan", l))
                    mm(psm[:, 1, 0:24], atr[0:24, 2, :], c("ident")[0:24, 0:24])
                    mm(psm[:, 1, 24:48], atr[0:24, 3, :], c("ident")[0:24, 0:24]).then_inc(*ev.mark("pe", "LM", l))
                    pe.wait_ge(*ev.at("LMb", l))
                    mm(psm[:, 1, 48:72], c("flip"), gm[:, 5, 24:48]).then_inc(*ev.mark("pe", "LMf", l))
                elif kind in ("mqk", "rqk", "aq", "up"):
                    part_a(st)
                elif kind == "akv":
                    part_a(st)
                    part_b(st, P, P)
                elif kind == "arot":
                    for ct in range(1 + (st["g"] < 2)):
                        pe.wait_ge(*ev.at("araw", l, st["g"], ct))
                        x = ak[:, CTX:TOK] if st["g"] == 2 else aq[:, 2 * st["g"] + ct, CTX:TOK]
                        mm(psm[:, 2 * st["g"] + ct, 0:SEQ], c("rot"), x).then_inc(
                            *ev.mark("pe", "arot", l, st["g"], ct))
                elif kind in ("mvo", "rv", "rg", "gate", "wout"):
                    part_b(st, 0, COLS)
                elif kind == "branch":
                    w = halves(s)
                    for n, tt in banks_b(st):
                        free_bank(n)
                        for j, t_ in enumerate(tt):
                            pe.wait_ge(*ev.at("ysplit", l, st["br"], t_))
                            wa = [lambda k, x=x: x[:, k, :] for x in w]
                            ya = [lambda k, x=x: x[:, k, t_ * P:(t_ + 1) * P] for x in (yh, yl)]
                            last = three(psg[:, n % RING, j * 256:j * 256 + 256], wa, ya, range(st["kt"]), False,
                                         0, st["kt"])
                        last.then_inc(*ev.mark("pe", "bank", n))
                elif kind == "down":
                    w = halves(s)
                    for j, t_ in enumerate(range(st["first"], TILES)):
                        n = st["bank"] + j
                        free_bank(n)
                        pe.wait_ge(*ev.at("u", l, st["g"] * GROUP + st["kt"] - 1))
                        wa = [lambda k, x=x: x[:, k, :] for x in w]
                        ha = [lambda k, x=x: x[:, (st["g"] * GROUP + k) % URING, t_ * P:(t_ + 1) * P]
                              for x in (uh, ul)]
                        three(psg[:, n % RING, :], wa, ha, range(st["kt"]), False, 0, st["kt"]).then_inc(
                            *ev.mark("pe", "bank", n))
                elif kind in ("mstates", "rstates"):
                    r_ = kind[0]
                    if 0 in st["ticks"]:
                        pe.wait_ge(*ev.at(r_ + "qk", l, hd))
                    for t in range(TILES) if 0 in st["ticks"] else ():
                        a = at_tile(t) if r_ == "m" else t * P
                        src = (mqk if r_ == "m" else rqk)[:, 1, a:a + P]
                        last = nc.tensor.transpose(psm[:, 3 - t // 4, (t % 4) * P:(t % 4 + 1) * P], src, c("ident"))
                    if 0 in st["ticks"]:
                        last.then_inc(*ev.mark("pe", r_ + "ktokT", l, hd))
                        continue
                    pe.wait_ge(*ev.at(r_ + "kt", l, hd))
                    for j in state_turns(st):
                        t = j // 2 if j % 2 == 0 else BACK[j // 2]
                        pe.wait_ge(*ev.at(r_ + "vw", l, hd, j))
                        if j >= 3:
                            pe.wait_ge(*ev.at(r_ + "C", l, hd, j - 3))
                        b = (0, 1, 4)[j % 3]
                        o, k_, v_ = (psm[:, b, 0:P + 1], mktok, mvw[:, j % 4, :]) if r_ == "m" else \
                            (psm[:, b, 0:RV], rktok, rvw[:, j % 4, :])
                        mm(o, k_[:, t, :], v_).then_inc(*ev.mark("pe", r_ + "kv", l, hd, j))

                elif kind == "mtiles":
                    n = len(st["tiles"])
                    for i_ in st["ticks"]:
                        if i_ >= 5:
                            j = i_ - 5
                            if j >= 1:
                                pe.wait_ge(*ev.at("myT_sb", l, hd, j - 1))
                            pe.wait_ge(*ev.at("my", l, hd, j))
                            nc.tensor.transpose(psm[:, 4, 0:P], my[:, j % 2, 2, :], c("ident")).then_inc(
                                *ev.mark("pe", "myT", l, hd, j))
                        if i_ < n:
                            t = st["tiles"][i_]
                            a = at_tile(t)
                            ba = psm[:, i_ % 2]
                            if i_ >= 2:
                                pe.wait_ge(*ev.at("mw", l, hd, i_ - 2))
                            mm(ba[:, 0:P], mqk[:, 1, a:a + P], mqk[:, 0, a:a + P])
                            for d in range(2):
                                s_ = t if d == 0 else BACK.index(t)
                                col = d * 24 + s_ * 4 + hd
                                last = mm(ba[:, (1 + d) * P:(2 + d) * P], gm[:, 9, col:col + 1].broadcast_to((P, P)),
                                          c("ident"))
                            last.then_inc(*ev.mark("pe", "mscore", l, hd, i_))
                        if 2 <= i_ <= n + 1:
                            j = i_ - 2
                            t = st["tiles"][j]
                            a = at_tile(t)
                            if j >= 1:
                                pe.wait_ge(*ev.at("mnd", l, hd, j - 1))
                            mm(psm[:, 2, 0:P + 1], mqk[:, 0, a:a + P], mcf[:, t, :])
                            mm(psm[:, 2, P + 1:2 * (P + 1)], mqk[:, 0, a:a + P], mcb[:, BACK.index(t), :]).then_inc(
                                *ev.mark("pe", "minter", l, hd, j))
                            if j >= 1:
                                pe.wait_ge(*ev.at("mintra_sb", l, hd, j - 1))
                            pe.wait_ge(*ev.at("mw", l, hd, j))
                            mm(psm[:, 3, 0:P + 1], msc[:, j % 2, 2, :], mv[:, t, :])
                            mm(psm[:, 3, P + 1:2 * (P + 1)], msc[:, j % 2, 3, :], mv[:, t, :]).then_inc(
                                *ev.mark("pe", "mintra", l, hd, j))
                elif kind == "attend":
                    n = len(st["heads"])
                    pe.wait_ge(*ev.at("arope", l))
                    for i_ in st["ticks"]:
                        if i_ < n:
                            t, hd = st["heads"][i_]
                            lo = (hd // 4) * AD
                            if i_ >= 1:
                                pe.wait_ge(*ev.at("as", l, i_ - 1))
                            q_ = aq[lo:lo + AD, hd % 4, t * P:(t + 1) * P]
                            if t >= CT:
                                k0, k1 = max(CT, t - 1), min(TILES, t + 2)
                                mm(psm[:, 0, 0:(k1 - k0) * P], q_, ak[lo:lo + AD, k0 * P:k1 * P])
                            mm(psm[:, 1, 0:CTX], q_, ak[lo:lo + AD, 0:CTX]).then_inc(
                                *ev.mark("pe", "ascore", l, i_))
                        if 2 <= i_ <= n + 1:
                            j = i_ - 2
                            t, hd = st["heads"][j]
                            pe.wait_ge(*ev.at("ap", l, j))
                            if j >= 1:
                                pe.wait_ge(*ev.at("apt", l, j - 1))
                            for m in range(len(akeys(t))):
                                o = psm[:, 2, m * P:(m + 1) * P] if m < 4 else psm[:, 3, 0:P]
                                last = nc.tensor.transpose(o, asb[:, j % 4, m * P:(m + 1) * P], c("ident"))
                            last.then_inc(*ev.mark("pe", "apT", l, j))
                        if i_ >= 3:
                            j = i_ - 3
                            t, hd = st["heads"][j]
                            lo = (hd // 4) * AD
                            pe.wait_ge(*ev.at("apt", l, j))
                            if j >= 1:
                                pe.wait_ge(*ev.at("ay", l, j - 1))
                                if hd == 0:
                                    pe.wait_ge(*ev.at("yT", l, "a", st["heads"][j - 1][0]))
                            keys = akeys(t)
                            for m, kt_ in enumerate(keys):
                                last = mm(psm[:, 4, 0:AD], apt[:, j % 2, m * P:(m + 1) * P],
                                          av[:, kt_, lo:lo + AD], m == 0, m == len(keys) - 1)
                            last.then_inc(*ev.mark("pe", "apv", l, j))
                            if hd == AH - 1:
                                pe.wait_ge(*ev.at("ay", l, j))
                                for m in range(4):
                                    last = nc.tensor.transpose(psm[:, 4, m * P:(m + 1) * P],
                                                               ay[:, t % 2, m * P:(m + 1) * P], c("ident"))
                                last.then_inc(*ev.mark("pe", "ayT", l, t))



                elif kind == "rtiles":
                    n = len(st["tiles"])
                    for i_ in st["ticks"]:
                        if i_ < n:
                            t = st["tiles"][i_]
                            if i_ >= 1:
                                pe.wait_ge(*ev.at("rs", l, hd, i_ - 1))
                            mm(psm[:, 0, 0:P], rqk[:, 1, t * P:(t + 1) * P],
                               rqk[:, 0, t * P:(t + 1) * P]).then_inc(*ev.mark("pe", "rscore", l, hd, i_))
                        if 1 <= i_ <= n:
                            j = i_ - 1
                            t = st["tiles"][j]
                            o = psm[:, 2 + j % 3, 0:RV]
                            if j >= 3:
                                pe.wait_ge(*ev.at("rnormed", l, hd, j - 3))
                            pe.wait_ge(*ev.at("rs", l, hd, j))
                            parts = [(rs[:, j % 2, 0, :], rv[:, t, :])]
                            if t > 0:
                                parts.append((rs[:, j % 2, 1, :], rf[:, t - 1, :]))
                            if BACK.index(t) > 0:
                                parts.append((rs[:, j % 2, 2, :], rb[:, BACK.index(t) - 1, :]))
                            pe.wait_ge(*ev.at("rq", l, hd, j))
                            for m, (a, b) in enumerate(parts):
                                last = mm(o, a, b, m == 0, m == len(parts) - 1)
                            last.then_inc(*ev.mark("pe", "rout", l, hd, j))
                        if i_ >= 4:
                            j = i_ - 4
                            if j >= 1:
                                pe.wait_ge(*ev.at("ryT_sb", l, hd, j - 1))
                            pe.wait_ge(*ev.at("ry", l, hd, j))
                            for m in range(2):
                                last = nc.tensor.transpose(psm[:, 1, m * P:(m + 1) * P],
                                                           ry[:, j % 2, 1, m * P:(m + 1) * P], c("ident"))
                            last.then_inc(*ev.mark("pe", "ryT", l, hd, j))
                if s is not None:
                    if kind == "vector" and st["piece"] == 4:
                        continue
                    ev.now[("w_free", s["n"])] = {"pe": ev.count["pe"]}
                    if s["sp"] is not None:
                        ev.now[("w_free_sp", s["sp"])] = {"pe": ev.count["pe"]}
                    if s["sp"] is None:
                        ev.now[("raw_free", s["n"])] = {"pe": ev.count["pe"]}

        @block.scalar
        def _(act):
            act.wait_ge(*ev.at("cvec"))
            nc.scalar.activation(cvec[:, 1], cvec[:, 0], ACT.Tanh, scale=0.5).then_inc(*ev.mark("act", "tanh_c"))
            act.wait_ge(*ev.at("par"))
            act.wait_ge(*ev.at("const"))
            for i, st in walk("act"):
                kind, s = st["kind"], st["slot"]
                l, hd, t = st.get("l"), st.get("hd"), st.get("t")
                if kind == "region":
                    phase_end(act, i)
                if kind == "split":
                    n = s["kt"] * s["cols"]
                    act.wait_ge(*ev.at("raw", s["n"]))
                    if s["sp"] >= 2:
                        act.wait_ge(*ev.at("w_free_sp", s["sp"] - 2))
                    nc.scalar.activation(wh[:, s["sp"] % 2, 0:n], raw[:, s["n"] % 2, 0:n], ACT.Copy).then_inc(*ev.mark("act", "head", s["n"]))
                elif kind == "ysplit":
                    for t in st["tiles"]:
                        ts = slice(t * P, (t + 1) * P)
                        nc.scalar.activation(yh[:, 0:st["kt"], ts], yT[:, 0:st["kt"], ts], ACT.Copy).then_inc(
                            *ev.mark("act", "yh", l, st["br"], t))
                elif kind == "norms":
                    use, n = st["use"], len(st["tiles"])
                    for k in range(n + 2):
                        cc = 4 * (k % 2)
                        if k < n:
                            act.wait_ge(*(ev.at("stage", i, k) if use == "first" else ev.at("rsum", i, k)))
                            if k >= 2 and use != "last":
                                act.wait_ge(*ev.at("xT", i, k - 2))
                            nc.scalar.activation(xs[:, k % 2], stage[:, k % 3], ACT.Square,
                                                 accum_out=small[:, cc:cc + 1]).then_inc(*ev.mark("act", "ss", i, k))
                            if use in ("mid", "end"):
                                act.dma_start(res[st["tiles"][k]], stage[:, k % 3]).then_inc(
                                    *ev.mark(f"store{k % 3}", "stored", i, k, by=16))
                        if 1 <= k <= n and use == "last":
                            act.wait_ge(*ev.at("outrow", i, k - 1))
                            t = st["tiles"][k - 1]
                            act.dma_start(out[0, (t - CT) * P:(t - CT + 1) * P, :], stage[:, (k - 1) % 3]).then_inc(
                                *ev.mark(f"out{(k - 1) % 3}", "stored", i, k - 1, by=16))
                        if k >= 2 and use != "last":
                            if k == 2 and st["h_slot"] is not None:
                                act.wait_ge(*ev.at("w_free", st["h_slot"]))
                            t = st["tiles"][k - 2]
                            act.wait_ge(*ev.at("hf", i, k - 2))
                            nc.scalar.activation(hh[:, :, t * P:(t + 1) * P], hf[:, k % 2], ACT.Copy).then_inc(
                                *ev.mark("act", "hh", i, k - 2))
                        if k < n and use != "last":
                            act.wait_ge(*ev.at("rstd", i, k))
                            act.wait_ge(*ev.at("ss", i, k))
                            nc.scalar.activation(xs[:, k % 2], stage[:, k % 3], ACT.Copy,
                                                 scale=small[:, cc + 2:cc + 3]).then_inc(*ev.mark("act", "xs", i, k))
                elif kind == "turns":
                    act.wait_ge(*ev.at("w_free", st["h_slot"]))
                    for k, t in enumerate(st["tiles"]):
                        for half in range(2):
                            act.wait_ge(*ev.at("turned", l, t, half))
                            nc.scalar.activation(
                                hh[:, half * 4:half * 4 + 4, t * P:(t + 1) * P],
                                psm[:, half + 2 * (k % 2), :].rearrange("p (k c) -> p k c", k=4),
                                ACT.Copy).then_inc(*ev.mark("act", "turn_hh", l, t, half))
                elif kind == "mgates":
                    act.wait_ge(*ev.at("Fx", l))
                    nc.scalar.activation(gm[:, 1, :], gm[:, 0, :], ACT.Abs).then_inc(*ev.mark("act", "absf", l))
                    act.wait_ge(*ev.last("act"))
                    nc.scalar.activation(gm[:, 3, :], gm[:, 1, :], ACT.Exp, scale=-1.0).then_inc(*ev.mark("act", "expf", l))
                    act.wait_ge(*ev.last("act"))
                    nc.scalar.activation(gm[:, 1, :], gm[:, 3, :], ACT.Ln, bias=c("one")).then_inc(*ev.mark("act", "lnf", l))
                elif kind == "mgates3":
                    act.wait_ge(*ev.at("mlogs", l))
                    nc.scalar.activation(gm[:, 6:9, :], gm[:, 6:9, :], ACT.Exp).then_inc(*ev.mark("act", "mexp1", l))
                    nc.scalar.activation(gm[:, 10, :], gm[:, 10, :], ACT.Exp).then_inc(*ev.mark("act", "mexp", l))
                elif kind == "mqk":
                    if hd:
                        act.wait_ge(*ev.at("mt", l, hd - 1))
                    for n, ct, (q, t0, size) in banks_a(st):
                        act.wait_ge(*ev.at("bank", n))
                        a = at_tile(t0 // P)
                        nc.scalar.activation(ma[:, ct, a:a + size], psg[:, n % RING, 0:size], ACT.Copy).then_inc(*ev.mark("act", "bank_free", n))
                        ev.now[("ma", l, hd, ct)] = {"act": ev.count["act"]}
                    for ct in range(2):
                        r0 = 1 if (st["ctx"] or ct == 1) else at_tile(CT)
                        act.wait_ge(*ev.at("conv", l, hd, ct))
                        nc.scalar.activation(mt[:, ct, r0:PADDED - 1], mc[:, ct, r0:PADDED - 1], ACT.Tanh, scale=0.5).then_inc(*ev.mark("act", "mt_", l, hd, ct))
                elif kind == "mvo":
                    for n, tt in banks_b(st):
                        act.wait_ge(*ev.at("bank", n))
                        if st["prev_head"] is not None:
                            act.wait_ge(*ev.at("pe_step", st["prev_head"]))
                            act.wait_ge(*ev.at("dve_step", st["prev_head"]))
                            act.wait_ge(*ev.at("pool_step", st["prev_head"]))
                        ps = psg[:, n % RING, :].rearrange("p (j c) -> p j c", j=2)
                        nc.scalar.activation(mv[:, tt[0]:tt[0] + 2, 0:P], ps[:, :, 0:P], ACT.Copy).then_inc(*ev.mark("act", "mv", l, hd, tt[0] // 2))
                        nc.scalar.activation(mo[:, tt[0]:tt[0] + 2, :], ps[:, :, P:2 * P], ACT.Tanh, scale=0.5).then_inc(*ev.mark("act", "bank_free", n))
                        ev.now[("mo", l, hd)] = {"act": ev.count["act"]}
                elif kind in ("mstates", "rstates"):
                    r_ = kind[0]
                    for j in state_turns(st):
                        if j % 2 == 1:
                            weigh_values(act, "act", lambda o_, x_, w_: nc.scalar.activation(
                                o_, x_, ACT.Copy, scale=w_), st, j)
                    if 0 not in st["ticks"]:
                        continue
                    dst = mktok if r_ == "m" else rktok
                    act.wait_ge(*ev.at(r_ + "ktokT", l, hd))
                    if st["prev_head"] is not None:
                        act.wait_ge(*ev.at("pe_step", st["prev_head"]))
                    nc.scalar.activation(dst[:, 0:4, :], psm[:, 3, :].rearrange("p (k c) -> p k c", k=4),
                                         ACT.Copy).then_inc(*ev.mark("act", "kt_", l))
                    nc.scalar.activation(dst[:, 4:6, :], psm[:, 2, 0:2 * P].rearrange("p (k c) -> p k c", k=2),
                                         ACT.Copy).then_inc(*ev.mark("act", r_ + "kt", l, hd))
                elif kind == "mtiles":
                    n = len(st["tiles"])
                    for i_ in st["ticks"]:
                        if 2 <= i_ <= n + 1:
                            j = i_ - 2
                            if j >= 2:
                                act.wait_ge(*ev.at("mnd", l, hd, j - 2))
                            act.wait_ge(*ev.at("mintra", l, hd, j))
                            nc.scalar.activation(
                                mnd[:, j % 2, 0:2, :], psm[:, 3, 0:2 * (P + 1)].rearrange("p (d c) -> p d c", d=2),
                                ACT.Copy).then_inc(*ev.mark("act", "mintra_sb", l, hd, j))
                        if i_ < n:
                            act.wait_ge(*ev.at("marg", l, hd, i_))
                            nc.scalar.activation(msc[:, i_ % 2, 0:2, :], msc[:, i_ % 2, 0:2, :], ACT.Exp).then_inc(
                                *ev.mark("act", "mexpw", l, hd, i_))
                        if i_ >= 5:
                            j = i_ - 5
                            t = st["tiles"][j]
                            act.wait_ge(*ev.at("myT", l, hd, j))
                            nc.scalar.activation(yT[:, hd, t * P:(t + 1) * P], psm[:, 4, 0:P], ACT.Copy,
                                                 scale=pr(l, "m_norm", hd)).then_inc(
                                *ev.mark("act", "yT", l, "m", t))
                            ev.now["myT_sb", l, hd, j] = {"act": ev.count["act"]}
                elif kind == "gate" and st.get("piece", 3) == 3:
                    for n, tt in banks_b(st):
                        act.wait_ge(*ev.at("bank", n))
                        if st["prev_branch"] is not None:
                            act.wait_ge(*ev.at("dve_step", st["prev_branch"]))
                        ps = psg[:, n % RING, :].rearrange("p (j c) -> p j c", j=2)
                        nc.scalar.activation(gate_place(st, tt[0]), ps, ACT.Tanh, scale=0.5).then_inc(*ev.mark("act", "bank_free", n))
                        ev.now[("tg", l, st["br"], st["n"], tt[0])] = {"act": ev.count["act"]}
                elif kind in ("aq", "akv"):
                    for n, ct, (q, t0, size) in banks_a(st):
                        act.wait_ge(*ev.at("bank", n))
                        dst = ak[:, t0:t0 + size] if kind == "akv" else aq[:, 2 * st["g"] + ct, t0:t0 + size]
                        nc.scalar.activation(dst, psg[:, n % RING, 0:size], ACT.Copy).then_inc(*ev.mark("act", "bank_free", n))
                        ev.now[("araw", l, st.get("g", 2), ct)] = {"act": ev.count["act"]}
                    if kind == "akv":
                        for n, tt in banks_b(st):
                            act.wait_ge(*ev.at("bank", n))
                            ps = psg[:, n % RING, :].rearrange("p (j c) -> p j c", j=2)
                            nc.scalar.activation(av[:, tt[0]:tt[0] + 2, :], ps[:, :, 0:P], ACT.Copy).then_inc(*ev.mark("act", "bank_free", n))
                            ev.now[("av", l)] = {"act": ev.count["act"]}
                elif kind == "attend":
                    n = len(st["heads"])
                    for i_ in st["ticks"]:
                        if 2 <= i_ <= n + 1:
                            j = i_ - 2
                            nk = len(akeys(st["heads"][j][0])) * P
                            n1 = min(nk, 512)
                            act.wait_ge(*ev.at("apT", l, j))
                            if j >= 2:
                                act.wait_ge(*ev.at("apv", l, j - 2))
                            nc.scalar.activation(apt[:, j % 2, 0:n1], psm[:, 2, 0:n1], ACT.Copy).then_inc(
                                *ev.mark("act", "apt", l, j))
                            if nk > 512:
                                nc.scalar.activation(apt[:, j % 2, 512:640], psm[:, 3, 0:P], ACT.Copy).then_inc(
                                    *ev.mark("act", "apt", l, j))
                        if i_ < n:
                            t, hd = st["heads"][i_]
                            nk = len(akeys(t)) * P
                            s0 = 64 + 8 * (i_ % 4)
                            act.wait_ge(*ev.at("anm", l, i_))
                            nc.scalar.activation(asb[:, i_ % 4, 0:nk], asb[:, i_ % 4, 0:nk], ACT.Exp,
                                                 bias=small[:, s0 + 1:s0 + 2],
                                                 accum_out=small[:, s0 + 2:s0 + 3]).then_inc(
                                *ev.mark("act", "ap_", l, i_))
                            nc.scalar.activation(small[:, s0 + 3:s0 + 4], pr(l, "sink", hd), ACT.Exp,
                                                 bias=small[:, s0 + 1:s0 + 2]).then_inc(*ev.mark("act", "ap", l, i_))
                        if i_ >= 3 and st["heads"][i_ - 3][1] == AH - 1:
                            t = st["heads"][i_ - 3][0]
                            act.wait_ge(*ev.at("ayT", l, t))
                            nc.scalar.activation(yT[:, 0:4, t * P:(t + 1) * P],
                                                 psm[:, 4, :].rearrange("p (k c) -> p k c", k=4),
                                                 ACT.Copy).then_inc(*ev.mark("act", "yT", l, "a", t))

                elif kind == "rqk":
                    if hd == 0:
                        x = small[:, 104:112]
                        nc.scalar.activation(x, pr(l, "ret", 0, 8), ACT.Abs).then_inc(*ev.mark("act", "r", l))
                        act.wait_ge(*ev.last("act"))
                        nc.scalar.activation(x, x, ACT.Exp, scale=-1.0).then_inc(*ev.mark("act", "r", l))
                        act.wait_ge(*ev.last("act"))
                        nc.scalar.activation(x, x, ACT.Ln, bias=c("one")).then_inc(*ev.mark("act", "rabs", l))
                    for ct in (0, 1):
                        for n, ct_, (q, t0, size) in banks_a(st):
                            if ct_ != ct:
                                continue
                            act.wait_ge(*ev.at("bank", n))
                            if ct or hd:
                                act.wait_ge(*ev.at("rtmp_done", l, hd if ct else hd - 1, 1 - ct))
                            if st["prev_head"] is not None:
                                act.wait_ge(*ev.at("pe_step", st["prev_head"]))
                                act.wait_ge(*ev.at("dve_step", st["prev_head"]))
                            nc.scalar.activation(rtmp[0:64, t0:t0 + size], psg[64:128, n % RING, 0:size], ACT.Copy).then_inc(*ev.mark("act", "rsw", l, hd, ct, q))
                            nc.scalar.activation(rtmp[64:128, t0:t0 + size], psg[0:64, n % RING, 0:size], ACT.Copy).then_inc(*ev.mark("act", "rsw", l, hd, ct, q))
                    act.wait_ge(*ev.at("logg", l))
                    if st["prev_head"] is not None:
                        act.wait_ge(*ev.at("dve_step", st["prev_head"]))
                        act.wait_ge(*ev.at("pool_step", st["prev_head"]))
                    for d in range(2):
                        g = small[:, 96 + d * 4 + hd:97 + d * 4 + hd]
                        nc.scalar.activation(rd[:, d, :], c("ahead" if d == 0 else "behind"), ACT.Exp, scale=g).then_inc(*ev.mark("act", "rdec", l, hd))
                    act.wait_ge(*ev.at("rdecD", l, hd))
                    for d in range(2):
                        g = small[:, 96 + d * 4 + hd:97 + d * 4 + hd]
                        nc.scalar.activation(rd[:, 1 + d, :], c("row_f" if d == 0 else "row_b"), ACT.Exp, scale=g).then_inc(*ev.mark("act", "rrow", l, hd))
                        nc.scalar.activation(small[:, 112 + d:113 + d], c("col_f" if d == 0 else "col_b"), ACT.Exp, scale=g).then_inc(*ev.mark("act", "rcol", l, hd))
                        nc.scalar.activation(small[:, 114 + d:115 + d], c("cd"), ACT.Exp, scale=g).then_inc(*ev.mark("act", "rcd", l, hd))
                elif kind == "rv":
                    for n, tt in banks_b(st):
                        act.wait_ge(*ev.at("bank", n))
                        if st["prev_head"] is not None:
                            act.wait_ge(*ev.at("pe_step", st["prev_head"]))
                            act.wait_ge(*ev.at("pool_step", st["prev_head"]))
                        ps = psg[:, n % RING, :].rearrange("p (j c) -> p j c", j=2)
                        nc.scalar.activation(rv[:, tt[0]:tt[0] + 2, :], ps, ACT.Copy).then_inc(*ev.mark("act", "bank_free", n))
                        ev.now[("rv_sb", l, hd)] = {"act": ev.count["act"]}
                elif kind == "rg":
                    for n, tt in banks_b(st):
                        act.wait_ge(*ev.at("bank", n))
                        if st["prev_head"] is not None:
                            act.wait_ge(*ev.at("dve_step", st["prev_head"]))
                        ps = psg[:, n % RING, :].rearrange("p (j c) -> p j c", j=2)
                        nc.scalar.activation(rg[:, tt[0]:tt[0] + 2, :], ps, ACT.Tanh, scale=0.5).then_inc(*ev.mark("act", "rgt", l, hd, tt[0]))
                elif kind == "rtiles":
                    n = len(st["tiles"])
                    for j in [i_ - 4 for i_ in st["ticks"] if i_ >= 4]:
                        t = st["tiles"][j]
                        act.wait_ge(*ev.at("ryT", l, hd, j))
                        for m in range(2):
                            nc.scalar.activation(yT[:, 2 * hd + m, t * P:(t + 1) * P],
                                                 psm[:, 1, m * P:(m + 1) * P], ACT.Copy,
                                                 scale=pr(l, "r_norm", 2 * hd + m)).then_inc(
                                *ev.mark("act", "yT", l, "r", t))
                        ev.now["ryT_sb", l, hd, j] = {"act": ev.count["act"]}
                elif kind == "up":
                    u, b = st["u"], st["u"] % 2
                    r0 = 1 if st["ctx"] else at_tile(CT)
                    if u >= 2:
                        act.wait_ge(*ev.at("fa_free", l, u - 2))
                    for n, ct, (q, t0, size) in banks_a(st):
                        act.wait_ge(*ev.at("bank", n))
                        if ct == 0:
                            a = at_tile(t0 // P)
                            nc.scalar.activation(fa[:, b, a:a + size], psg[:, n % RING, 0:size], ACT.Copy).then_inc(*ev.mark("act", "bank_free", n))
                            ev.now[("fa", l, u)] = {"act": ev.count["act"]}
                        else:
                            if u:
                                act.wait_ge(*ev.at("u_", l, u - 1))
                            nc.scalar.activation(fb[:, t0:t0 + size], psg[:, n % RING, 0:size], ACT.Copy, scale=0.5).then_inc(*ev.mark("act", "bank_free", n))
                            ev.now[("fb", l, u)] = {"act": ev.count["act"]}
                    act.wait_ge(*ev.at("fc", l, u))
                    if u:
                        act.wait_ge(*ev.at("u_", l, u - 1))
                    for q, t0, size in seqs[st["ctx"]]:
                        a = at_tile(t0 // P)
                        nc.scalar.activation(ft[:, t0:t0 + size], fc[:, a:a + size], ACT.Tanh, scale=0.5).then_inc(*ev.mark("act", "ft", l, u))
                    act.wait_ge(*ev.at("u_", l, u))
                    if st["ring_free"] is not None:
                        act.wait_ge(*ev.at("w_free", st["ring_free"]))
                    t0 = 0 if st["ctx"] else CTX
                    nc.scalar.activation(uh[:, u % URING, t0:TOK], fu[:, t0:TOK], ACT.Copy).then_inc(*ev.mark("act", "uh", l, u))
            for k in ("store0", "store1", "store2", "out0", "out1", "out2"):
                if ev.count.get(k, 0):
                    act.wait_ge(semaphore(k), ev.count[k])

        def head_norm(dve, x, cc, *key):
            dve.bn_stats(small[:, cc:cc + 6], x).then_inc(*ev.mark("dve", "hn"))
            dve.wait_ge(*ev.last("dve"))
            dve.bn_aggr(small[:, cc + 8:cc + 10], small[:, cc:cc + 6]).then_inc(*ev.mark("dve", "hn"))
            dve.wait_ge(*ev.last("dve"))
            dve.tensor_scalar(small[:, cc + 10:cc + 11], small[:, cc + 9:cc + 10], EPS, None, ALU.add).then_inc(
                *ev.mark("dve", *key))

        @block.vector
        def _(dve):
            V = nc.vector

            dve.wait_ge(*ev.at("cvec"))
            dve.wait_ge(*ev.at("const"))
            dve.wait_ge(*ev.at("par"))
            dve.wait_ge(*ev.at("tanh_c"))
            V.scalar_tensor_tensor(out=cvec[:, 1], in0=cvec[:, 1], scalar=1.0, in1=cvec[:, 0], op0=ALU.add,
                                      op1=ALU.mult).then_inc(*ev.mark("dve", "c1"))
            dve.wait_ge(*ev.last("dve"))
            V.tensor_scalar(cvec[:, 2], cvec[:, 1], 0.5, None, ALU.mult).then_inc(*ev.mark("dve", "silu_c"))
            for i, st in walk("dve"):
                kind, s = st["kind"], st["slot"]
                l, hd, t = st.get("l"), st.get("hd"), st.get("t")
                if kind == "region":
                    phase_end(dve, i)
                    if st["name"] == "mlstm":
                        for b in range(2):
                            for z in (0, at_tile(CT) - 2, at_tile(CT) - 1, PADDED - 1):
                                V.memset(ma[:, b, z:z + 1], 0.0).then_inc(*ev.mark("dve", "pads", i))
                        V.memset(mv[:, :, P:P + 1], 1.0).then_inc(*ev.mark("dve", "pads", i))
                if kind == "vector" and st["piece"] == 3:
                    dve.wait_ge(*ev.at("vrow", l, st["n"]))
                    V.tensor_copy(vrow[0:2, :], psg[0:2, st["bank"] % RING, 0:COLS]).then_inc(
                        *ev.mark("dve", "vrow_sb", l, st["n"]))
                if kind == "vector" and st["piece"] == 4:
                    n = st["bank"]
                    dve.wait_ge(*ev.at("bank", n))
                    m = st["n"] * 2
                    V.tensor_tensor(vec[:, l, m:m + 2, :], psg[:, n % RING, 0:4].rearrange("p (a b) -> p a b", a=2),
                                    pr(l, "mod_b", m, 2).rearrange("p (a b) -> p a b", b=1).broadcast_to((P, 2, 2)),
                                    ALU.add).then_inc(*ev.mark("dve", "bank_free", n))
                    ev.now[("vec", l, st["n"])] = {"dve": ev.count["dve"]}
                elif kind == "affine":
                    w = st["which"]
                    dve.wait_ge(*ev.last("dve"))
                    nw = pr(l, "norm1" if w == 0 else "norm2", 0, 8)
                    nwb = nw.rearrange("p (a b) -> p a b", b=1).broadcast_to((P, KD, 2))
                    V.scalar_tensor_tensor(out=aff[:, w, 0], in0=vec[:, l, (3 * w + 1) * KD:(3 * w + 2) * KD, :],
                                              scalar=1.0, in1=nwb, op0=ALU.add, op1=ALU.mult).then_inc(*ev.mark("dve", "affine", l, w))
                    V.tensor_copy(aff[:, w, 1], vec[:, l, 3 * w * KD:(3 * w + 1) * KD, :]).then_inc(*ev.mark("dve", "affine", l, w))
                elif kind == "gates":
                    dve.wait_ge(*ev.last("dve"))
                    for n, q, half in gate_banks(st):
                        dve.wait_ge(*ev.at("bank", n))
                        V.tensor_scalar(gate_b[:, q, half * 512:half * 512 + 512], psg[:, n % RING, :],
                                        1.0 if st["which"] else 0.5, None, ALU.mult).then_inc(
                            *ev.mark("dve", "bank_free", n))
                elif kind == "norms":
                    use, n = st["use"], len(st["tiles"])
                    w = 0 if use in ("first", "end") else 1
                    dve.wait_ge(*ev.last("dve"))
                    for k in range(n + 1):
                        cc = 4 * (k % 2)
                        if k < n:
                            t = st["tiles"][k]
                            sg = stage[:, k % 3]
                            dve.wait_ge(*ev.at("stage", i, k))
                            if use != "first":
                                V.tensor_tensor(sg, sg, acc[:, t, :], ALU.add).then_inc(*ev.mark("dve", "rsum", i, k))
                        if k >= 1 and use == "last":
                            sg = stage[:, (k - 1) % 3]
                            dve.wait_ge(*ev.at("rstd", i, k - 1))
                            dve.wait_ge(*ev.at("fnorm"))
                            V.scalar_tensor_tensor(out=sg, in0=sg, scalar=small[:, 4 - cc + 2:4 - cc + 3],
                                                   in1=bias_b[:], op0=ALU.mult, op1=ALU.mult).then_inc(
                                *ev.mark("dve", "outrow", i, k - 1))
                        if k >= 1 and use != "last":
                            q = int(st["tiles"][k - 1] >= CT)
                            j = k - 1
                            dve.wait_ge(*ev.at("xT", i, j))
                            if j >= 2:
                                dve.wait_ge(*ev.at("h", st["gen"], st["tiles"][j - 2]))
                            for kk in range(KD):
                                last = V.tensor_scalar(
                                    hf[:, j % 2, kk, :], psm[:, 2 * (j % 2) + kk // 4, (kk % 4) * P:(kk % 4 + 1) * P],
                                    aff[:, w, 0, kk, q:q + 1], aff[:, w, 1, kk, q:q + 1], ALU.mult, ALU.add)
                            last.then_inc(*ev.mark("dve", "hf", i, j))
                elif kind == "turns":
                    for k, t in enumerate(st["tiles"]):
                        ts = slice(t * P, (t + 1) * P)
                        for half in range(2):
                            dve.wait_ge(*ev.at("turn_hh", l, t, half))
                            ks = slice(half * 4, half * 4 + 4)
                            V.tensor_tensor(hl[:, ks, ts],
                                            psm[:, half + 2 * (k % 2), :].rearrange("p (k c) -> p k c", k=4),
                                            hh[:, ks, ts].bitcast(F32), ALU.subtract).then_inc(
                                *ev.mark("dve", "h", st["gen"], t))
                elif kind == "wout":
                    for n, tt in banks_b(st):
                        dve.wait_ge(*ev.at("bank", n))
                        dve.wait_ge(*ev.at("h", st["gen"], TILES - 1))
                        cs = slice(st["n"] * COLS, (st["n"] + 1) * COLS)
                        ps = psg[:, n % RING, :].rearrange("p (j c) -> p j c", j=2)
                        g_ = gate_b[:, int(tt[0] >= CT), cs].rearrange("p (j c) -> p j c", j=1).broadcast_to((P, 2, COLS))
                        V.tensor_tensor(acc[:, tt[0]:tt[0] + 2, cs], ps, g_, ALU.mult).then_inc(
                            *ev.mark("dve", "bank_free", n))
                elif kind == "down":
                    for j, t_ in enumerate(range(st["first"], TILES)):
                        n = st["bank"] + j
                        dve.wait_ge(*ev.at("bank", n))
                        cs = slice(st["half"] * 512, st["half"] * 512 + 512)
                        if st["g"] == 0:
                            V.tensor_copy(acc[:, t_, cs], psg[:, n % RING, :]).then_inc(*ev.mark("dve", "bank_free", n))
                        else:
                            V.tensor_tensor(acc[:, t_, cs], acc[:, t_, cs], psg[:, n % RING, :], ALU.add).then_inc(
                                *ev.mark("dve", "bank_free", n))
                        if (st["g"] + 1) * GROUP >= FT:
                            dve.wait_ge(*ev.last("dve"))
                            V.tensor_tensor(acc[:, t_, cs], acc[:, t_, cs], gate_b[:, int(t_ >= CT), cs],
                                            ALU.mult).then_inc(*ev.mark("dve", "gated_sum"))
                elif kind == "up":
                    u, b = st["u"], st["u"] % 2
                    if u == 0:
                        for b_ in range(2):
                            for z in (0, at_tile(CT) - 2, at_tile(CT) - 1, PADDED - 1):
                                V.memset(fa[:, b_, z:z + 1], 0.0).then_inc(*ev.mark("dve", "fpads", l))
                    r0 = 1 if st["ctx"] else at_tile(CT)
                    r1 = PADDED - 1
                    dve.wait_ge(*ev.at("fa", l, u))
                    dve.wait_ge(*ev.last("dve"))
                    w = [pr(l, "f_conv", j * FT + u) for j in range(3)]
                    if u:
                        dve.wait_ge(*ev.at("ft", l, u - 1))
                    V.tensor_scalar(fc[:, r0:r1], fa[:, b, r0 - 1:r1 - 1], w[0], pr(l, "f_bias", u), ALU.mult,
                                       ALU.add).then_inc(*ev.mark("dve", "fc0"))
                    for j in (1, 2):
                        dve.wait_ge(*ev.last("dve"))
                        V.scalar_tensor_tensor(out=fc[:, r0:r1], in0=fa[:, b, r0 - 1 + j:r1 - 1 + j],
                                                  scalar=w[j], in1=fc[:, r0:r1], op0=ALU.mult, op1=ALU.add).then_inc(*ev.mark("dve", "fc", l, u))
                    ev.now[("fa_free", l, u)] = {"dve": ev.count["dve"]}
                    dve.wait_ge(*ev.at("ft", l, u))
                    if u:
                        dve.wait_ge(*ev.at("uh", l, u - 1))
                        dve.wait_ge(*ev.at("u", l, u - 1))
                    for q, t0, size in seqs[st["ctx"]]:
                        a = at_tile(t0 // P)
                        V.scalar_tensor_tensor(out=fu[:, t0:t0 + size], in0=ft[:, t0:t0 + size], scalar=1.0,
                                                  in1=fc[:, a:a + size], op0=ALU.add, op1=ALU.mult).then_inc(*ev.mark("dve", "fp"))
                    dve.wait_ge(*ev.at("fb", l, u))
                    dve.wait_ge(*ev.last("dve"))
                    t0 = 0 if st["ctx"] else CTX
                    V.tensor_tensor(fu[:, t0:], fu[:, t0:], fb[:, t0:], ALU.mult).then_inc(*ev.mark("dve", "u_", l, u))
                elif kind == "mgates":
                    for n, _, (q, t0, size) in banks_a(st):
                        dve.wait_ge(*ev.at("bank", n))
                        V.tensor_copy(grow[0:16, t0:t0 + size], psg[0:16, n % RING, 0:size]).then_inc(
                            *ev.mark("dve", "bank_free", n))
                        ev.now[("grow", l)] = {"dve": ev.count["dve"]}
                    dve.wait_ge(*ev.at("gturned", l))
                    V.tensor_tensor(g16[:], psm[:, 3, 0:16 * TILES].rearrange("p (t g) -> p t g", t=TILES),
                                    pr(l, "gate", 0, 16).rearrange("p (a b) -> p a b", a=1).broadcast_to((P, TILES, 16)),
                                    ALU.add).then_inc(*ev.mark("dve", "g16"))
                    dve.wait_ge(*ev.last("dve"))
                    Fv = gm[:, 0, :].rearrange("p (d s h) -> p d s h", d=2, s=TILES)
                    Iv = gm[:, 11, :].rearrange("p (d s h) -> p d s h", d=2, s=TILES)
                    V.tensor_copy(Iv[:, 0], g16[:, :, 0:4]).then_inc(*ev.mark("dve", "gI"))
                    V.tensor_copy(Fv[:, 0], g16[:, :, 4:8]).then_inc(*ev.mark("dve", "gF"))
                    for s_, t_ in enumerate(BACK):
                        V.tensor_copy(Iv[:, 1, s_], g16[:, t_, 8:12]).then_inc(*ev.mark("dve", "gI"))
                        V.tensor_copy(Fv[:, 1, s_], g16[:, t_, 12:16]).then_inc(*ev.mark("dve", "Fx", l))
                    dve.wait_ge(*ev.at("lnf", l))
                    V.scalar_tensor_tensor(out=gm[:, 2, :], in0=gm[:, 0, :], scalar=0.0, in1=gm[:, 1, :],
                                              op0=ALU.min, op1=ALU.subtract).then_inc(*ev.mark("dve", "logf", l))
                elif kind == "mgates2":
                    dve.wait_ge(*ev.at("sums", l))
                    V.tensor_tensor(gm[:, 4, :], gm[:, 11, :], psm[:, 3, 0:48], ALU.subtract).then_inc(*ev.mark("dve", "A", l))
                    dve.wait_ge(*ev.at("AT", l))
                    V.tensor_copy(atr[0:24, 0:2, :], psm[0:24, 2, 0:2 * P].rearrange("p (a b) -> p a b", a=2)).then_inc(*ev.mark("dve", "atr"))
                    dve.wait_ge(*ev.last("dve"))
                    for d in range(2):
                        V.tensor_tensor_scan(atr[0:24, 2 + d, :], atr[0:24, d, :], atr[0:24, d, :], NEG,
                                                ALU.max, ALU.max).then_inc(*ev.mark("dve", "scan", l))
                elif kind == "mgates3":
                    dve.wait_ge(*ev.at("LM", l))
                    V.tensor_copy(gm[:, 5, :], psm[:, 1, 0:48]).then_inc(*ev.mark("dve", "LMb", l))
                    dve.wait_ge(*ev.at("LMf", l))
                    V.tensor_copy(gm[:, 5, 24:48], psm[:, 1, 48:72]).then_inc(*ev.mark("dve", "LM2"))
                    dve.wait_ge(*ev.at("cmax", l))
                    v = {k: gm[:, k, :].rearrange("p (d s h) -> p d s h", d=2, s=TILES) for k in (0, 1, 3)}
                    g_ = psm[:, 3, 48:96].rearrange("p (d s h) -> p d s h", d=2, s=TILES)
                    V.memset(v[3][:, :, 0, :], 0.0).then_inc(*ev.mark("dve", "ms0"))
                    for s_ in range(TILES):
                        dve.wait_ge(*ev.last("dve"))
                        V.tensor_tensor(v[1][:, :, s_, :], v[3][:, :, s_, :], v[0][:, :, s_, :], ALU.max).then_inc(*ev.mark("dve", "mm"))
                        if s_ < TILES - 1:
                            dve.wait_ge(*ev.last("dve"))
                            V.tensor_tensor(v[3][:, :, s_ + 1, :], v[1][:, :, s_, :], g_[:, :, s_, :], ALU.add).then_inc(*ev.mark("dve", "mm"))
                    dve.wait_ge(*ev.last("dve"))
                    V.tensor_tensor(gm[:, 5, :], gm[:, 3, :], gm[:, 5, :], ALU.max).then_inc(*ev.mark("dve", "M"))
                    dve.wait_ge(*ev.last("dve"))
                    V.tensor_tensor(gm[:, 6, :], gm[:, 4, :], gm[:, 1, :], ALU.subtract).then_inc(*ev.mark("dve", "e"))
                    V.tensor_tensor(gm[:, 7, :], gm[:, 3, :], gm[:, 1, :], ALU.subtract).then_inc(*ev.mark("dve", "e"))
                    V.tensor_tensor(gm[:, 8, :], gm[:, 3, :], gm[:, 5, :], ALU.subtract).then_inc(*ev.mark("dve", "e"))
                    V.tensor_scalar(gm[:, 9, :], gm[:, 5, :], -1.0, None, ALU.mult).then_inc(*ev.mark("dve", "negM", l))
                    dve.wait_ge(*ev.last("dve"))
                    V.tensor_tensor(gm[:, 10, :], gm[:, 9, :], psm[:, 3, 0:48], ALU.subtract).then_inc(*ev.mark("dve", "mlogs", l))
                    dve.wait_ge(*ev.at("mexp", l))
                    V.tensor_scalar(gm[:, 6, :], gm[:, 6, :], M_SCALE, None, ALU.mult).then_inc(*ev.mark("dve", "mcols", l))
                elif kind == "mqk":
                    for ct in range(2):
                        r0 = 1 if (st["ctx"] or ct == 1) else at_tile(CT)
                        r1 = PADDED - 1
                        dve.wait_ge(*ev.at("ma", l, hd, ct))
                        dve.wait_ge(*ev.last("dve"))
                        w = [pr(l, "conv_q" if ct == 0 else "conv_k", j * MH + hd) for j in range(3)]
                        V.tensor_scalar(mc[:, ct, r0:r1], ma[:, ct, r0 - 1:r1 - 1], w[0], None, ALU.mult).then_inc(*ev.mark("dve", "c"))
                        for j in (1, 2):
                            dve.wait_ge(*ev.last("dve"))
                            V.scalar_tensor_tensor(out=mc[:, ct, r0:r1], in0=ma[:, ct, r0 - 1 + j:r1 - 1 + j],
                                                      scalar=w[j], in1=mc[:, ct, r0:r1], op0=ALU.mult,
                                                      op1=ALU.add).then_inc(*ev.mark("dve", "conv", l, hd, ct))
                    for ct in range(2):
                        r0 = 1 if (st["ctx"] or ct == 1) else at_tile(CT)
                        dve.wait_ge(*ev.at("mt_", l, hd, ct))
                        if st["prev_head"] is not None:
                            dve.wait_ge(*ev.at("pe_step", st["prev_head"]))
                        V.scalar_tensor_tensor(out=mqk[:, ct, r0:r1], in0=mt[:, ct, r0:r1], scalar=1.0,
                                                  in1=mc[:, ct, r0:r1], op0=ALU.add, op1=ALU.mult).then_inc(*ev.mark("dve", "mqk", l, hd))
                    ev.now[("mt", l, hd)] = {"dve": ev.count["dve"]}
                elif kind in ("mstates", "rstates"):
                    r_ = kind[0]
                    if 1 in st["ticks"] and st["prev_head"] is not None:
                        dve.wait_ge(*ev.at("pe_step", st["prev_head"]))
                    if r_ == "m" and 1 in st["ticks"]:
                        V.memset(mcf[:, 0, :], 0.0).then_inc(*ev.mark("dve", "z"))
                        V.memset(mcb[:, 0, :], 0.0).then_inc(*ev.mark("dve", "z"))
                    for j in state_turns(st):
                        d, s_ = j % 2, j // 2
                        dve.wait_ge(*ev.at(r_ + "kv", l, hd, j))
                        dve.wait_ge(*ev.last("dve"))
                        if r_ == "m":
                            col = 24 * d + s_ * 4 + hd
                            x = mcb if d else mcf
                            V.scalar_tensor_tensor(out=x[:, s_ + 1, :], in0=x[:, s_, :], scalar=gm[:, 7, col:col + 1],
                                                   in1=psm[:, (0, 1, 4)[j % 3], 0:P + 1], op0=ALU.mult, op1=ALU.add).then_inc(
                                *ev.mark("dve", "mC", l, hd, j))
                            continue
                        x = rb if d else rf
                        if s_ == 0:
                            V.tensor_copy(x[:, 0, :], psm[:, (0, 1, 4)[j % 3], 0:RV]).then_inc(*ev.mark("dve", "rC", l, hd, j))
                        else:
                            V.scalar_tensor_tensor(out=x[:, s_, :], in0=x[:, s_ - 1, :],
                                                   scalar=small[:, 114 + d:115 + d], in1=psm[:, (0, 1, 4)[j % 3], 0:RV],
                                                   op0=ALU.mult, op1=ALU.add).then_inc(*ev.mark("dve", "rC", l, hd, j))
                elif kind == "mtiles":
                    n = len(st["tiles"])
                    for i_ in st["ticks"]:
                        j, k = i_ - 3, i_ - 4
                        tail, end = 0 <= j < n, 0 <= k < n
                        if tail:
                            t = st["tiles"][j]
                            cc = 16 + 24 * (j % 2)
                            cf, cb = t * 4 + hd, 24 + BACK.index(t) * 4 + hd
                            nd, y = mnd[:, j % 2], my[:, j % 2]
                            den, a, b = nd[:, 2:4, P], small[:, cc + 12:cc + 14], small[:, cc + 14:cc + 16]
                            dve.wait_ge(*ev.at("mintra_sb", l, hd, j))
                            dve.wait_ge(*ev.at("minter", l, hd, j))
                            for d, col in ((0, cf), (1, cb)):
                                V.scalar_tensor_tensor(out=nd[:, 2 + d, :], in0=psm[:, 2, d * (P + 1):(d + 1) * (P + 1)],
                                                       scalar=gm[:, 8, col:col + 1], in1=nd[:, d, :],
                                                       op0=ALU.mult, op1=ALU.add).then_inc(
                                    *ev.mark("dve", "mnd", l, hd, j))
                        if 1 <= i_ <= n:
                            m = i_ - 1
                            dve.wait_ge(*ev.at("mexpw", l, hd, m))
                            if m >= 2:
                                dve.wait_ge(*ev.at("mintra", l, hd, m - 2))
                            for d in range(2):
                                V.scalar_tensor_tensor(out=msc[:, m % 2, 2 + d, :], in0=psm[:, m % 2, 0:P],
                                                       scalar=M_SCALE, in1=msc[:, m % 2, d, :], op0=ALU.mult,
                                                       op1=ALU.mult).then_inc(*ev.mark("dve", "mw", l, hd, m))
                        if tail:
                            dve.wait_ge(*ev.at("mnd", l, hd, j))
                            V.scalar_tensor_tensor(out=a, in0=den, scalar=-1.0, in1=den, op0=ALU.mult,
                                                   op1=ALU.max).then_inc(*ev.mark("dve", "mabs", l, hd, j))
                        if end:
                            ce = 16 + 24 * (k % 2)
                            ye = my[:, k % 2]
                            dve.wait_ge(*ev.at("mrstd", l, hd, k))
                            V.tensor_scalar(ye[:, 1, :], ye[:, 1, :], small[:, ce + 8:ce + 9],
                                            small[:, ce + 11:ce + 12], ALU.subtract, ALU.mult).then_inc(
                                *ev.mark("dve", "mnormed", l, hd, k))
                        if tail:
                            dve.wait_ge(*ev.at("mabs", l, hd, j))
                            V.tensor_tensor(a[:, 0:1], a[:, 0:1], gm[:, 10, cf:cf + 1], ALU.max).then_inc(
                                *ev.mark("dve", "mden", l, hd, j))
                            V.tensor_tensor(a[:, 1:2], a[:, 1:2], gm[:, 10, cb:cb + 1], ALU.max).then_inc(
                                *ev.mark("dve", "mden", l, hd, j))
                        if end:
                            dve.wait_ge(*ev.at("mnormed", l, hd, k))
                            dve.wait_ge(*ev.at("mo_gate", l, hd))
                            if k >= 2:
                                dve.wait_ge(*ev.at("myT", l, hd, k - 2))
                            V.tensor_tensor(ye[:, 2, :], ye[:, 1, :], mo[:, st["tiles"][k], :], ALU.mult).then_inc(
                                *ev.mark("dve", "my", l, hd, k))
                        if tail:
                            dve.wait_ge(*ev.at("mden", l, hd, j))
                            V.reciprocal(b, a).then_inc(*ev.mark("dve", "mrec", l, hd, j))
                        if i_ < n:
                            tq = st["tiles"][i_]
                            dve.wait_ge(*ev.at("mscore", l, hd, i_))
                            for d, col in ((0, tq * 4 + hd), (1, 24 + BACK.index(tq) * 4 + hd)):
                                V.scalar_tensor_tensor(out=msc[:, i_ % 2, d, :],
                                                       in0=psm[:, i_ % 2, (1 + d) * P:(2 + d) * P],
                                                       scalar=gm[:, 4, col:col + 1],
                                                       in1=c("hide_f" if d == 0 else "hide_b"), op0=ALU.add,
                                                       op1=ALU.add).then_inc(*ev.mark("dve", "marg", l, hd, i_))
                        if tail:
                            dve.wait_ge(*ev.at("mrec", l, hd, j))
                            V.tensor_scalar(y[:, 0, :], nd[:, 2, 0:P], b[:, 0:1], None, ALU.mult).then_inc(
                                *ev.mark("dve", "d"))
                            dve.wait_ge(*ev.last("dve"))
                            V.scalar_tensor_tensor(out=y[:, 1, :], in0=nd[:, 3, 0:P], scalar=b[:, 1:2], in1=y[:, 0, :],
                                                   op0=ALU.mult, op1=ALU.add).then_inc(*ev.mark("dve", "d"))
                            dve.wait_ge(*ev.last("dve"))
                            head_norm(dve, y[:, 1, :], cc, "mvar", l, hd, j)
                elif kind == "branch":
                    first = st["br"] == "m"
                    cs = slice(st["n"] * COLS, (st["n"] + 1) * COLS)
                    for j, (n, tt) in enumerate(banks_b(st)):
                        dve.wait_ge(*ev.at("bank", n))
                        dve.wait_ge(*ev.at("tg", l, st["br"], st["n"], tt[0]))
                        ps = psg[:, n % RING, :].rearrange("p (j c) -> p j c", j=2)
                        dst = acc[:, tt[0]:tt[0] + 2, cs] if first else \
                            bt[:, n % 2, :].rearrange("p (j c) -> p j c", j=2)
                        if not first:
                            if st["prev_branch"] is not None:
                                dve.wait_ge(*ev.at("pool_step", st["prev_branch"]))
                            if j == 2:
                                dve.wait_ge(*ev.at("summed", n - 2))
                        V.scalar_tensor_tensor(out=dst, in0=gate_place(st, tt[0]), scalar=1.0, in1=ps,
                                                  op0=ALU.add, op1=ALU.mult).then_inc(*ev.mark("dve", "bank_free", n))
                        ev.now[("gated", l, st["br"], st["n"], tt[0])] = {"dve": ev.count["dve"]}
                elif kind == "arot":
                    g = st["g"]
                    for ct in range(1 + (g < 2)):
                        x = ak[:, CTX:TOK] if g == 2 else aq[:, 2 * g + ct, CTX:TOK]
                        dve.wait_ge(*ev.at("arot", l, g, ct))
                        dve.wait_ge(*ev.at("rope", st["region"]))
                        dve.wait_ge(*ev.last("dve"))
                        V.tensor_tensor(atmp[:], psm[:, 2 * g + ct, 0:SEQ], ropea[:, 1, :], ALU.mult).then_inc(*ev.mark("dve", "amix_", l, g, ct))
                        V.tensor_tensor(x, x, ropea[:, 0, :], ALU.mult).then_inc(*ev.mark("dve", "x"))
                        dve.wait_ge(*ev.last("dve"))
                        V.tensor_tensor(x, x, atmp[:], ALU.add).then_inc(*ev.mark("dve", "arope", l))
                elif kind == "attend":
                    n = len(st["heads"])
                    for i_ in st["ticks"]:
                        if i_ < n:
                            t, hd = st["heads"][i_]
                            b, s0 = i_ % 4, 64 + 8 * (i_ % 4)
                            nw = len(akeys(t)) - 2
                            dve.wait_ge(*ev.at("ascore", l, i_))
                            if i_ >= 4:
                                dve.wait_ge(*ev.at("apT", l, i_ - 4))
                            if nw:
                                c0 = (max(CT, t - 1) - (t - 1)) * P
                                V.scalar_tensor_tensor(out=asb[:, b, 0:nw * P], in0=psm[:, 0, 0:nw * P],
                                                       scalar=AD ** -0.5, in1=c("window")[:, c0:c0 + nw * P],
                                                       op0=ALU.mult, op1=ALU.add).then_inc(*ev.mark("dve", "a"))
                            V.tensor_scalar(asb[:, b, nw * P:(nw + 2) * P], psm[:, 1, 0:CTX], AD ** -0.5, None,
                                            ALU.mult).then_inc(*ev.mark("dve", "as", l, i_))
                        if 2 <= i_ <= n + 1:
                            s2 = 64 + 8 * ((i_ - 2) % 4)
                            dve.wait_ge(*ev.at("ap", l, i_ - 2))
                            V.tensor_tensor(small[:, s2 + 4:s2 + 5], small[:, s2 + 2:s2 + 3], small[:, s2 + 3:s2 + 4],
                                            ALU.add).then_inc(*ev.mark("dve", "asum", l, i_ - 2))
                        if i_ < n:
                            dve.wait_ge(*ev.at("as", l, i_))
                            V.tensor_reduce(small[:, s0:s0 + 1], asb[:, b, 0:(nw + 2) * P], AX.X, ALU.max).then_inc(
                                *ev.mark("dve", "amax", l, i_))
                        if 2 <= i_ <= n + 1:
                            dve.wait_ge(*ev.at("asum", l, i_ - 2))
                            V.reciprocal(small[:, s2 + 5:s2 + 6], small[:, s2 + 4:s2 + 5]).then_inc(
                                *ev.mark("dve", "ard", l, i_ - 2))
                        if i_ < n:
                            dve.wait_ge(*ev.at("amax", l, i_))
                            V.tensor_scalar(small[:, s0 + 1:s0 + 2], small[:, s0:s0 + 1], pr(l, "sink", hd), -1.0,
                                            ALU.max, ALU.mult).then_inc(*ev.mark("dve", "anm", l, i_))
                        if i_ >= 3:
                            j = i_ - 3
                            t, hd = st["heads"][j]
                            s0 = 64 + 8 * (j % 4)
                            dve.wait_ge(*ev.at("apv", l, j))
                            dve.wait_ge(*ev.at("ard", l, j))
                            V.tensor_scalar(ay[:, t % 2, hd * AD:(hd + 1) * AD], psm[:, 4, 0:AD],
                                            small[:, s0 + 5:s0 + 6], None, ALU.mult).then_inc(
                                *ev.mark("dve", "ay", l, j))
                elif kind == "rqk":
                    if hd == 0:
                        dve.wait_ge(*ev.last("dve"))
                        x = small[:, 104:112]
                        dve.wait_ge(*ev.at("rabs", l))
                        V.scalar_tensor_tensor(out=small[:, 96:104], in0=pr(l, "ret", 0, 8), scalar=0.0,
                                                  in1=x, op0=ALU.min, op1=ALU.subtract).then_inc(*ev.mark("dve", "logg", l))
                    for ct in (0, 1):
                        for n, ct_, (q, t0, size) in banks_a(st):
                            if ct_ != ct:
                                continue
                            dve.wait_ge(*ev.at("bank", n))
                            dve.wait_ge(*ev.at("rope", st["region"]))
                            if st["prev_head"] is not None:
                                dve.wait_ge(*ev.at("pe_step", st["prev_head"]))
                                dve.wait_ge(*ev.at("pool_step", st["prev_head"]))
                            dve.wait_ge(*ev.at("rsw", l, hd, ct, q))
                            x = rqk[:, ct, t0:t0 + size]
                            V.tensor_tensor(x, psg[:, n % RING, 0:size], roper[:, 0, t0:t0 + size], ALU.mult).then_inc(*ev.mark("dve", "bank_free", n))
                            V.tensor_tensor(rtmp[:, t0:t0 + size], rtmp[:, t0:t0 + size],
                                               roper[:, 1, t0:t0 + size], ALU.mult).then_inc(*ev.mark("dve", "r"))
                            dve.wait_ge(*ev.last("dve"))
                            V.tensor_tensor(x, x, rtmp[:, t0:t0 + size], ALU.add).then_inc(*ev.mark("dve", "rqk", l, hd))
                        ev.now[("rtmp_done", l, hd, ct)] = {"dve": ev.count["dve"]}
                    dve.wait_ge(*ev.at("rdec", l, hd))
                    V.scalar_tensor_tensor(out=rd[:, 0, :], in0=rd[:, 0, :], scalar=R_SCALE, in1=c("upto"),
                                              op0=ALU.mult, op1=ALU.mult).then_inc(*ev.mark("dve", "r"))
                    V.scalar_tensor_tensor(out=rd[:, 1, :], in0=rd[:, 1, :], scalar=R_SCALE, in1=c("since"),
                                              op0=ALU.mult, op1=ALU.mult).then_inc(*ev.mark("dve", "r"))
                    dve.wait_ge(*ev.last("dve"))
                    V.tensor_tensor(rd[:, 0, :], rd[:, 0, :], rd[:, 1, :], ALU.add).then_inc(*ev.mark("dve", "rdecD", l, hd))
                    dve.wait_ge(*ev.at("rcd", l, hd))
                    V.tensor_scalar(small[:, 116:118], small[:, 112:114], R_SCALE, None, ALU.mult).then_inc(*ev.mark("dve", "rw", l, hd))
                elif kind == "rg":
                    for n, tt in banks_b(st):
                        dve.wait_ge(*ev.at("rgt", l, hd, tt[0]))
                        ps = psg[:, n % RING, :].rearrange("p (j c) -> p j c", j=2)
                        x = rg[:, tt[0]:tt[0] + 2, :]
                        V.scalar_tensor_tensor(out=x, in0=x, scalar=1.0, in1=ps, op0=ALU.add, op1=ALU.mult).then_inc(*ev.mark("dve", "bank_free", n))
                        ev.now[("rg_sb", l, hd)] = {"dve": ev.count["dve"]}

                elif kind == "rtiles":
                    n = len(st["tiles"])
                    for i_ in st["ticks"]:
                        if i_ < n:
                            dve.wait_ge(*ev.at("rscore", l, hd, i_))
                            if i_ >= 2:
                                dve.wait_ge(*ev.at("rout", l, hd, i_ - 2))
                            V.tensor_tensor(rs[:, i_ % 2, 0, :], psm[:, 0, 0:P], rd[:, 0, :], ALU.mult).then_inc(
                                *ev.mark("dve", "rs", l, hd, i_))
                        if 2 <= i_ <= n + 1:
                            j = i_ - 2
                            o = psm[:, 2 + j % 3, 0:RV]
                            dve.wait_ge(*ev.at("rout", l, hd, j))
                            head_norm(dve, o, 16 + 24 * (j % 2), "rvar", l, hd, j)
                        if 3 <= i_ <= n + 2:
                            j = i_ - 3
                            t = st["tiles"][j]
                            cc = 16 + 24 * (j % 2)
                            o = psm[:, 2 + j % 3, 0:RV]
                            dve.wait_ge(*ev.at("rrstd", l, hd, j))
                            V.tensor_scalar(ry[:, j % 2, 0, :], o, small[:, cc + 8:cc + 9], small[:, cc + 11:cc + 12],
                                            ALU.subtract, ALU.mult).then_inc(*ev.mark("dve", "rnormed", l, hd, j))
                            dve.wait_ge(*ev.last("dve"))
                            dve.wait_ge(*ev.at("rg_sb", l, hd))
                            if j >= 2:
                                dve.wait_ge(*ev.at("ryT", l, hd, j - 2))
                            V.scalar_tensor_tensor(out=ry[:, j % 2, 1, :], in0=ry[:, j % 2, 0, :], scalar=0.5,
                                                   in1=rg[:, t, :], op0=ALU.mult, op1=ALU.mult).then_inc(
                                *ev.mark("dve", "ry", l, hd, j))
        @block.gpsimd
        def _(pool):
            G = nc.gpsimd

            pool.wait_ge(*ev.at("const"))
            for i, st in walk("pool"):
                kind, s = st["kind"], st["slot"]
                l, hd, t = st.get("l"), st.get("hd"), st.get("t")
                if kind == "region":
                    phase_end(pool, i)
                if kind == "split":
                    n = s["kt"] * s["cols"]
                    pool.wait_ge(*ev.at("head", s["n"]))
                    G.tensor_tensor(wl[:, s["sp"] % 2, 0:n], raw[:, s["n"] % 2, 0:n],
                                       wh[:, s["sp"] % 2, 0:n].bitcast(F32), ALU.subtract).then_inc(*ev.mark("pool", "rest", s["n"]))
                    ev.now[("raw_free", s["n"])] = {"pool": ev.count["pool"]}
                elif kind == "ysplit":
                    for t in st["tiles"]:
                        ts = slice(t * P, (t + 1) * P)
                        pool.wait_ge(*ev.at("yh", l, st["br"], t))
                        G.tensor_tensor(yl[:, 0:st["kt"], ts], yT[:, 0:st["kt"], ts],
                                        yh[:, 0:st["kt"], ts].bitcast(F32), ALU.subtract).then_inc(
                            *ev.mark("pool", "ysplit", l, st["br"], t))
                elif kind == "norms":
                    n = len(st["tiles"])
                    for k in range(n + 2):
                        cc = 4 * (k % 2)
                        if k < n:
                            pool.wait_ge(*ev.at("ss", i, k))
                            G.tensor_scalar(small[:, cc + 1:cc + 2], small[:, cc:cc + 1], 1.0 / D, EPS, ALU.mult,
                                            ALU.add).then_inc(*ev.mark("pool", "ms", i, k))
                            pool.wait_ge(*ev.at("ms", i, k))
                            G.tensor_tensor(small[:, cc + 2:cc + 3], small[:, cc + 1:cc + 2], c("neg_half"),
                                            ALU.pow).then_inc(*ev.mark("pool", "rstd", i, k))
                        if k >= 2 and st["use"] != "last":
                            t = st["tiles"][k - 2]
                            ts = slice(t * P, (t + 1) * P)
                            pool.wait_ge(*ev.at("hh", i, k - 2))
                            G.tensor_tensor(hl[:, :, ts], hf[:, k % 2], hh[:, :, ts].bitcast(F32),
                                            ALU.subtract).then_inc(*ev.mark("pool", "h", st["gen"], t))
                elif kind == "up":
                    u = st["u"]
                    pool.wait_ge(*ev.at("uh", l, u))
                    t0 = 0 if st["ctx"] else CTX
                    G.tensor_tensor(ul[:, u % URING, t0:TOK], fu[:, t0:TOK],
                                       uh[:, u % URING, t0:TOK].bitcast(F32), ALU.subtract).then_inc(*ev.mark("pool", "u", l, u))
                elif kind == "mgates2":
                    pool.wait_ge(*ev.at("A", l))
                    G.partition_all_reduce(gm[:, 0, :], gm[:, 4, :], P, bass.bass_isa.ReduceOp.max).then_inc(*ev.mark("pool", "cmax", l))
                elif kind in ("mstates", "rstates"):
                    r_ = kind[0]
                    for j in state_turns(st):
                        if j % 2 == 0:
                            weigh_values(pool, "pool", lambda o_, x_, w_: G.tensor_scalar(
                                o_, x_, w_, None, ALU.mult), st, j)
                    if r_ == "m" and 3 in st["ticks"]:
                        pool.wait_ge(*ev.at("mo", l, hd))
                        m0 = 0 if st["ctx"] else CT
                        G.tensor_scalar(mo[:, m0:, :], mo[:, m0:, :], 1.0, 0.5, ALU.add, ALU.mult).then_inc(
                            *ev.mark("pool", "mo_gate", l, hd))
                elif kind in ("mtiles", "rtiles"):
                    n = len(st["tiles"])
                    for i_ in st["ticks"]:
                        if i_ < n and kind == "rtiles":
                            t = st["tiles"][i_]
                            pool.wait_ge(*ev.at("rqk", l, hd))
                            pool.wait_ge(*ev.at("rrow", l, hd))
                            if i_ >= 2:
                                pool.wait_ge(*ev.at("rout", l, hd, i_ - 2))
                            for d in range(2):
                                G.tensor_tensor(rs[:, i_ % 2, 1 + d, :], rqk[:, 0, t * P:(t + 1) * P],
                                                rd[:, 1 + d, :], ALU.mult).then_inc(*ev.mark("pool", "rq", l, hd, i_))
                        lag = 3 if kind == "mtiles" else 2
                        if lag <= i_ < n + lag:
                            j = i_ - lag
                            cc = 16 + 24 * (j % 2)
                            pool.wait_ge(*ev.at(kind[0] + "var", l, hd, j))
                            G.tensor_tensor(small[:, cc + 11:cc + 12], small[:, cc + 10:cc + 11], c("neg_half"),
                                            ALU.pow).then_inc(*ev.mark("pool", kind[0] + "rstd", l, hd, j))
                if kind == "branch" and st["br"] != "m":
                    cs = slice(st["n"] * COLS, (st["n"] + 1) * COLS)
                    for n, tt in banks_b(st):
                        pool.wait_ge(*ev.at("gated", l, st["br"], st["n"], tt[0]))
                        x = acc[:, tt[0]:tt[0] + 2, cs]
                        G.tensor_tensor(x, x, bt[:, n % 2, :].rearrange("p (j c) -> p j c", j=2), ALU.add).then_inc(*ev.mark("pool", "summed", n))
        return ev.now


def arena_offset(nc, arena):
    return nc.sbuf_base - ARENA_BYTES


def build(bacc, args, shape, stop=None):
    known = None
    for _ in range(2):
        nc = bacc.Bacc("TRN2", target_bir_lowering=False, num_devices=1)
        ins = {k: nc.dram_tensor(f"in_{k}", v.shape, F32, kind="ExternalInput").ap() for k, v in args.items()}
        out = nc.dram_tensor("out", shape, F32, kind="ExternalOutput").ap()
        known = backbone(nc, ins, out, known, stop)
    return nc


def layout(inputs, stop=None):
    consts, _, rope_a, rope_r = constants()
    PP, NPAR = param_places()
    plan, stream = make_plan()
    if stop is not None:
        used = {id(s["slot"]) for s in plan[:stop] if s["slot"] is not None}
        stream = [s for s in stream if id(s) in used]
    g = {k: np.ascontiguousarray(v) for k, v in inputs.items()}
    flat = np.empty(sum(s["kt"] * s["cols"] * P for s in stream), np.float32)
    off = 0
    for s in stream:
        name, row, cols = s["blocks"]
        w = g[name][s["l"], row:row + s["kt"] * P]
        w = np.concatenate([w[:, a:a + n] for a, n in cols], 1)
        n = w.size
        flat[off:off + n] = w.reshape(s["kt"], P, -1).transpose(1, 0, 2).ravel()
        off += n
    par = np.empty((P, DEPTH, NPAR), np.float32)
    for l in range(DEPTH):
        tap = g["m_conv_w"][l]
        rows = {
            "mod_b": g["mod_b"][l], "norm1": g["norm1_w"][l], "norm2": g["norm2_w"][l],
            "conv_q": tap[:, :MH * P].ravel(), "conv_k": tap[:, MH * P:].ravel(), "m_norm": g["m_norm_w"][l],
            "r_norm": g["ret_norm_w"][l], "f_conv": g["ffn_conv_w"][l].ravel(), "f_bias": g["ffn_conv_b"][l]}
        for k, v in rows.items():
            a, n = PP[k]
            par[:, l, a:a + n] = v.reshape(n, P).T
        for k, v in (("sink", g["a_sink"][l]), ("ret", g["ret_logit"][l].ravel()), ("gate", g["m_gate_bias"][l])):
            a, n = PP[k]
            par[:, l, a:a + n] = v[None, :]
    cvec = np.stack([g["c_ctx"].reshape(KD, P), g["c"][0].reshape(KD, P)], 0).transpose(2, 1, 0)
    return {"stream": flat, "consts": consts, "params": par, "cvec": np.ascontiguousarray(cvec),
            "rope_a": rope_a, "rope_r": rope_r, "mod_b": g["mod_b"], "final_w": g["final_norm_w"][None, :],
            "x": g["x"], "ctx": g["ctx"]}


def kernel(**inputs):
    from concourse.bass_utils import run_bass_kernel_spmd as run
    import concourse.bacc as bacc
    args = layout(inputs)
    nc = build(bacc, args, inputs["x"].shape)
    r = run(nc, [{f"in_{k}": v for k, v in args.items()}], core_ids=[0])
    return r.results[0]["out"]
```

```python
from contextlib import ExitStack
from itertools import chain, islice

import numpy as np
import concourse.bass as bass
from concourse import mybir

F32, F32R = mybir.dt.float32, mybir.dt.float32r
ALU, ACT, AX = mybir.AluOpType, mybir.ActivationFunctionType, mybir.AxisListType

P = 128
D, SEQ, CTX, DEPTH, GRID_W = 1024, 512, 256, 2, 64
KD = D // P
TILES, CT = (SEQ + CTX) // P, CTX // P
TOK = SEQ + CTX
MH, AH, AKV, RH, RV = 4, 8, 2, 4, 256
AD = 64
FFN = 2816
FT = FFN // P
GROUP = 4
RING = 3
URING = 6
ARENA_BYTES = 74 * 1024
EPS = 1e-6
NEG = -1e30
COLS = 256
SLOT = KD * COLS
PADDED = TOK + 4
BACK = [1, 0, 5, 4, 3, 2]
M_SCALE = 0.25 * P ** -0.5
R_SCALE = P ** -0.5
IN_OFF = dict(mq=0, mk=512, mv=1024, mo=1536, mg=2048, aq=2064, ak=2576, av=2704, rq=2832, rk=3344,
              rv=3856, rg=4880, gm=5904, ga=6928, gr=7952)


def at_tile(t):
    return 1 + P * t + (2 if t >= CT else 0)


def constants():
    r, j = np.meshgrid(np.arange(P), np.arange(P), indexing="ij")
    rot = np.zeros((P, P), np.float32)
    for m in range(P):
        if m % 32 < 16:
            rot[m + 16, m] = -1.0
        else:
            rot[m - 16, m] = 1.0
    window = np.concatenate([np.where(j >= r, 0.0, NEG), np.zeros((P, P)), np.where(j <= r, 0.0, NEG)], 1)
    parts = dict(
        ident=np.eye(P), upto=(r <= j), since=(r >= j), ones=np.ones((P, P)),
        hide_f=np.where(r <= j, 0.0, NEG), hide_b=np.where(r >= j, 0.0, NEG), window=window,
        ahead=np.maximum(j - r, 0), behind=np.maximum(r - j, 0), row_f=j + 1, row_b=P - j,
        col_f=127 - r[:, :1], col_b=r[:, :1], rot=rot, flip=np.eye(P)[::-1],
        neg_half=np.full((P, 1), -0.5), one=np.ones((P, 1)), cd=np.full((P, 1), float(P)))
    place, cols = {}, []
    n = 0
    for k, v in parts.items():
        place[k] = (n, n + v.shape[1])
        cols.append(v.astype(np.float32))
        n += v.shape[1]
    f = np.float32
    inv16 = (f(10000.0) ** (-np.arange(16, dtype=f) / f(16))).astype(f)
    t = np.arange(SEQ)
    ang = np.zeros((P, SEQ), f)
    for m in range(P):
        pos = (t // GRID_W) if m % 64 < 32 else (t % GRID_W)
        ang[m] = pos.astype(f) * inv16[m % 16]
    rope_a = np.stack([np.cos(ang), np.sin(ang)], 1).astype(f)
    inv64 = (f(10000.0) ** (-np.arange(64, dtype=f) / f(64))).astype(f)
    ang = np.arange(TOK).astype(f)[None, :] * inv64[np.arange(P) % 64][:, None]
    sign = np.where(np.arange(P) < 64, -1.0, 1.0)[:, None]
    rope_r = np.stack([np.cos(ang), np.sin(ang) * sign], 1).astype(f)
    return np.concatenate(cols, 1), place, rope_a, rope_r


def param_places():
    sizes = [("mod_b", 48), ("norm1", 8), ("norm2", 8), ("conv_q", 12), ("conv_k", 12), ("m_norm", 4),
             ("r_norm", 8), ("f_conv", 3 * FT), ("f_bias", FT), ("sink", AH), ("ret", 2 * RH), ("gate", 16)]
    place, n = {}, 0
    for k, s in sizes:
        place[k] = (n, s)
        n += s
    return place, n


def make_plan():
    plan, stream, bank, split = [], [], [0], [0]

    def slot(l, blocks, kt=KD, splits=True):
        s = dict(n=len(stream), l=l, blocks=blocks, kt=kt, cols=sum(b[1] for b in blocks[2]), sp=None)
        if splits:
            s["sp"] = split[0]
            split[0] += 1
        stream.append(s)
        return s

    def step(kind, slot=None, banks=0, **k):
        if "piece" in k:
            if k["piece"] == 0:
                slot["bank"], banks = bank[0], 1
            k.update(kind=kind, slot=slot, bank=slot["bank"])
        else:
            if not k.get("ctx", True):
                banks = {"mqk": 3, "rqk": 3, "mvo": 3}.get(kind, 2)
            k.update(kind=kind, slot=slot, bank=bank[0])
        bank[0] += banks
        plan.append(k)

    def seqs(ctx):
        return ((0, 0, CTX), (1, CTX, SEQ)) if ctx else ((1, CTX, SEQ),)

    def pairs(ctx):
        return (0, 1, 2) if ctx else (1, 2)

    def cols(name, l, c0, n=COLS, kt=KD, row=0, splits=True):
        return slot(l, (name, row, [(c0, n)]), kt, splits)

    modulation = iter([(l, n) for l in range(DEPTH) for n in range(6 * D // COLS)])

    def vectors(count):
        turn = None
        for l, n in islice(modulation, count):
            s = cols("mod_w", l, n * COLS, splits=False)
            for piece in range(4):
                yield step("vector", s, l=l, n=n, piece=piece)
                if piece == 0 and turn:
                    yield step("vector", **turn)
            turn = dict(slot=s, l=l, n=n, piece=4)
        yield step("vector", **turn)

    def gate(l, which, n, h, ctx):
        c0 = IN_OFF[{"m": "gm", "a": "ga", "r": "gr"}[which]] + n * COLS
        s = cols("w_in", l, c0)
        for pair in pairs(ctx):
            for piece in range(4):
                yield step("gate", s, l=l, gen=h, br=which, n=n, ctx=ctx, pair=pair, piece=piece,
                           open=pair != pairs(ctx)[-1])

    def ticks(kind, count, fill=iter(()), pieces=0, start=0, stop=None, **k):
        before = 0
        for i in range(start, stop or count):
            step(kind, ticks=range(i, i + 1), **k)
            upto = round((i + 1) * pieces / count)
            for _ in islice(fill, upto - before):
                pass
            before = upto

    gen = 0
    step("setup")
    for l in range(DEPTH):
        ctx = l < DEPTH - 1
        tiles = list(range(0 if ctx else CT, TILES))
        if l == 0:
            step("region", name="norm")
            first = dict(count=TILES + 2, l=0, use="first", tiles=list(range(TILES)), gen=gen)
            ticks("norms", stop=1, **first)
            for _ in vectors(2 * D // COLS):
                pass
            step("affine", l=0, which=0)
            ticks("norms", start=1, **first)
        h = gen
        o = IN_OFF

        def aq_slot(g):
            return slot(l, ("w_in", 0, [(o["aq"] + (2 * g + i + 4 * half) * AD, AD)
                                        for i in range(2) for half in range(2)]))

        step("region", name="mlstm")
        step("mgates", slot(l, ("w_in", 0, [(o["mg"], 16)])), 2, l=l, gen=h)
        s = None
        for hd in range(MH):
            s = s or slot(l, ("w_in", 0, [(o["mq"] + hd * P, P), (o["mk"] + hd * P, P)]))
            step("mqk", s, 4, l=l, gen=h, hd=hd, ctx=ctx)
            if hd == 0:
                step("mgates2", l=l)
            step("mvo", slot(l, ("w_in", 0, [(o["mv"] + hd * P, P), (o["mo"] + hd * P, P)])), 3, l=l, gen=h,
                 hd=hd, ctx=ctx)
            if hd == 0:
                step("mgates3", l=l)
            fill = gate(l, "m", hd, h, ctx)
            ticks("mstates", 4, fill, 4, l=l, hd=hd, ctx=True)
            s = slot(l, ("w_in", 0, [(o["mq"] + (hd + 1) * P, P), (o["mk"] + (hd + 1) * P, P)])) \
                if hd + 1 < MH else cols("w_br_m", l, 0, kt=4)
            pieces = 4 * len(pairs(ctx)) + 1
            fill = chain(vectors(1), fill)
            ticks("mtiles", len(tiles) + 5, fill, pieces, l=l, hd=hd, tiles=tiles)
        step("region", name="branch")
        step("ysplit", l=l, br="m", kt=4, tiles=tiles)
        for n in range(4):
            branch(step, cols, l, ctx, "m", n, None if n else s)
        step("region", name="attn")
        step("aq", aq_slot(0), 4, l=l, gen=h, g=0, ctx=ctx)
        step("akv", slot(l, ("w_in", 0, [(o["ak"], P), (o["av"], P)])), 4, l=l, gen=h)
        step("arot", l=l, g=0, first=True)
        step("avturn", None, 2, l=l)
        step("aq", aq_slot(1), 4, l=l, gen=h, g=1, ctx=ctx)
        step("arot", l=l, g=2, first=False)
        step("arot", l=l, g=1, first=False)
        count = AH * len(tiles) + 2
        fill = chain(*[gate(l, "a", n, h, ctx) for n in range(3)])
        ticks("attend", AH * len(tiles) + 3, fill, 12 * len(pairs(ctx)), l=l,
              heads=[(t, hd) for t in tiles for hd in range(AH)])
        step("region", name="branch")
        step("ysplit", l=l, br="a", kt=4, tiles=tiles)
        step("gate", cols("w_in", l, o["ga"] + 3 * COLS), 3, l=l, gen=h, br="a", n=3, ctx=ctx)
        for n in range(4):
            branch(step, cols, l, ctx, "a", n)
        step("region", name="ret")
        s = slot(l, ("w_in", 0, [(o["rq"], P), (o["rk"], P)]))
        for hd in range(RH):
            step("rqk", s, 4, l=l, gen=h, hd=hd, ctx=ctx)
            step("rv", cols("w_in", l, o["rv"] + hd * RV), 3, l=l, gen=h, hd=hd)
            step("rg", cols("w_in", l, o["rg"] + hd * RV), 3, l=l, gen=h, hd=hd, ctx=ctx)
            s = slot(l, ("w_in", 0, [(o["rq"] + (hd + 1) * P, P), (o["rk"] + (hd + 1) * P, P)])) \
                if hd + 1 < RH else cols("w_in", l, o["gr"])
            fill = vectors(3)
            ticks("rstates", 4, fill, 4, l=l, hd=hd)
            ticks("rtiles", len(tiles) + 4, fill, 11, l=l, hd=hd, tiles=tiles)
        step("region", name="branch")
        step("ysplit", l=l, br="r", kt=8, tiles=tiles)
        for n in range(4):
            step("gate", cols("w_in", l, o["gr"] + n * COLS) if n else s, 3, l=l, gen=h, br="r", n=n, ctx=ctx)
            branch(step, cols, l, ctx, "r", n)
        step("region", name="norm")
        first = 0 if ctx else CT
        gen += 1
        step("gates", None, 4, l=l, which=0, ctx=ctx)
        step("turns", l=l, tiles=tiles, gen=gen)
        for n in range(4):
            step("wout", cols("w_out", l, n * COLS), 3, l=l, gen=gen, n=n, ctx=ctx)
        step("affine", l=l, which=1)
        gen += 1
        s = slot(l, ("ffn_up", 0, [(0, P), (FFN, P)]))
        fill = vectors(2 * D // COLS) if ctx else iter(())
        ticks("norms", len(tiles) + 2, fill, 5 * 2 * D // COLS, l=l, use="mid", tiles=tiles, gen=gen)
        step("gates", None, 4, l=l, which=1, ctx=ctx)
        step("region", name="mlp")
        down = 0
        for u in range(FT):
            step("up", slot(l, ("ffn_up", 0, [(u * P, P), (FFN + u * P, P)])) if u else s, 4, l=l, gen=gen,
                 u=u, ctx=ctx)
            if u >= GROUP and u % GROUP == 0 and u + GROUP < FT or u == FT - 1:
                while down * GROUP < FT and (down + 1) * GROUP <= u or (u == FT - 1 and down * GROUP < FT):
                    kt = min(GROUP, FT - down * GROUP)
                    for half in range(2):
                        step("down", slot(l, ("ffn_down", down * GROUP * P, [(half * 512, 512)]), kt),
                             TILES - first, l=l, g=down, half=half, kt=kt, first=first)
                    down += 1
        last = l == DEPTH - 1
        step("region", name="final" if last else "norm")
        if not last:
            step("affine", l=l + 1, which=0)
        gen += 1
        ticks("norms", len(tiles) + 2, l=l, use="last" if last else "end", tiles=tiles, gen=gen)
    splits = [s for s in stream if s["sp"] is not None]
    order, done, used = [], 0, set()
    for st in plan:
        if st["kind"] == "norms" and st["use"] == "first" and 3 in st["ticks"]:
            while done < 2:
                order.append(dict(kind="split", slot=splits[done]))
                done += 1
        if st["slot"] is not None:
            n, sp = st["slot"]["n"], st["slot"]["sp"]
            upto = done if sp is None else sp + 1
            if sp is not None and not st.get("open") and sp + 1 < len(splits):
                waiting = [s["n"] for s in stream[n:splits[sp + 1]["n"]] if s["sp"] is None and s["n"] not in used]
                upto += len(waiting) <= 1
            while done < upto:
                order.append(dict(kind="split", slot=splits[done]))
                done += 1
            if sp is None:
                used.add(n)
        order.append(st)
    annotate(order)
    return order, stream


MIXING = ("norms", "turns", "mgates", "mgates2", "mgates3", "arot", "mstates", "mtiles", "attend",
          "rstates", "rtiles")


def annotate(order):
    last, head_end, downs, norms = {}, {}, {}, []
    for i, st in enumerate(order):
        kind = st["kind"]
        st["i"] = i
        own_banks = kind == "arot" and not st["first"] or st.get("ticks", range(1)).start > 0
        st["prev"] = None if own_banks else last.get("mixing")
        st["region"] = last.get("region")
        st["h_slot"] = last.get("h")
        st["prev_branch"] = last.get("branch")
        if kind in MIXING:
            last["mixing"] = i
        if kind in ("region", "branch"):
            last[kind] = i
        if st.get("gen") is not None and st["slot"] is not None:
            last["h"] = st["slot"]["n"]
        if kind[0] in "mr" and "hd" in st:
            st["prev_head"] = head_end.get((kind[0], st["l"], st["hd"] - 1))
            if kind in ("mtiles", "rtiles"):
                head_end[kind[0], st["l"], st["hd"]] = i
        if kind == "down":
            for u in range(st["g"] * GROUP, st["g"] * GROUP + st["kt"]):
                downs[st["l"], u] = st["slot"]["n"]
        if kind == "up":
            st["ring_free"] = downs.get((st["l"], st["u"] - URING))
        if kind == "norms":
            st["back"] = {t: (n["gen"], n["tiles"].index(t)) for n in norms for t in st["tiles"]}
            norms += [st] if st["use"] in ("mid", "end") and st["ticks"].stop == len(st["tiles"]) + 2 else []
        if kind == "region":
            n = norms[-1] if norms else None
            st["stores"] = [(n["gen"], len(n["tiles"]) - 3 + b) for b in range(3)] if n else []


def branch(step, cols, l, ctx, which, n, s=None):
    name = {"m": "w_br_m", "a": "w_br_a", "r": "w_br_r"}[which]
    kt = 8 if which == "r" else 4
    step("branch", s or cols(name, l, n * COLS, kt=kt), 3, l=l, br=which, n=n, ctx=ctx, kt=kt)


class Events:

    def __init__(self, known, sems):
        self.known, self.sems, self.count, self.now = known, sems, {}, {}

    def mark(self, sem, *key, by=1):
        self.count[sem] = self.count.get(sem, 0) + by
        self.now.setdefault(key, {})[sem] = self.count[sem]
        return self.sems(sem), by

    def at(self, *key):
        if self.known is None:
            return self.sems("dry_run"), 1
        (sem, value), = self.known[key].items()
        return self.sems(sem), value

    def last(self, sem):
        return self.sems(sem), self.count.get(sem, 0)


def backbone(nc, ins, out, known):
    consts_np, CP, _, _ = constants()
    PP, NPAR = param_places()
    PLAN, STREAM = make_plan()
    seqs = {True: ((0, 0, CTX), (1, CTX, SEQ)), False: ((1, CTX, SEQ),)}

    with ExitStack() as ctx:
        semaphores = {}

        def semaphore(name):
            if name not in semaphores:
                semaphores[name] = ctx.enter_context(nc.semaphore(name))
            return semaphores[name]

        ev = Events(known, semaphore)

        def sb(name, shape, dt=F32):
            return ctx.enter_context(nc.sbuf_tensor(name, shape, dt))

        psg = ctx.enter_context(nc.psum_tensor("psum_products", [P, RING, 512], F32))
        psm = ctx.enter_context(nc.psum_tensor("psum_mixers", [P, 8 - RING, 512], F32))
        hh = sb("h_head", [P, KD, TOK], F32R)
        hl = sb("h_rest", [P, KD, TOK], F32R)
        acc = sb("acc", [P, TILES, D])
        raw = sb("raw", [P, 2, SLOT])
        wh = sb("w_head", [P, 2, SLOT], F32R)
        wl = sb("w_rest", [P, 2, SLOT], F32R)
        const = sb("const", [P, consts_np.shape[1]])
        par = sb("par", [P, DEPTH, NPAR])
        cvec = sb("cvec", [P, 3, KD, 2])
        vrow = sb("vrow", [P, COLS])
        vec = sb("vec", [P, DEPTH, 6 * KD, 2])
        aff = sb("aff", [P, 2, 2, KD, 2])
        small = sb("small", [P, 128])
        arena_size = ARENA_BYTES
        arena = sb("arena", [P, arena_size // 4])

        class Region:

            def __init__(self, start=0):
                self.off = start

            def __call__(self, name, shape, dt=F32):
                n = int(np.prod(shape[1:])) * 4
                t = nc.alloc_sbuf_tensor_at(name, shape, dt, offset=ARENA + self.off)
                self.off += -(-n // 32) * 32
                assert self.off <= arena_size, (name, self.off)
                return t

        ARENA = arena_offset(nc, arena)
        R = Region()
        gate_b = R("gate_b", [P, 2, D])
        stage = R("stage", [P, 3, D])
        bias_b = R("bias_b", [P, D])
        xs = R("xs", [P, 2, D])
        hf = R("hf", [P, 2, KD, P])
        R = Region(8 * 1024)
        uh = R("u_head", [P, URING, TOK], F32R)
        ul = R("u_rest", [P, URING, TOK], F32R)
        fa = R("f_a", [P, 2, PADDED])
        fc = R("f_c", [P, PADDED])
        ft = R("f_t", [P, TOK])
        fb = R("f_b", [P, TOK])
        fu = R("f_u", [P, TOK])
        R = Region()
        yT = R("yT", [P, 8, TOK])
        yh = Region(34 * 1024)("y_head", [P, 8, TOK], F32R)
        yl = Region()("y_rest", [P, 8, TOK], F32R)
        R = Region(12 * 1024)
        gm = R("gm", [P, 12, 48])
        g16 = R("g16", [P, TILES, 16])
        atr = R("atr", [P, 4, P])
        ma = R("m_a", [P, 2, PADDED])
        mc = R("m_c", [P, 2, PADDED])
        mt = R("m_t", [P, 2, PADDED])
        mqk = R("m_qk", [P, 2, PADDED])
        here = R.off
        mktok = R("m_ktok", [P, TILES, P])
        grow = Region(here)("m_grow", [P, TOK])
        mv = R("m_v", [P, TILES, P + 1])
        mo = R("m_o", [P, TILES, P])
        mcb = R("m_cb", [P, TILES, P + 1])
        mcf = R("m_cf", [P, TILES, P + 1])
        mvw = R("m_vw", [P, 4, P + 1])
        msc = R("m_sc", [P, 2, 4, P])
        mnd = R("m_nd", [P, 2, 4, P + 1])
        my = R("m_y", [P, 2, 3, P])
        R = Region(12 * 1024)
        ropea = R("rope_a", [P, 2, SEQ])
        aq = R("a_q", [P, 4, TOK])
        ak = R("a_k", [P, TOK])
        av = R("a_v", [P, TILES, P])
        atmp = R("a_tmp", [P, SEQ])
        here = R.off
        asb = R("a_s", [P, 4, 640])
        avt = Region(here)("a_vt", [P, TOK])
        apt = R("a_pt", [P, 2, 640])
        ay = R("a_y", [P, 2, 512])
        tga = R("a_tg", [P, 3, TILES, COLS])
        R = Region(24 * 1024)
        roper = R("rope_r", [P, 2, TOK])
        rqk = R("r_qk", [P, 2, TOK])
        rktok = R("r_ktok", [P, TILES, P])
        rv = R("r_v", [P, TILES, RV])
        rg = R("r_g", [P, TILES, RV])
        rb = R("r_b", [P, TILES - 1, RV])
        rf = R("r_f", [P, TILES - 1, RV])
        rvw = R("r_vw", [P, 4, RV])
        rs = R("r_s", [P, 2, 3, P])
        rd = R("r_d", [P, 3, P])
        here = R.off
        ry = R("r_y", [P, 2, 2, RV])
        rtmp = Region(here)("r_tmp", [P, TOK])
        R = Region(24 * 1024)
        tg = R("tg", [P, TILES, COLS])
        bt = R("bt", [P, 2, 512])

        def c(name):
            a, b = CP[name]
            return const[:, a:b]

        def pr(l, name, i=0, n=1):
            return par[:, l, PP[name][0] + i:PP[name][0] + i + n]

        res = nc.dram_tensor("residual", (TILES, P, D), F32, kind="Internal").ap()

        def raw_of(s):
            return raw[:, s["n"] % 2, 0:s["kt"] * s["cols"]].rearrange("p (k c) -> p k c", k=s["kt"])

        def halves(s):
            n = s["kt"] * s["cols"]
            a = wh[:, s["sp"] % 2, 0:n].rearrange("p (k c) -> p k c", k=s["kt"])
            b = wl[:, s["sp"] % 2, 0:n].rearrange("p (k c) -> p k c", k=s["kt"])
            return a, b

        def banks_a(st):
            out_, n = [], st["bank"]
            for ct in range(2):
                if st["kind"] == "mgates" and ct == 1:
                    continue
                both = st.get("ctx", True) or st["kind"] in ("mqk", "rqk") and ct == 1
                for q in seqs[both]:
                    out_.append((n, ct, q))
                    n += 1
            return out_

        def banks_b(st):
            n = st["bank"]
            if "pair" in st:
                return [(n, (2 * st["pair"], 2 * st["pair"] + 1))]
            both = st.get("ctx", True) or st["kind"] == "mvo"
            return [(n + i, (2 * p_, 2 * p_ + 1)) for i, p_ in enumerate((0, 1, 2) if both else (1, 2))]

        def gate_banks(st):
            which = [(q, half) for q in ((0, 1) if st["ctx"] else (1,)) for half in range(2)]
            return [(st["bank"] + i, q, half) for i, (q, half) in enumerate(which)]

        def gate_place(st, t):
            if st["br"] == "m":
                return acc[:, t:t + 2, st["n"] * COLS:(st["n"] + 1) * COLS]
            if st["br"] == "a" and st["n"] < 3:
                return tga[:, st["n"], t:t + 2, :]
            return tg[:, t:t + 2, :]

        def state_turns(st):
            return [j for j in range(2 * (TILES - 1)) if j // 4 + 1 in st["ticks"]]

        def weigh_values(eng, name, scaled, st, j):
            r_, l, hd = st["kind"][0], st["l"], st["hd"]
            d, s_ = j % 2, j // 2
            t = BACK[s_] if d else s_
            if j < 2:
                eng.wait_ge(*(ev.at("mcols", l) if r_ == "m" else ev.at("rw", l, hd)))
                eng.wait_ge(*(ev.at("mv", l, hd, 2) if r_ == "m" else ev.at("rv_sb", l, hd)))
                if r_ == "m":
                    eng.wait_ge(*ev.at("pads", st["region"]))
            if j >= 4:
                eng.wait_ge(*ev.at(r_ + "kv", l, hd, j - 4))
            elif st["prev_head"] is not None:
                eng.wait_ge(*ev.at("pe_step", st["prev_head"]))
            if r_ == "m":
                col = 24 * d + s_ * 4 + hd
                scaled(mvw[:, j % 4, :], mv[:, t, :], gm[:, 6, col:col + 1]).then_inc(
                    *ev.mark(name, "mvw", l, hd, j))
            else:
                scaled(rvw[:, j % 4, :], rv[:, t, :], small[:, 116 + d:117 + d]).then_inc(
                    *ev.mark(name, "rvw", l, hd, j))

        def av_banks(st):
            return [(st["bank"], range(0, 4)), (st["bank"] + 1, range(4, TILES))]

        block = ctx.enter_context(nc.Block())

        def walk(name):
            for i, st in enumerate(PLAN):
                yield i, st
                ev.now[name + "_step", i] = {name: ev.count.get(name, 0)}

        def phase_end(eng, i):
            if PLAN[i]["region"] is None:
                return
            for name in ("pe", "act", "dve", "pool"):
                eng.wait_ge(*ev.at(name + "_step", i - 1))
            for n, k in PLAN[i]["stores"]:
                eng.wait_ge(*ev.at("stored", n, k))

        @block.sync
        def _(sp):
            sp.dma_start(cvec[:, 0], ins["cvec"]).then_inc(*ev.mark("cvec_in", "cvec", by=16))
            offs = np.cumsum([0] + [s["kt"] * s["cols"] * P for s in STREAM])
            order = {id(s): i for i, s in enumerate(STREAM)}

            def load(i):
                s = STREAM[i]
                if i >= 2:
                    sp.wait_ge(*ev.at("raw_free", STREAM[i - 2]["n"]))
                n = s["kt"] * s["cols"]
                src = ins["stream"][int(offs[i]):int(offs[i]) + n * P].rearrange("(p c) -> p c", p=P)
                sp.dma_start(raw[:, s["n"] % 2, 0:n], src).then_inc(
                    *ev.mark(f"raw{s['n'] % 2}_in", "raw", s["n"], by=16))

            load(0)
            load(1)
            loaded = 2
            sp.dma_start(par[:], ins["params"]).then_inc(*ev.mark("par_in", "par", by=16))
            sp.dma_start(const[:], ins["consts"]).then_inc(*ev.mark("const_in", "const", by=16))
            for i, st in enumerate(PLAN):
                kind = st["kind"]
                s = st["slot"]
                if s is not None:
                    ahead = 1 if kind == "split" else 3 if s["sp"] is not None else 2
                    while loaded < min(order[id(s)] + ahead, len(STREAM)):
                        load(loaded)
                        loaded += 1
                if kind == "region":
                    if st["name"] == "attn":
                        phase_end(sp, i)
                        sp.dma_start(ropea[:], ins["rope_a"]).then_inc(*ev.mark("rope_in", "rope", i, by=16))
                    if st["name"] == "ret":
                        phase_end(sp, i)
                        sp.dma_start(roper[:], ins["rope_r"]).then_inc(*ev.mark("rope_in", "rope", i, by=16))
                    if st["name"] in ("norm", "final"):
                        phase_end(sp, i)
                    if st["name"] == "final":
                        sp.dma_start(bias_b[:], ins["final_w"].broadcast_to((P, D))).then_inc(
                            *ev.mark("fnorm_in", "fnorm", by=16))
                if kind == "norms":
                    l, use = st["l"], st["use"]
                    ahead = [k + 2 for k in st["ticks"]] + ([0, 1] if 0 in st["ticks"] else [])
                    for k, t in [(k, st["tiles"][k]) for k in sorted(ahead) if k < len(st["tiles"])]:
                        if k >= 3:
                            if use != "last":
                                sp.wait_ge(*ev.at("xs", st["gen"], k - 3))
                            if use != "first":
                                sp.wait_ge(*ev.at("stored", st["gen"], k - 3))
                        if t not in st["back"]:
                            src = ins["ctx"][0, t * P:(t + 1) * P, :] if t < CT else \
                                ins["x"][0, (t - CT) * P:(t - CT + 1) * P, :]
                        else:
                            sp.wait_ge(*ev.at("stored", *st["back"][t]))
                            src = res[t]
                        sp.dma_start(stage[:, k % 3], src).then_inc(
                            *ev.mark(f"stage{k % 3}_in", "stage", st["gen"], k, by=16))

        def akeys(t):
            return ([*range(max(CT, t - 1), min(TILES, t + 2))] if t >= CT else []) + [0, 1]

        @block.tensor
        def _(pe):
            def mm(o, a, b, start=True, stop=True):
                return nc.tensor.matmul(o, a, b, start=start, stop=stop)

            def three(o, wa, ha, kts, w_first, first=0, end=KD):
                last = None
                for k in kts:
                    for j, (a, b) in enumerate(((0, 0), (1, 0), (0, 1))):
                        w, h = wa[a](k), ha[b](k)
                        x, y = (w, h) if w_first else (h, w)
                        last = mm(o, x, y, k == first and j == 0, k == end - 1 and j == 2)
                return last

            def free_bank(n):
                if n >= RING:
                    pe.wait_ge(*ev.at("bank_free", n - RING))

            def part_a(st):
                w = halves(st["slot"])
                for n, ct, (q, t0, size) in banks_a(st):
                    free_bank(n)
                    for t in range(t0 // P, (t0 + size) // P):
                        pe.wait_ge(*ev.at("h", st["gen"], t))
                    wa = [lambda k, x=x: x[:, k, ct * P:(ct + 1) * P] for x in w]
                    ha = [lambda k, x=x: x[:, k, t0:t0 + size] for x in (hh, hl)]
                    three(psg[:, n % RING, 0:size], wa, ha, range(KD), True).then_inc(*ev.mark("pe", "bank", n))

            def part_b(st, c0, cn):
                w = halves(st["slot"])
                piece = st.get("piece")
                for n, tt in banks_b(st):
                    if not piece:
                        free_bank(n)
                    for i, t in enumerate(tt):
                        if piece is not None and i != piece // 2:
                            continue
                        kts = range(KD) if piece is None else range(4 * (piece % 2), 4 * (piece % 2) + 4)
                        pe.wait_ge(*ev.at("h", st["gen"], t))
                        wa = [lambda k, x=x: x[:, k, c0:c0 + cn] for x in w]
                        ha = [lambda k, x=x: x[:, k, t * P:(t + 1) * P] for x in (hh, hl)]
                        last = three(psg[:, n % RING, i * 256:i * 256 + cn], wa, ha, kts, False)
                    last.then_inc(*(ev.mark("pe", "bank", n) if piece in (None, 3) else ev.mark("pe", "piece")))

            for i, st in walk("pe"):
                kind, s = st["kind"], st["slot"]
                l, hd, t = st.get("l"), st.get("hd"), st.get("t")
                if kind == "split":
                    continue
                if kind in MIXING:
                    if st["prev"] is not None:
                        pe.wait_ge(*ev.at("act_step", st["prev"]))
                        pe.wait_ge(*ev.at("dve_step", st["prev"]))
                        pe.wait_ge(*ev.at("pool_step", st["prev"]))
                if s is not None:
                    if s["sp"] is not None:
                        pe.wait_ge(*ev.at("rest", s["n"]))
                    else:
                        pe.wait_ge(*ev.at("raw", s["n"]))
                if kind == "vector":
                    pe.wait_ge(*ev.at("silu_c"))
                    piece = st["piece"]
                    if piece == 0:
                        free_bank(st["bank"])
                    w = raw_of(s)
                    bank = psg[:, st["bank"] % RING, :]
                    if piece < 4:
                        for k in (2 * piece, 2 * piece + 1):
                            last = mm(bank[0:2, 0:COLS], cvec[:, 2, k, :], w[:, k, :], k == 0, k == KD - 1)
                        last.then_inc(*ev.mark("pe", "vrow", l, st["n"]))
                    else:
                        pe.wait_ge(*ev.at("vrow_sb", l, st["n"]))
                        if (l, st["n"]) == (0, 0):
                            pe.wait_ge(*ev.at("const"))
                        for ct in range(2):
                            last = mm(bank[:, 2 * ct:2 * ct + 2], vrow[0:2, ct * P:(ct + 1) * P],
                                      c("ident")[0:2, 0:2])
                        last.then_inc(*ev.mark("pe", "bank", st["bank"]))
                elif kind == "gates":
                    pe.wait_ge(*ev.at("vec", l, 11 + 12 * st["which"]))
                    for n, q, half in gate_banks(st):
                        free_bank(n)
                        for j in range(4):
                            m = (2 + 3 * st["which"]) * KD + 4 * half + j
                            last = mm(psg[:, n % RING, j * P:(j + 1) * P],
                                      vec[:, l, m, q:q + 1].broadcast_to((P, P)), c("ident"))
                        last.then_inc(*ev.mark("pe", "bank", n))
                elif kind == "norms":
                    if st["use"] == "last":
                        continue
                    for k in [k - 1 for k in st["ticks"] if 1 <= k <= len(st["tiles"])]:
                        pe.wait_ge(*ev.at("xs", st["gen"], k))
                        if k >= 2:
                            pe.wait_ge(*ev.at("hf", st["gen"], k - 2))
                        for half in range(2):
                            for kk in range(4 * half, 4 * half + 4):
                                last = nc.tensor.transpose(psm[:, 2 * (k % 2) + half, (kk % 4) * P:(kk % 4 + 1) * P],
                                                           xs[:, k % 2, kk * P:(kk + 1) * P], c("ident"))
                        last.then_inc(*ev.mark("pe", "xT", st["gen"], k))
                elif kind == "turns":
                    pe.wait_ge(*ev.at("pool_step", st["prev_branch"]))
                    pe.wait_ge(*ev.at("dve_step", st["prev_branch"]))
                    for k, t in enumerate(st["tiles"]):
                        if k >= 2:
                            pe.wait_ge(*ev.at("h", st["gen"], st["tiles"][k - 2]))
                        for half in range(2):
                            for kk in range(4 * half, 4 * half + 4):
                                last = nc.tensor.transpose(psm[:, half + 2 * (k % 2), (kk % 4) * P:(kk % 4 + 1) * P],
                                                           acc[:, t, kk * P:(kk + 1) * P], c("ident"))
                            last.then_inc(*ev.mark("pe", "turned", l, t, half))
                elif kind == "mgates":
                    w = halves(st["slot"])
                    for n, _, (q, t0, size) in banks_a(st):
                        free_bank(n)
                        for t in range(t0 // P, (t0 + size) // P):
                            pe.wait_ge(*ev.at("h", st["gen"], t))
                        wa = [lambda k, x=x: x[:, k, :] for x in w]
                        ha = [lambda k, x=x: x[:, k, t0:t0 + size] for x in (hh, hl)]
                        three(psg[0:16, n % RING, 0:size], wa, ha, range(KD), True).then_inc(
                            *ev.mark("pe", "bank", n))
                    pe.wait_ge(*ev.at("grow", l))
                    for t in range(TILES):
                        last = mm(psm[:, 3, 16 * t:16 * t + 16], grow[0:16, t * P:(t + 1) * P], c("ident")[0:16, 0:16])
                    last.then_inc(*ev.mark("pe", "gturned", l))
                elif kind == "mgates2":
                    pe.wait_ge(*ev.at("logf", l))
                    mm(psm[:, 3, 0:24], c("upto"), gm[:, 2, 0:24])
                    mm(psm[:, 3, 24:48], c("since"), gm[:, 2, 24:48])
                    mm(psm[:, 3, 48:96], c("ones"), gm[:, 2, :]).then_inc(*ev.mark("pe", "sums", l))
                    pe.wait_ge(*ev.at("A", l))
                    mm(psm[0:24, 2, 0:P], gm[:, 4, 0:24], c("ident"))
                    mm(psm[0:24, 2, P:2 * P], gm[:, 4, 24:48], c("flip")).then_inc(*ev.mark("pe", "AT", l))
                elif kind == "mgates3":
                    pe.wait_ge(*ev.at("scan", l))
                    mm(psm[:, 1, 0:24], atr[0:24, 2, :], c("ident")[0:24, 0:24])
                    mm(psm[:, 1, 24:48], atr[0:24, 3, :], c("ident")[0:24, 0:24]).then_inc(
                        *ev.mark("pe", "LM", l))
                    pe.wait_ge(*ev.at("LMb", l))
                    mm(psm[:, 1, 48:72], c("flip"), gm[:, 5, 24:48]).then_inc(*ev.mark("pe", "LMf", l))
                elif kind in ("mqk", "rqk", "aq", "up"):
                    part_a(st)
                elif kind == "akv":
                    part_a(st)
                elif kind == "avturn":
                    pe.wait_ge(*ev.at("araw", l, 2, 1))
                    for n, tt in av_banks(st):
                        free_bank(n)
                        for j, t_ in enumerate(tt):
                            last = nc.tensor.transpose(psg[:, n % RING, j * P:(j + 1) * P],
                                                       avt[:, t_ * P:(t_ + 1) * P], c("ident"))
                        last.then_inc(*ev.mark("pe", "bank", n))
                elif kind == "arot":
                    for ct in range(1 + (st["g"] < 2)):
                        pe.wait_ge(*ev.at("araw", l, st["g"], ct))
                        x = ak[:, CTX:TOK] if st["g"] == 2 else aq[:, 2 * st["g"] + ct, CTX:TOK]
                        mm(psm[:, 2 * st["g"] + ct, 0:SEQ], c("rot"), x).then_inc(
                            *ev.mark("pe", "arot", l, st["g"], ct))
                elif kind in ("mvo", "rv", "rg", "gate", "wout"):
                    part_b(st, 0, COLS)
                elif kind == "branch":
                    w = halves(s)
                    for n, tt in banks_b(st):
                        free_bank(n)
                        for j, t_ in enumerate(tt):
                            pe.wait_ge(*ev.at("ysplit", l, st["br"], t_))
                            wa = [lambda k, x=x: x[:, k, :] for x in w]
                            ya = [lambda k, x=x: x[:, k, t_ * P:(t_ + 1) * P] for x in (yh, yl)]
                            last = three(psg[:, n % RING, j * 256:j * 256 + 256], wa, ya, range(st["kt"]), False,
                                         0, st["kt"])
                        last.then_inc(*ev.mark("pe", "bank", n))
                elif kind == "down":
                    w = halves(s)
                    for j, t_ in enumerate(range(st["first"], TILES)):
                        n = st["bank"] + j
                        free_bank(n)
                        pe.wait_ge(*ev.at("u", l, st["g"] * GROUP + st["kt"] - 1))
                        wa = [lambda k, x=x: x[:, k, :] for x in w]
                        ha = [lambda k, x=x: x[:, (st["g"] * GROUP + k) % URING, t_ * P:(t_ + 1) * P]
                              for x in (uh, ul)]
                        three(psg[:, n % RING, :], wa, ha, range(st["kt"]), False, 0, st["kt"]).then_inc(
                            *ev.mark("pe", "bank", n))
                elif kind in ("mstates", "rstates"):
                    r_ = kind[0]
                    if 0 in st["ticks"]:
                        pe.wait_ge(*ev.at(r_ + "qk", l, hd))
                    for t in range(TILES) if 0 in st["ticks"] else ():
                        a = at_tile(t) if r_ == "m" else t * P
                        src = (mqk if r_ == "m" else rqk)[:, 1, a:a + P]
                        last = nc.tensor.transpose(psm[:, 3 - t // 4, (t % 4) * P:(t % 4 + 1) * P], src, c("ident"))
                    if 0 in st["ticks"]:
                        last.then_inc(*ev.mark("pe", r_ + "ktokT", l, hd))
                        continue
                    pe.wait_ge(*ev.at(r_ + "kt", l, hd))
                    for j in state_turns(st):
                        t = j // 2 if j % 2 == 0 else BACK[j // 2]
                        pe.wait_ge(*ev.at(r_ + "vw", l, hd, j))
                        if j >= 3:
                            pe.wait_ge(*ev.at(r_ + "C", l, hd, j - 3))
                        b = (0, 1, 4)[j % 3]
                        o, k_, v_ = (psm[:, b, 0:P + 1], mktok, mvw[:, j % 4, :]) if r_ == "m" else \
                            (psm[:, b, 0:RV], rktok, rvw[:, j % 4, :])
                        mm(o, k_[:, t, :], v_).then_inc(*ev.mark("pe", r_ + "kv", l, hd, j))
                elif kind == "mtiles":
                    n = len(st["tiles"])
                    for i_ in st["ticks"]:
                        if i_ >= 5:
                            j = i_ - 5
                            if j >= 1:
                                pe.wait_ge(*ev.at("myT_sb", l, hd, j - 1))
                            pe.wait_ge(*ev.at("my", l, hd, j))
                            nc.tensor.transpose(psm[:, 4, 0:P], my[:, j % 2, 2, :], c("ident")).then_inc(
                                *ev.mark("pe", "myT", l, hd, j))
                        if i_ < n:
                            t = st["tiles"][i_]
                            a = at_tile(t)
                            ba = psm[:, i_ % 2]
                            if i_ >= 2:
                                pe.wait_ge(*ev.at("mw", l, hd, i_ - 2))
                            mm(ba[:, 0:P], mqk[:, 1, a:a + P], mqk[:, 0, a:a + P])
                            for d in range(2):
                                s_ = t if d == 0 else BACK.index(t)
                                col = d * 24 + s_ * 4 + hd
                                last = mm(ba[:, (1 + d) * P:(2 + d) * P], gm[:, 9, col:col + 1].broadcast_to((P, P)),
                                          c("ident"))
                            last.then_inc(*ev.mark("pe", "mscore", l, hd, i_))
                        if 2 <= i_ <= n + 1:
                            j = i_ - 2
                            t = st["tiles"][j]
                            a = at_tile(t)
                            if j >= 1:
                                pe.wait_ge(*ev.at("mnd", l, hd, j - 1))
                            mm(psm[:, 2, 0:P + 1], mqk[:, 0, a:a + P], mcf[:, t, :])
                            mm(psm[:, 2, P + 1:2 * (P + 1)], mqk[:, 0, a:a + P], mcb[:, BACK.index(t), :]).then_inc(
                                *ev.mark("pe", "minter", l, hd, j))
                            if j >= 1:
                                pe.wait_ge(*ev.at("mintra_sb", l, hd, j - 1))
                            pe.wait_ge(*ev.at("mw", l, hd, j))
                            mm(psm[:, 3, 0:P + 1], msc[:, j % 2, 2, :], mv[:, t, :])
                            mm(psm[:, 3, P + 1:2 * (P + 1)], msc[:, j % 2, 3, :], mv[:, t, :]).then_inc(
                                *ev.mark("pe", "mintra", l, hd, j))
                elif kind == "attend":
                    n = len(st["heads"])
                    pe.wait_ge(*ev.at("arope", l))
                    for i_ in st["ticks"]:
                        if i_ < n:
                            t, hd = st["heads"][i_]
                            lo = (hd // 4) * AD
                            if i_ >= 1:
                                pe.wait_ge(*ev.at("as", l, i_ - 1))
                            q_ = aq[lo:lo + AD, hd % 4, t * P:(t + 1) * P]
                            if t >= CT:
                                k0, k1 = max(CT, t - 1), min(TILES, t + 2)
                                mm(psm[:, 0, 0:(k1 - k0) * P], q_, ak[lo:lo + AD, k0 * P:k1 * P])
                            mm(psm[:, 1, 0:CTX], q_, ak[lo:lo + AD, 0:CTX]).then_inc(
                                *ev.mark("pe", "ascore", l, i_))
                        if 2 <= i_ <= n + 1:
                            j = i_ - 2
                            t, hd = st["heads"][j]
                            pe.wait_ge(*ev.at("ap", l, j))
                            if j >= 1:
                                pe.wait_ge(*ev.at("apt", l, j - 1))
                            for m in range(len(akeys(t))):
                                o = psm[:, 2, m * P:(m + 1) * P] if m < 4 else psm[:, 3, 0:P]
                                last = nc.tensor.transpose(o, asb[:, j % 4, m * P:(m + 1) * P], c("ident"))
                            last.then_inc(*ev.mark("pe", "apT", l, j))
                        if i_ >= 3:
                            j = i_ - 3
                            t, hd = st["heads"][j]
                            lo = (hd // 4) * AD
                            pe.wait_ge(*ev.at("apt", l, j))
                            if j >= 1:
                                pe.wait_ge(*ev.at("ay", l, j - 1))
                                if hd == 0:
                                    pe.wait_ge(*ev.at("yT", l, "a", st["heads"][j - 1][0]))
                            keys = akeys(t)
                            for m, kt_ in enumerate(keys):
                                last = mm(psm[:, 4, 0:AD], apt[:, j % 2, m * P:(m + 1) * P],
                                          av[:, kt_, lo:lo + AD], m == 0, m == len(keys) - 1)
                            last.then_inc(*ev.mark("pe", "apv", l, j))
                            if hd == AH - 1:
                                pe.wait_ge(*ev.at("ay", l, j))
                                for m in range(4):
                                    last = nc.tensor.transpose(psm[:, 4, m * P:(m + 1) * P],
                                                               ay[:, t % 2, m * P:(m + 1) * P], c("ident"))
                                last.then_inc(*ev.mark("pe", "ayT", l, t))
                elif kind == "rtiles":
                    n = len(st["tiles"])
                    for i_ in st["ticks"]:
                        if i_ < n:
                            t = st["tiles"][i_]
                            if i_ >= 1:
                                pe.wait_ge(*ev.at("rs", l, hd, i_ - 1))
                            mm(psm[:, 0, 0:P], rqk[:, 1, t * P:(t + 1) * P],
                               rqk[:, 0, t * P:(t + 1) * P]).then_inc(*ev.mark("pe", "rscore", l, hd, i_))
                        if 1 <= i_ <= n:
                            j = i_ - 1
                            t = st["tiles"][j]
                            o = psm[:, 2 + j % 3, 0:RV]
                            if j >= 3:
                                pe.wait_ge(*ev.at("rnormed", l, hd, j - 3))
                            pe.wait_ge(*ev.at("rs", l, hd, j))
                            parts = [(rs[:, j % 2, 0, :], rv[:, t, :])]
                            if t > 0:
                                parts.append((rs[:, j % 2, 1, :], rf[:, t - 1, :]))
                            if BACK.index(t) > 0:
                                parts.append((rs[:, j % 2, 2, :], rb[:, BACK.index(t) - 1, :]))
                            pe.wait_ge(*ev.at("rq", l, hd, j))
                            for m, (a, b) in enumerate(parts):
                                last = mm(o, a, b, m == 0, m == len(parts) - 1)
                            last.then_inc(*ev.mark("pe", "rout", l, hd, j))
                        if i_ >= 4:
                            j = i_ - 4
                            if j >= 1:
                                pe.wait_ge(*ev.at("ryT_sb", l, hd, j - 1))
                            pe.wait_ge(*ev.at("ry", l, hd, j))
                            for m in range(2):
                                last = nc.tensor.transpose(psm[:, 1, m * P:(m + 1) * P],
                                                           ry[:, j % 2, 1, m * P:(m + 1) * P], c("ident"))
                            last.then_inc(*ev.mark("pe", "ryT", l, hd, j))
                if s is not None:
                    if kind == "vector" and st["piece"] == 4:
                        continue
                    ev.now[("w_free", s["n"])] = {"pe": ev.count["pe"]}
                    if s["sp"] is not None:
                        ev.now[("w_free_sp", s["sp"])] = {"pe": ev.count["pe"]}
                    if s["sp"] is None:
                        ev.now[("raw_free", s["n"])] = {"pe": ev.count["pe"]}

        @block.scalar
        def _(act):
            act.wait_ge(*ev.at("cvec"))
            nc.scalar.activation(cvec[:, 1], cvec[:, 0], ACT.Tanh, scale=0.5).then_inc(
                *ev.mark("act", "tanh_c"))
            act.wait_ge(*ev.at("par"))
            act.wait_ge(*ev.at("const"))
            for i, st in walk("act"):
                kind, s = st["kind"], st["slot"]
                l, hd, t = st.get("l"), st.get("hd"), st.get("t")
                if kind == "region":
                    phase_end(act, i)
                if kind == "split":
                    n = s["kt"] * s["cols"]
                    act.wait_ge(*ev.at("raw", s["n"]))
                    if s["sp"] >= 2:
                        act.wait_ge(*ev.at("w_free_sp", s["sp"] - 2))
                    nc.scalar.activation(wh[:, s["sp"] % 2, 0:n], raw[:, s["n"] % 2, 0:n], ACT.Copy).then_inc(
                        *ev.mark("act", "head", s["n"]))
                elif kind == "ysplit":
                    for t in st["tiles"]:
                        ts = slice(t * P, (t + 1) * P)
                        nc.scalar.activation(yh[:, 0:st["kt"], ts], yT[:, 0:st["kt"], ts], ACT.Copy).then_inc(
                            *ev.mark("act", "yh", l, st["br"], t))
                elif kind == "norms":
                    use, n = st["use"], len(st["tiles"])
                    for k in st["ticks"]:
                        cc = 4 * (k % 2)
                        if k < n:
                            act.wait_ge(*ev.at("stage" if use == "first" else "rsum", st["gen"], k))
                            if k >= 2 and use != "last":
                                act.wait_ge(*ev.at("xT", st["gen"], k - 2))
                            nc.scalar.activation(xs[:, k % 2], stage[:, k % 3], ACT.Square,
                                                 accum_out=small[:, cc:cc + 1]).then_inc(
                                                     *ev.mark("act", "ss", st["gen"], k))
                            if use in ("mid", "end"):
                                act.dma_start(res[st["tiles"][k]], stage[:, k % 3]).then_inc(
                                    *ev.mark(f"store{k % 3}", "stored", st["gen"], k, by=16))
                        if 1 <= k <= n and use == "last":
                            act.wait_ge(*ev.at("outrow", st["gen"], k - 1))
                            t = st["tiles"][k - 1]
                            act.dma_start(out[0, (t - CT) * P:(t - CT + 1) * P, :], stage[:, (k - 1) % 3]).then_inc(
                                *ev.mark(f"out{(k - 1) % 3}", "stored", st["gen"], k - 1, by=16))
                        if k >= 2 and use != "last":
                            if k == 2 and st["h_slot"] is not None:
                                act.wait_ge(*ev.at("w_free", st["h_slot"]))
                            t = st["tiles"][k - 2]
                            act.wait_ge(*ev.at("hf", st["gen"], k - 2))
                            nc.scalar.activation(hh[:, :, t * P:(t + 1) * P], hf[:, k % 2], ACT.Copy).then_inc(
                                *ev.mark("act", "hh", st["gen"], k - 2))
                        if k < n and use != "last":
                            act.wait_ge(*ev.at("rstd", st["gen"], k))
                            act.wait_ge(*ev.at("ss", st["gen"], k))
                            nc.scalar.activation(xs[:, k % 2], stage[:, k % 3], ACT.Copy,
                                                 scale=small[:, cc + 2:cc + 3]).then_inc(
                                                     *ev.mark("act", "xs", st["gen"], k))
                elif kind == "turns":
                    act.wait_ge(*ev.at("w_free", st["h_slot"]))
                    for k, t in enumerate(st["tiles"]):
                        for half in range(2):
                            act.wait_ge(*ev.at("turned", l, t, half))
                            nc.scalar.activation(
                                hh[:, half * 4:half * 4 + 4, t * P:(t + 1) * P],
                                psm[:, half + 2 * (k % 2), :].rearrange("p (k c) -> p k c", k=4),
                                ACT.Copy).then_inc(*ev.mark("act", "turn_hh", l, t, half))
                elif kind == "mgates":
                    act.wait_ge(*ev.at("Fx", l))
                    nc.scalar.activation(gm[:, 1, :], gm[:, 0, :], ACT.Abs).then_inc(*ev.mark("act", "absf", l))
                    act.wait_ge(*ev.last("act"))
                    nc.scalar.activation(gm[:, 3, :], gm[:, 1, :], ACT.Exp, scale=-1.0).then_inc(
                        *ev.mark("act", "expf", l))
                    act.wait_ge(*ev.last("act"))
                    nc.scalar.activation(gm[:, 1, :], gm[:, 3, :], ACT.Ln, bias=c("one")).then_inc(
                        *ev.mark("act", "lnf", l))
                elif kind == "mgates3":
                    act.wait_ge(*ev.at("mlogs", l))
                    nc.scalar.activation(gm[:, 6:9, :], gm[:, 6:9, :], ACT.Exp).then_inc(
                        *ev.mark("act", "mexp1", l))
                    nc.scalar.activation(gm[:, 10, :], gm[:, 10, :], ACT.Exp).then_inc(
                        *ev.mark("act", "mexp", l))
                elif kind == "mqk":
                    if hd:
                        act.wait_ge(*ev.at("mt", l, hd - 1))
                    for n, ct, (q, t0, size) in banks_a(st):
                        act.wait_ge(*ev.at("bank", n))
                        a = at_tile(t0 // P)
                        nc.scalar.activation(ma[:, ct, a:a + size], psg[:, n % RING, 0:size], ACT.Copy).then_inc(
                            *ev.mark("act", "bank_free", n))
                        ev.now[("ma", l, hd, ct)] = {"act": ev.count["act"]}
                    for ct in range(2):
                        r0 = 1 if (st["ctx"] or ct == 1) else at_tile(CT)
                        act.wait_ge(*ev.at("conv", l, hd, ct))
                        nc.scalar.activation(mt[:, ct, r0:PADDED - 1], mc[:, ct, r0:PADDED - 1], ACT.Tanh, scale=0.5).then_inc(
                            *ev.mark("act", "mt_", l, hd, ct))
                elif kind == "mvo":
                    for n, tt in banks_b(st):
                        act.wait_ge(*ev.at("bank", n))
                        if st["prev_head"] is not None:
                            act.wait_ge(*ev.at("pe_step", st["prev_head"]))
                            act.wait_ge(*ev.at("dve_step", st["prev_head"]))
                            act.wait_ge(*ev.at("pool_step", st["prev_head"]))
                        ps = psg[:, n % RING, :].rearrange("p (j c) -> p j c", j=2)
                        nc.scalar.activation(mv[:, tt[0]:tt[0] + 2, 0:P], ps[:, :, 0:P], ACT.Copy).then_inc(
                            *ev.mark("act", "mv", l, hd, tt[0] // 2))
                        nc.scalar.activation(mo[:, tt[0]:tt[0] + 2, :], ps[:, :, P:2 * P], ACT.Tanh, scale=0.5).then_inc(
                            *ev.mark("act", "bank_free", n))
                        ev.now[("mo", l, hd)] = {"act": ev.count["act"]}
                elif kind in ("mstates", "rstates"):
                    r_ = kind[0]
                    for j in state_turns(st):
                        if j % 2 == 1:
                            weigh_values(act, "act", lambda o_, x_, w_: nc.scalar.activation(
                                o_, x_, ACT.Copy, scale=w_), st, j)
                    if 0 not in st["ticks"]:
                        continue
                    dst = mktok if r_ == "m" else rktok
                    act.wait_ge(*ev.at(r_ + "ktokT", l, hd))
                    if st["prev_head"] is not None:
                        act.wait_ge(*ev.at("pe_step", st["prev_head"]))
                    nc.scalar.activation(dst[:, 0:4, :], psm[:, 3, :].rearrange("p (k c) -> p k c", k=4),
                                         ACT.Copy).then_inc(*ev.mark("act", "kt_", l))
                    nc.scalar.activation(dst[:, 4:6, :], psm[:, 2, 0:2 * P].rearrange("p (k c) -> p k c", k=2),
                                         ACT.Copy).then_inc(*ev.mark("act", r_ + "kt", l, hd))
                elif kind == "mtiles":
                    n = len(st["tiles"])
                    for i_ in st["ticks"]:
                        if 2 <= i_ <= n + 1:
                            j = i_ - 2
                            if j >= 2:
                                act.wait_ge(*ev.at("mnd", l, hd, j - 2))
                            act.wait_ge(*ev.at("mintra", l, hd, j))
                            nc.scalar.activation(
                                mnd[:, j % 2, 0:2, :], psm[:, 3, 0:2 * (P + 1)].rearrange("p (d c) -> p d c", d=2),
                                ACT.Copy).then_inc(*ev.mark("act", "mintra_sb", l, hd, j))
                        if i_ < n:
                            act.wait_ge(*ev.at("marg", l, hd, i_))
                            nc.scalar.activation(msc[:, i_ % 2, 0:2, :], msc[:, i_ % 2, 0:2, :], ACT.Exp).then_inc(
                                *ev.mark("act", "mexpw", l, hd, i_))
                        if i_ >= 5:
                            j = i_ - 5
                            t = st["tiles"][j]
                            act.wait_ge(*ev.at("myT", l, hd, j))
                            nc.scalar.activation(yT[:, hd, t * P:(t + 1) * P], psm[:, 4, 0:P], ACT.Copy,
                                                 scale=pr(l, "m_norm", hd)).then_inc(
                                *ev.mark("act", "yT", l, "m", t))
                            ev.now["myT_sb", l, hd, j] = {"act": ev.count["act"]}
                elif kind == "gate" and st.get("piece", 3) == 3:
                    for n, tt in banks_b(st):
                        act.wait_ge(*ev.at("bank", n))
                        if st["prev_branch"] is not None:
                            act.wait_ge(*ev.at("dve_step", st["prev_branch"]))
                        ps = psg[:, n % RING, :].rearrange("p (j c) -> p j c", j=2)
                        nc.scalar.activation(gate_place(st, tt[0]), ps, ACT.Tanh, scale=0.5).then_inc(
                            *ev.mark("act", "bank_free", n))
                        ev.now[("tg", l, st["br"], st["n"], tt[0])] = {"act": ev.count["act"]}
                elif kind in ("aq", "akv"):
                    for n, ct, (q, t0, size) in banks_a(st):
                        act.wait_ge(*ev.at("bank", n))
                        dst = (avt if ct else ak) if kind == "akv" else aq[:, 2 * st["g"] + ct]
                        dst = dst[:, t0:t0 + size]
                        nc.scalar.activation(dst, psg[:, n % RING, 0:size], ACT.Copy).then_inc(
                            *ev.mark("act", "bank_free", n))
                        ev.now[("araw", l, st.get("g", 2), ct)] = {"act": ev.count["act"]}
                elif kind == "avturn":
                    for n, tt in av_banks(st):
                        act.wait_ge(*ev.at("bank", n))
                        nc.scalar.activation(av[:, tt[0]:tt[-1] + 1, :],
                                             psg[:, n % RING, 0:P * len(tt)].rearrange("p (t c) -> p t c", t=len(tt)),
                                             ACT.Copy).then_inc(*ev.mark("act", "bank_free", n))
                elif kind == "attend":
                    n = len(st["heads"])
                    for i_ in st["ticks"]:
                        if 2 <= i_ <= n + 1:
                            j = i_ - 2
                            nk = len(akeys(st["heads"][j][0])) * P
                            n1 = min(nk, 512)
                            act.wait_ge(*ev.at("apT", l, j))
                            if j >= 2:
                                act.wait_ge(*ev.at("apv", l, j - 2))
                            nc.scalar.activation(apt[:, j % 2, 0:n1], psm[:, 2, 0:n1], ACT.Copy).then_inc(
                                *ev.mark("act", "apt", l, j))
                            if nk > 512:
                                nc.scalar.activation(apt[:, j % 2, 512:640], psm[:, 3, 0:P], ACT.Copy).then_inc(
                                    *ev.mark("act", "apt", l, j))
                        if i_ < n:
                            t, hd = st["heads"][i_]
                            nk = len(akeys(t)) * P
                            s0 = 64 + 8 * (i_ % 4)
                            act.wait_ge(*ev.at("anm", l, i_))
                            nc.scalar.activation(asb[:, i_ % 4, 0:nk], asb[:, i_ % 4, 0:nk], ACT.Exp,
                                                 bias=small[:, s0 + 1:s0 + 2],
                                                 accum_out=small[:, s0 + 2:s0 + 3]).then_inc(
                                *ev.mark("act", "ap_", l, i_))
                            nc.scalar.activation(small[:, s0 + 3:s0 + 4], pr(l, "sink", hd), ACT.Exp,
                                                 bias=small[:, s0 + 1:s0 + 2]).then_inc(
                                                     *ev.mark("act", "ap", l, i_))
                        if i_ >= 3 and st["heads"][i_ - 3][1] == AH - 1:
                            t = st["heads"][i_ - 3][0]
                            act.wait_ge(*ev.at("ayT", l, t))
                            nc.scalar.activation(yT[:, 0:4, t * P:(t + 1) * P],
                                                 psm[:, 4, :].rearrange("p (k c) -> p k c", k=4),
                                                 ACT.Copy).then_inc(*ev.mark("act", "yT", l, "a", t))
                elif kind == "rqk":
                    if hd == 0:
                        x = small[:, 104:112]
                        nc.scalar.activation(x, pr(l, "ret", 0, 8), ACT.Abs).then_inc(*ev.mark("act", "r", l))
                        act.wait_ge(*ev.last("act"))
                        nc.scalar.activation(x, x, ACT.Exp, scale=-1.0).then_inc(*ev.mark("act", "r", l))
                        act.wait_ge(*ev.last("act"))
                        nc.scalar.activation(x, x, ACT.Ln, bias=c("one")).then_inc(*ev.mark("act", "rabs", l))
                    for ct in (0, 1):
                        for n, ct_, (q, t0, size) in banks_a(st):
                            if ct_ != ct:
                                continue
                            act.wait_ge(*ev.at("bank", n))
                            if ct or hd:
                                act.wait_ge(*ev.at("rtmp_done", l, hd if ct else hd - 1, 1 - ct))
                            if st["prev_head"] is not None:
                                act.wait_ge(*ev.at("pe_step", st["prev_head"]))
                                act.wait_ge(*ev.at("dve_step", st["prev_head"]))
                            nc.scalar.activation(rtmp[0:64, t0:t0 + size], psg[64:128, n % RING, 0:size], ACT.Copy).then_inc(
                                *ev.mark("act", "rsw", l, hd, ct, q))
                            nc.scalar.activation(rtmp[64:128, t0:t0 + size], psg[0:64, n % RING, 0:size], ACT.Copy).then_inc(
                                *ev.mark("act", "rsw", l, hd, ct, q))
                    act.wait_ge(*ev.at("logg", l))
                    if st["prev_head"] is not None:
                        act.wait_ge(*ev.at("dve_step", st["prev_head"]))
                        act.wait_ge(*ev.at("pool_step", st["prev_head"]))
                    for d in range(2):
                        g = small[:, 96 + d * 4 + hd:97 + d * 4 + hd]
                        nc.scalar.activation(rd[:, d, :], c("ahead" if d == 0 else "behind"), ACT.Exp, scale=g).then_inc(
                            *ev.mark("act", "rdec", l, hd))
                    act.wait_ge(*ev.at("rdecD", l, hd))
                    for d in range(2):
                        g = small[:, 96 + d * 4 + hd:97 + d * 4 + hd]
                        nc.scalar.activation(rd[:, 1 + d, :], c("row_f" if d == 0 else "row_b"), ACT.Exp, scale=g).then_inc(
                            *ev.mark("act", "rrow", l, hd))
                        nc.scalar.activation(small[:, 112 + d:113 + d], c("col_f" if d == 0 else "col_b"), ACT.Exp, scale=g).then_inc(
                            *ev.mark("act", "rcol", l, hd))
                        nc.scalar.activation(small[:, 114 + d:115 + d], c("cd"), ACT.Exp, scale=g).then_inc(
                            *ev.mark("act", "rcd", l, hd))
                elif kind == "rv":
                    for n, tt in banks_b(st):
                        act.wait_ge(*ev.at("bank", n))
                        if st["prev_head"] is not None:
                            act.wait_ge(*ev.at("pe_step", st["prev_head"]))
                            act.wait_ge(*ev.at("pool_step", st["prev_head"]))
                        ps = psg[:, n % RING, :].rearrange("p (j c) -> p j c", j=2)
                        nc.scalar.activation(rv[:, tt[0]:tt[0] + 2, :], ps, ACT.Copy).then_inc(
                            *ev.mark("act", "bank_free", n))
                        ev.now[("rv_sb", l, hd)] = {"act": ev.count["act"]}
                elif kind == "rg":
                    for n, tt in banks_b(st):
                        act.wait_ge(*ev.at("bank", n))
                        if st["prev_head"] is not None:
                            act.wait_ge(*ev.at("dve_step", st["prev_head"]))
                        ps = psg[:, n % RING, :].rearrange("p (j c) -> p j c", j=2)
                        nc.scalar.activation(rg[:, tt[0]:tt[0] + 2, :], ps, ACT.Tanh, scale=0.5).then_inc(
                            *ev.mark("act", "rgt", l, hd, tt[0]))
                elif kind == "rtiles":
                    n = len(st["tiles"])
                    for j in [i_ - 4 for i_ in st["ticks"] if i_ >= 4]:
                        t = st["tiles"][j]
                        act.wait_ge(*ev.at("ryT", l, hd, j))
                        for m in range(2):
                            nc.scalar.activation(yT[:, 2 * hd + m, t * P:(t + 1) * P],
                                                 psm[:, 1, m * P:(m + 1) * P], ACT.Copy,
                                                 scale=pr(l, "r_norm", 2 * hd + m)).then_inc(
                                *ev.mark("act", "yT", l, "r", t))
                        ev.now["ryT_sb", l, hd, j] = {"act": ev.count["act"]}
                elif kind == "up":
                    u, b = st["u"], st["u"] % 2
                    r0 = 1 if st["ctx"] else at_tile(CT)
                    if u >= 2:
                        act.wait_ge(*ev.at("fa_free", l, u - 2))
                    for n, ct, (q, t0, size) in banks_a(st):
                        act.wait_ge(*ev.at("bank", n))
                        if ct == 0:
                            a = at_tile(t0 // P)
                            nc.scalar.activation(fa[:, b, a:a + size], psg[:, n % RING, 0:size], ACT.Copy).then_inc(
                                *ev.mark("act", "bank_free", n))
                            ev.now[("fa", l, u)] = {"act": ev.count["act"]}
                        else:
                            if u:
                                act.wait_ge(*ev.at("u_", l, u - 1))
                            nc.scalar.activation(fb[:, t0:t0 + size], psg[:, n % RING, 0:size], ACT.Copy, scale=0.5).then_inc(
                                *ev.mark("act", "bank_free", n))
                            ev.now[("fb", l, u)] = {"act": ev.count["act"]}
                    act.wait_ge(*ev.at("fc", l, u))
                    if u:
                        act.wait_ge(*ev.at("u_", l, u - 1))
                    for q, t0, size in seqs[st["ctx"]]:
                        a = at_tile(t0 // P)
                        nc.scalar.activation(ft[:, t0:t0 + size], fc[:, a:a + size], ACT.Tanh, scale=0.5).then_inc(
                            *ev.mark("act", "ft", l, u))
                    act.wait_ge(*ev.at("u_", l, u))
                    if st["ring_free"] is not None:
                        act.wait_ge(*ev.at("w_free", st["ring_free"]))
                    t0 = 0 if st["ctx"] else CTX
                    nc.scalar.activation(uh[:, u % URING, t0:TOK], fu[:, t0:TOK], ACT.Copy).then_inc(
                        *ev.mark("act", "uh", l, u))
            for k in ("store0", "store1", "store2", "out0", "out1", "out2"):
                if ev.count.get(k, 0):
                    act.wait_ge(semaphore(k), ev.count[k])

        def head_norm(dve, x, cc, *key):
            dve.bn_stats(small[:, cc:cc + 6], x).then_inc(*ev.mark("dve", "hn"))
            dve.wait_ge(*ev.last("dve"))
            dve.bn_aggr(small[:, cc + 8:cc + 10], small[:, cc:cc + 6]).then_inc(*ev.mark("dve", "hn"))
            dve.wait_ge(*ev.last("dve"))
            dve.tensor_scalar(small[:, cc + 10:cc + 11], small[:, cc + 9:cc + 10], EPS, None, ALU.add).then_inc(
                *ev.mark("dve", *key))

        @block.vector
        def _(dve):
            V = nc.vector

            dve.wait_ge(*ev.at("cvec"))
            dve.wait_ge(*ev.at("tanh_c"))
            V.scalar_tensor_tensor(out=cvec[:, 1], in0=cvec[:, 1], scalar=1.0, in1=cvec[:, 0], op0=ALU.add,
                                      op1=ALU.mult).then_inc(*ev.mark("dve", "c1"))
            dve.wait_ge(*ev.last("dve"))
            V.tensor_scalar(cvec[:, 2], cvec[:, 1], 0.5, None, ALU.mult).then_inc(*ev.mark("dve", "silu_c"))
            dve.wait_ge(*ev.at("const"))
            dve.wait_ge(*ev.at("par"))
            for i, st in walk("dve"):
                kind, s = st["kind"], st["slot"]
                l, hd, t = st.get("l"), st.get("hd"), st.get("t")
                if kind == "region":
                    phase_end(dve, i)
                    if st["name"] == "mlstm":
                        for b in range(2):
                            for z in (0, at_tile(CT) - 2, at_tile(CT) - 1, PADDED - 1):
                                V.memset(ma[:, b, z:z + 1], 0.0).then_inc(*ev.mark("dve", "pads", i))
                        V.memset(mv[:, :, P:P + 1], 1.0).then_inc(*ev.mark("dve", "pads", i))
                if kind == "vector" and st["piece"] == 3:
                    dve.wait_ge(*ev.at("vrow", l, st["n"]))
                    V.tensor_copy(vrow[0:2, :], psg[0:2, st["bank"] % RING, 0:COLS]).then_inc(
                        *ev.mark("dve", "vrow_sb", l, st["n"]))
                if kind == "vector" and st["piece"] == 4:
                    n = st["bank"]
                    dve.wait_ge(*ev.at("bank", n))
                    m = st["n"] * 2
                    V.tensor_tensor(vec[:, l, m:m + 2, :], psg[:, n % RING, 0:4].rearrange("p (a b) -> p a b", a=2),
                                    pr(l, "mod_b", m, 2).rearrange("p (a b) -> p a b", b=1).broadcast_to((P, 2, 2)),
                                    ALU.add).then_inc(*ev.mark("dve", "bank_free", n))
                    ev.now[("vec", l, st["n"])] = {"dve": ev.count["dve"]}
                elif kind == "affine":
                    w = st["which"]
                    dve.wait_ge(*ev.last("dve"))
                    nw = pr(l, "norm1" if w == 0 else "norm2", 0, 8)
                    nwb = nw.rearrange("p (a b) -> p a b", b=1).broadcast_to((P, KD, 2))
                    V.scalar_tensor_tensor(out=aff[:, w, 0], in0=vec[:, l, (3 * w + 1) * KD:(3 * w + 2) * KD, :],
                                              scalar=1.0, in1=nwb, op0=ALU.add, op1=ALU.mult).then_inc(
                                                  *ev.mark("dve", "affine", l, w))
                    V.tensor_copy(aff[:, w, 1], vec[:, l, 3 * w * KD:(3 * w + 1) * KD, :]).then_inc(
                        *ev.mark("dve", "affine", l, w))
                elif kind == "gates":
                    dve.wait_ge(*ev.last("dve"))
                    for n, q, half in gate_banks(st):
                        dve.wait_ge(*ev.at("bank", n))
                        V.tensor_scalar(gate_b[:, q, half * 512:half * 512 + 512], psg[:, n % RING, :],
                                        1.0 if st["which"] else 0.5, None, ALU.mult).then_inc(
                            *ev.mark("dve", "bank_free", n))
                elif kind == "norms":
                    use, n = st["use"], len(st["tiles"])
                    w = 0 if use in ("first", "end") else 1
                    dve.wait_ge(*ev.last("dve"))
                    for k in [k for k in st["ticks"] if k <= n]:
                        cc = 4 * (k % 2)
                        if k < n:
                            t = st["tiles"][k]
                            sg = stage[:, k % 3]
                            dve.wait_ge(*ev.at("stage", st["gen"], k))
                            if use != "first":
                                V.tensor_tensor(sg, sg, acc[:, t, :], ALU.add).then_inc(
                                    *ev.mark("dve", "rsum", st["gen"], k))
                        if k >= 1 and use == "last":
                            sg = stage[:, (k - 1) % 3]
                            dve.wait_ge(*ev.at("rstd", st["gen"], k - 1))
                            dve.wait_ge(*ev.at("fnorm"))
                            V.scalar_tensor_tensor(out=sg, in0=sg, scalar=small[:, 4 - cc + 2:4 - cc + 3],
                                                   in1=bias_b[:], op0=ALU.mult, op1=ALU.mult).then_inc(
                                *ev.mark("dve", "outrow", st["gen"], k - 1))
                        if k >= 1 and use != "last":
                            q = int(st["tiles"][k - 1] >= CT)
                            j = k - 1
                            dve.wait_ge(*ev.at("xT", st["gen"], j))
                            if j >= 2:
                                dve.wait_ge(*ev.at("h", st["gen"], st["tiles"][j - 2]))
                            for kk in range(KD):
                                last = V.tensor_scalar(
                                    hf[:, j % 2, kk, :], psm[:, 2 * (j % 2) + kk // 4, (kk % 4) * P:(kk % 4 + 1) * P],
                                    aff[:, w, 0, kk, q:q + 1], aff[:, w, 1, kk, q:q + 1], ALU.mult, ALU.add)
                            last.then_inc(*ev.mark("dve", "hf", st["gen"], j))
                elif kind == "turns":
                    for k, t in enumerate(st["tiles"]):
                        ts = slice(t * P, (t + 1) * P)
                        for half in range(2):
                            dve.wait_ge(*ev.at("turn_hh", l, t, half))
                            ks = slice(half * 4, half * 4 + 4)
                            V.tensor_tensor(hl[:, ks, ts],
                                            psm[:, half + 2 * (k % 2), :].rearrange("p (k c) -> p k c", k=4),
                                            hh[:, ks, ts].bitcast(F32), ALU.subtract).then_inc(
                                *ev.mark("dve", "h", st["gen"], t))
                elif kind == "wout":
                    for n, tt in banks_b(st):
                        dve.wait_ge(*ev.at("bank", n))
                        dve.wait_ge(*ev.at("h", st["gen"], TILES - 1))
                        cs = slice(st["n"] * COLS, (st["n"] + 1) * COLS)
                        ps = psg[:, n % RING, :].rearrange("p (j c) -> p j c", j=2)
                        g_ = gate_b[:, int(tt[0] >= CT), cs].rearrange("p (j c) -> p j c", j=1)
                        g_ = g_.broadcast_to((P, 2, COLS))
                        V.tensor_tensor(acc[:, tt[0]:tt[0] + 2, cs], ps, g_, ALU.mult).then_inc(
                            *ev.mark("dve", "bank_free", n))
                elif kind == "down":
                    for j, t_ in enumerate(range(st["first"], TILES)):
                        n = st["bank"] + j
                        dve.wait_ge(*ev.at("bank", n))
                        cs = slice(st["half"] * 512, st["half"] * 512 + 512)
                        if st["g"] == 0:
                            V.tensor_copy(acc[:, t_, cs], psg[:, n % RING, :]).then_inc(
                                *ev.mark("dve", "bank_free", n))
                        else:
                            V.tensor_tensor(acc[:, t_, cs], acc[:, t_, cs], psg[:, n % RING, :], ALU.add).then_inc(
                                *ev.mark("dve", "bank_free", n))
                        if (st["g"] + 1) * GROUP >= FT:
                            dve.wait_ge(*ev.last("dve"))
                            V.tensor_tensor(acc[:, t_, cs], acc[:, t_, cs], gate_b[:, int(t_ >= CT), cs],
                                            ALU.mult).then_inc(*ev.mark("dve", "gated_sum"))
                elif kind == "up":
                    u, b = st["u"], st["u"] % 2
                    if u == 0:
                        for b_ in range(2):
                            for z in (0, at_tile(CT) - 2, at_tile(CT) - 1, PADDED - 1):
                                V.memset(fa[:, b_, z:z + 1], 0.0).then_inc(*ev.mark("dve", "fpads", l))
                    r0 = 1 if st["ctx"] else at_tile(CT)
                    r1 = PADDED - 1
                    dve.wait_ge(*ev.at("fa", l, u))
                    dve.wait_ge(*ev.last("dve"))
                    w = [pr(l, "f_conv", j * FT + u) for j in range(3)]
                    if u:
                        dve.wait_ge(*ev.at("ft", l, u - 1))
                    V.tensor_scalar(fc[:, r0:r1], fa[:, b, r0 - 1:r1 - 1], w[0], pr(l, "f_bias", u), ALU.mult,
                                       ALU.add).then_inc(*ev.mark("dve", "fc0"))
                    for j in (1, 2):
                        dve.wait_ge(*ev.last("dve"))
                        V.scalar_tensor_tensor(out=fc[:, r0:r1], in0=fa[:, b, r0 - 1 + j:r1 - 1 + j],
                                                  scalar=w[j], in1=fc[:, r0:r1], op0=ALU.mult, op1=ALU.add).then_inc(
                                                      *ev.mark("dve", "fc", l, u))
                    ev.now[("fa_free", l, u)] = {"dve": ev.count["dve"]}
                    dve.wait_ge(*ev.at("ft", l, u))
                    if u:
                        dve.wait_ge(*ev.at("uh", l, u - 1))
                        dve.wait_ge(*ev.at("u", l, u - 1))
                    for q, t0, size in seqs[st["ctx"]]:
                        a = at_tile(t0 // P)
                        V.scalar_tensor_tensor(out=fu[:, t0:t0 + size], in0=ft[:, t0:t0 + size], scalar=1.0,
                                                  in1=fc[:, a:a + size], op0=ALU.add, op1=ALU.mult).then_inc(
                                                      *ev.mark("dve", "fp"))
                    dve.wait_ge(*ev.at("fb", l, u))
                    dve.wait_ge(*ev.last("dve"))
                    t0 = 0 if st["ctx"] else CTX
                    V.tensor_tensor(fu[:, t0:], fu[:, t0:], fb[:, t0:], ALU.mult).then_inc(
                        *ev.mark("dve", "u_", l, u))
                elif kind == "mgates":
                    for n, _, (q, t0, size) in banks_a(st):
                        dve.wait_ge(*ev.at("bank", n))
                        V.tensor_copy(grow[0:16, t0:t0 + size], psg[0:16, n % RING, 0:size]).then_inc(
                            *ev.mark("dve", "bank_free", n))
                        ev.now[("grow", l)] = {"dve": ev.count["dve"]}
                    dve.wait_ge(*ev.at("gturned", l))
                    V.tensor_tensor(g16[:], psm[:, 3, 0:16 * TILES].rearrange("p (t g) -> p t g", t=TILES),
                                    pr(l, "gate", 0, 16).rearrange("p (a b) -> p a b", a=1).broadcast_to((P, TILES, 16)),
                                    ALU.add).then_inc(*ev.mark("dve", "g16"))
                    dve.wait_ge(*ev.last("dve"))
                    Fv = gm[:, 0, :].rearrange("p (d s h) -> p d s h", d=2, s=TILES)
                    Iv = gm[:, 11, :].rearrange("p (d s h) -> p d s h", d=2, s=TILES)
                    V.tensor_copy(Iv[:, 0], g16[:, :, 0:4]).then_inc(*ev.mark("dve", "gI"))
                    V.tensor_copy(Fv[:, 0], g16[:, :, 4:8]).then_inc(*ev.mark("dve", "gF"))
                    for s_, t_ in enumerate(BACK):
                        V.tensor_copy(Iv[:, 1, s_], g16[:, t_, 8:12]).then_inc(*ev.mark("dve", "gI"))
                        V.tensor_copy(Fv[:, 1, s_], g16[:, t_, 12:16]).then_inc(*ev.mark("dve", "Fx", l))
                    dve.wait_ge(*ev.at("lnf", l))
                    V.scalar_tensor_tensor(out=gm[:, 2, :], in0=gm[:, 0, :], scalar=0.0, in1=gm[:, 1, :],
                                              op0=ALU.min, op1=ALU.subtract).then_inc(
                                                  *ev.mark("dve", "logf", l))
                elif kind == "mgates2":
                    dve.wait_ge(*ev.at("sums", l))
                    V.tensor_tensor(gm[:, 4, :], gm[:, 11, :], psm[:, 3, 0:48], ALU.subtract).then_inc(
                        *ev.mark("dve", "A", l))
                    dve.wait_ge(*ev.at("AT", l))
                    V.tensor_copy(atr[0:24, 0:2, :], psm[0:24, 2, 0:2 * P].rearrange("p (a b) -> p a b", a=2)).then_inc(
                        *ev.mark("dve", "atr"))
                    dve.wait_ge(*ev.last("dve"))
                    for d in range(2):
                        V.tensor_tensor_scan(atr[0:24, 2 + d, :], atr[0:24, d, :], atr[0:24, d, :], NEG,
                                                ALU.max, ALU.max).then_inc(*ev.mark("dve", "scan", l))
                elif kind == "mgates3":
                    dve.wait_ge(*ev.at("LM", l))
                    V.tensor_copy(gm[:, 5, :], psm[:, 1, 0:48]).then_inc(*ev.mark("dve", "LMb", l))
                    dve.wait_ge(*ev.at("LMf", l))
                    V.tensor_copy(gm[:, 5, 24:48], psm[:, 1, 48:72]).then_inc(*ev.mark("dve", "LM2"))
                    dve.wait_ge(*ev.at("cmax", l))
                    v = {k: gm[:, k, :].rearrange("p (d s h) -> p d s h", d=2, s=TILES) for k in (0, 1, 3)}
                    g_ = psm[:, 3, 48:96].rearrange("p (d s h) -> p d s h", d=2, s=TILES)
                    V.memset(v[3][:, :, 0, :], 0.0).then_inc(*ev.mark("dve", "ms0"))
                    for s_ in range(TILES):
                        dve.wait_ge(*ev.last("dve"))
                        V.tensor_tensor(v[1][:, :, s_, :], v[3][:, :, s_, :], v[0][:, :, s_, :], ALU.max).then_inc(
                            *ev.mark("dve", "mm"))
                        if s_ < TILES - 1:
                            dve.wait_ge(*ev.last("dve"))
                            V.tensor_tensor(v[3][:, :, s_ + 1, :], v[1][:, :, s_, :], g_[:, :, s_, :], ALU.add).then_inc(
                                *ev.mark("dve", "mm"))
                    dve.wait_ge(*ev.last("dve"))
                    V.tensor_tensor(gm[:, 5, :], gm[:, 3, :], gm[:, 5, :], ALU.max).then_inc(
                        *ev.mark("dve", "M"))
                    dve.wait_ge(*ev.last("dve"))
                    V.tensor_tensor(gm[:, 6, :], gm[:, 4, :], gm[:, 1, :], ALU.subtract).then_inc(
                        *ev.mark("dve", "e"))
                    V.tensor_tensor(gm[:, 7, :], gm[:, 3, :], gm[:, 1, :], ALU.subtract).then_inc(
                        *ev.mark("dve", "e"))
                    V.tensor_tensor(gm[:, 8, :], gm[:, 3, :], gm[:, 5, :], ALU.subtract).then_inc(
                        *ev.mark("dve", "e"))
                    V.tensor_scalar(gm[:, 9, :], gm[:, 5, :], -1.0, None, ALU.mult).then_inc(
                        *ev.mark("dve", "negM", l))
                    dve.wait_ge(*ev.last("dve"))
                    V.tensor_tensor(gm[:, 10, :], gm[:, 9, :], psm[:, 3, 0:48], ALU.subtract).then_inc(
                        *ev.mark("dve", "mlogs", l))
                    dve.wait_ge(*ev.at("mexp", l))
                    V.tensor_scalar(gm[:, 6, :], gm[:, 6, :], M_SCALE, None, ALU.mult).then_inc(
                        *ev.mark("dve", "mcols", l))
                elif kind == "mqk":
                    for ct in range(2):
                        r0 = 1 if (st["ctx"] or ct == 1) else at_tile(CT)
                        r1 = PADDED - 1
                        dve.wait_ge(*ev.at("ma", l, hd, ct))
                        dve.wait_ge(*ev.last("dve"))
                        w = [pr(l, "conv_q" if ct == 0 else "conv_k", j * MH + hd) for j in range(3)]
                        V.tensor_scalar(mc[:, ct, r0:r1], ma[:, ct, r0 - 1:r1 - 1], w[0], None, ALU.mult).then_inc(
                            *ev.mark("dve", "c"))
                        for j in (1, 2):
                            dve.wait_ge(*ev.last("dve"))
                            V.scalar_tensor_tensor(out=mc[:, ct, r0:r1], in0=ma[:, ct, r0 - 1 + j:r1 - 1 + j],
                                                      scalar=w[j], in1=mc[:, ct, r0:r1], op0=ALU.mult,
                                                      op1=ALU.add).then_inc(*ev.mark("dve", "conv", l, hd, ct))
                    for ct in range(2):
                        r0 = 1 if (st["ctx"] or ct == 1) else at_tile(CT)
                        dve.wait_ge(*ev.at("mt_", l, hd, ct))
                        if st["prev_head"] is not None:
                            dve.wait_ge(*ev.at("pe_step", st["prev_head"]))
                        V.scalar_tensor_tensor(out=mqk[:, ct, r0:r1], in0=mt[:, ct, r0:r1], scalar=1.0,
                                                  in1=mc[:, ct, r0:r1], op0=ALU.add, op1=ALU.mult).then_inc(
                                                      *ev.mark("dve", "mqk", l, hd))
                    ev.now[("mt", l, hd)] = {"dve": ev.count["dve"]}
                elif kind in ("mstates", "rstates"):
                    r_ = kind[0]
                    if 1 in st["ticks"] and st["prev_head"] is not None:
                        dve.wait_ge(*ev.at("pe_step", st["prev_head"]))
                    if r_ == "m" and 1 in st["ticks"]:
                        V.memset(mcf[:, 0, :], 0.0).then_inc(*ev.mark("dve", "z"))
                        V.memset(mcb[:, 0, :], 0.0).then_inc(*ev.mark("dve", "z"))
                    for j in state_turns(st):
                        d, s_ = j % 2, j // 2
                        dve.wait_ge(*ev.at(r_ + "kv", l, hd, j))
                        dve.wait_ge(*ev.last("dve"))
                        if r_ == "m":
                            col = 24 * d + s_ * 4 + hd
                            x = mcb if d else mcf
                            V.scalar_tensor_tensor(out=x[:, s_ + 1, :], in0=x[:, s_, :], scalar=gm[:, 7, col:col + 1],
                                                   in1=psm[:, (0, 1, 4)[j % 3], 0:P + 1], op0=ALU.mult, op1=ALU.add).then_inc(
                                *ev.mark("dve", "mC", l, hd, j))
                            continue
                        x = rb if d else rf
                        if s_ == 0:
                            V.tensor_copy(x[:, 0, :], psm[:, (0, 1, 4)[j % 3], 0:RV]).then_inc(
                                *ev.mark("dve", "rC", l, hd, j))
                        else:
                            V.scalar_tensor_tensor(out=x[:, s_, :], in0=x[:, s_ - 1, :],
                                                   scalar=small[:, 114 + d:115 + d], in1=psm[:, (0, 1, 4)[j % 3], 0:RV],
                                                   op0=ALU.mult, op1=ALU.add).then_inc(
                                                       *ev.mark("dve", "rC", l, hd, j))
                elif kind == "mtiles":
                    n = len(st["tiles"])
                    for i_ in st["ticks"]:
                        j, k = i_ - 3, i_ - 4
                        tail, end = 0 <= j < n, 0 <= k < n
                        if tail:
                            t = st["tiles"][j]
                            cc = 16 + 24 * (j % 2)
                            cf, cb = t * 4 + hd, 24 + BACK.index(t) * 4 + hd
                            nd, y = mnd[:, j % 2], my[:, j % 2]
                            den, a, b = nd[:, 2:4, P], small[:, cc + 12:cc + 14], small[:, cc + 14:cc + 16]
                            dve.wait_ge(*ev.at("mintra_sb", l, hd, j))
                            dve.wait_ge(*ev.at("minter", l, hd, j))
                            for d, col in ((0, cf), (1, cb)):
                                V.scalar_tensor_tensor(out=nd[:, 2 + d, :], in0=psm[:, 2, d * (P + 1):(d + 1) * (P + 1)],
                                                       scalar=gm[:, 8, col:col + 1], in1=nd[:, d, :],
                                                       op0=ALU.mult, op1=ALU.add).then_inc(
                                    *ev.mark("dve", "mnd", l, hd, j))
                        if 1 <= i_ <= n:
                            m = i_ - 1
                            dve.wait_ge(*ev.at("mexpw", l, hd, m))
                            if m >= 2:
                                dve.wait_ge(*ev.at("mintra", l, hd, m - 2))
                            for d in range(2):
                                V.scalar_tensor_tensor(out=msc[:, m % 2, 2 + d, :], in0=psm[:, m % 2, 0:P],
                                                       scalar=M_SCALE, in1=msc[:, m % 2, d, :], op0=ALU.mult,
                                                       op1=ALU.mult).then_inc(*ev.mark("dve", "mw", l, hd, m))
                        if tail:
                            dve.wait_ge(*ev.at("mnd", l, hd, j))
                            V.scalar_tensor_tensor(out=a, in0=den, scalar=-1.0, in1=den, op0=ALU.mult,
                                                   op1=ALU.max).then_inc(*ev.mark("dve", "mabs", l, hd, j))
                        if end:
                            ce = 16 + 24 * (k % 2)
                            ye = my[:, k % 2]
                            dve.wait_ge(*ev.at("mrstd", l, hd, k))
                            V.tensor_scalar(ye[:, 1, :], ye[:, 1, :], small[:, ce + 8:ce + 9],
                                            small[:, ce + 11:ce + 12], ALU.subtract, ALU.mult).then_inc(
                                *ev.mark("dve", "mnormed", l, hd, k))
                        if tail:
                            dve.wait_ge(*ev.at("mabs", l, hd, j))
                            V.tensor_tensor(a[:, 0:1], a[:, 0:1], gm[:, 10, cf:cf + 1], ALU.max).then_inc(
                                *ev.mark("dve", "mden", l, hd, j))
                            V.tensor_tensor(a[:, 1:2], a[:, 1:2], gm[:, 10, cb:cb + 1], ALU.max).then_inc(
                                *ev.mark("dve", "mden", l, hd, j))
                        if end:
                            dve.wait_ge(*ev.at("mnormed", l, hd, k))
                            dve.wait_ge(*ev.at("mo_gate", l, hd))
                            if k >= 2:
                                dve.wait_ge(*ev.at("myT", l, hd, k - 2))
                            V.tensor_tensor(ye[:, 2, :], ye[:, 1, :], mo[:, st["tiles"][k], :], ALU.mult).then_inc(
                                *ev.mark("dve", "my", l, hd, k))
                        if tail:
                            dve.wait_ge(*ev.at("mden", l, hd, j))
                            V.reciprocal(b, a).then_inc(*ev.mark("dve", "mrec", l, hd, j))
                        if i_ < n:
                            tq = st["tiles"][i_]
                            dve.wait_ge(*ev.at("mscore", l, hd, i_))
                            for d, col in ((0, tq * 4 + hd), (1, 24 + BACK.index(tq) * 4 + hd)):
                                V.scalar_tensor_tensor(out=msc[:, i_ % 2, d, :],
                                                       in0=psm[:, i_ % 2, (1 + d) * P:(2 + d) * P],
                                                       scalar=gm[:, 4, col:col + 1],
                                                       in1=c("hide_f" if d == 0 else "hide_b"), op0=ALU.add,
                                                       op1=ALU.add).then_inc(*ev.mark("dve", "marg", l, hd, i_))
                        if tail:
                            dve.wait_ge(*ev.at("mrec", l, hd, j))
                            V.tensor_scalar(y[:, 0, :], nd[:, 2, 0:P], b[:, 0:1], None, ALU.mult).then_inc(
                                *ev.mark("dve", "d"))
                            dve.wait_ge(*ev.last("dve"))
                            V.scalar_tensor_tensor(out=y[:, 1, :], in0=nd[:, 3, 0:P], scalar=b[:, 1:2], in1=y[:, 0, :],
                                                   op0=ALU.mult, op1=ALU.add).then_inc(*ev.mark("dve", "d"))
                            dve.wait_ge(*ev.last("dve"))
                            head_norm(dve, y[:, 1, :], cc, "mvar", l, hd, j)
                elif kind == "branch":
                    first = st["br"] == "m"
                    cs = slice(st["n"] * COLS, (st["n"] + 1) * COLS)
                    for j, (n, tt) in enumerate(banks_b(st)):
                        dve.wait_ge(*ev.at("bank", n))
                        dve.wait_ge(*ev.at("tg", l, st["br"], st["n"], tt[0]))
                        ps = psg[:, n % RING, :].rearrange("p (j c) -> p j c", j=2)
                        dst = acc[:, tt[0]:tt[0] + 2, cs] if first else \
                            bt[:, n % 2, :].rearrange("p (j c) -> p j c", j=2)
                        if not first:
                            if st["prev_branch"] is not None:
                                dve.wait_ge(*ev.at("pool_step", st["prev_branch"]))
                            if j == 2:
                                dve.wait_ge(*ev.at("summed", n - 2))
                        V.scalar_tensor_tensor(out=dst, in0=gate_place(st, tt[0]), scalar=1.0, in1=ps,
                                                  op0=ALU.add, op1=ALU.mult).then_inc(
                                                      *ev.mark("dve", "bank_free", n))
                        ev.now[("gated", l, st["br"], st["n"], tt[0])] = {"dve": ev.count["dve"]}
                elif kind == "arot":
                    g = st["g"]
                    for ct in range(1 + (g < 2)):
                        x = ak[:, CTX:TOK] if g == 2 else aq[:, 2 * g + ct, CTX:TOK]
                        dve.wait_ge(*ev.at("arot", l, g, ct))
                        dve.wait_ge(*ev.at("rope", st["region"]))
                        dve.wait_ge(*ev.last("dve"))
                        V.tensor_tensor(atmp[:], psm[:, 2 * g + ct, 0:SEQ], ropea[:, 1, :], ALU.mult).then_inc(
                            *ev.mark("dve", "amix_", l, g, ct))
                        V.tensor_tensor(x, x, ropea[:, 0, :], ALU.mult).then_inc(*ev.mark("dve", "x"))
                        dve.wait_ge(*ev.last("dve"))
                        V.tensor_tensor(x, x, atmp[:], ALU.add).then_inc(*ev.mark("dve", "arope", l))
                elif kind == "attend":
                    n = len(st["heads"])
                    for i_ in st["ticks"]:
                        if i_ < n:
                            t, hd = st["heads"][i_]
                            b, s0 = i_ % 4, 64 + 8 * (i_ % 4)
                            nw = len(akeys(t)) - 2
                            dve.wait_ge(*ev.at("ascore", l, i_))
                            if i_ >= 4:
                                dve.wait_ge(*ev.at("apT", l, i_ - 4))
                            if nw:
                                c0 = (max(CT, t - 1) - (t - 1)) * P
                                V.scalar_tensor_tensor(out=asb[:, b, 0:nw * P], in0=psm[:, 0, 0:nw * P],
                                                       scalar=AD ** -0.5, in1=c("window")[:, c0:c0 + nw * P],
                                                       op0=ALU.mult, op1=ALU.add).then_inc(*ev.mark("dve", "a"))
                            V.tensor_scalar(asb[:, b, nw * P:(nw + 2) * P], psm[:, 1, 0:CTX], AD ** -0.5, None,
                                            ALU.mult).then_inc(*ev.mark("dve", "as", l, i_))
                        if 2 <= i_ <= n + 1:
                            s2 = 64 + 8 * ((i_ - 2) % 4)
                            dve.wait_ge(*ev.at("ap", l, i_ - 2))
                            V.tensor_tensor(small[:, s2 + 4:s2 + 5], small[:, s2 + 2:s2 + 3], small[:, s2 + 3:s2 + 4],
                                            ALU.add).then_inc(*ev.mark("dve", "asum", l, i_ - 2))
                        if i_ < n:
                            dve.wait_ge(*ev.at("as", l, i_))
                            V.tensor_reduce(small[:, s0:s0 + 1], asb[:, b, 0:(nw + 2) * P], AX.X, ALU.max).then_inc(
                                *ev.mark("dve", "amax", l, i_))
                        if 2 <= i_ <= n + 1:
                            dve.wait_ge(*ev.at("asum", l, i_ - 2))
                            V.reciprocal(small[:, s2 + 5:s2 + 6], small[:, s2 + 4:s2 + 5]).then_inc(
                                *ev.mark("dve", "ard", l, i_ - 2))
                        if i_ < n:
                            dve.wait_ge(*ev.at("amax", l, i_))
                            V.tensor_scalar(small[:, s0 + 1:s0 + 2], small[:, s0:s0 + 1], pr(l, "sink", hd), -1.0,
                                            ALU.max, ALU.mult).then_inc(*ev.mark("dve", "anm", l, i_))
                        if i_ >= 3:
                            j = i_ - 3
                            t, hd = st["heads"][j]
                            s0 = 64 + 8 * (j % 4)
                            dve.wait_ge(*ev.at("apv", l, j))
                            dve.wait_ge(*ev.at("ard", l, j))
                            V.tensor_scalar(ay[:, t % 2, hd * AD:(hd + 1) * AD], psm[:, 4, 0:AD],
                                            small[:, s0 + 5:s0 + 6], None, ALU.mult).then_inc(
                                *ev.mark("dve", "ay", l, j))
                elif kind == "rqk":
                    if hd == 0:
                        dve.wait_ge(*ev.last("dve"))
                        x = small[:, 104:112]
                        dve.wait_ge(*ev.at("rabs", l))
                        V.scalar_tensor_tensor(out=small[:, 96:104], in0=pr(l, "ret", 0, 8), scalar=0.0,
                                                  in1=x, op0=ALU.min, op1=ALU.subtract).then_inc(
                                                      *ev.mark("dve", "logg", l))
                    for ct in (0, 1):
                        for n, ct_, (q, t0, size) in banks_a(st):
                            if ct_ != ct:
                                continue
                            dve.wait_ge(*ev.at("bank", n))
                            dve.wait_ge(*ev.at("rope", st["region"]))
                            if st["prev_head"] is not None:
                                dve.wait_ge(*ev.at("pe_step", st["prev_head"]))
                                dve.wait_ge(*ev.at("pool_step", st["prev_head"]))
                            dve.wait_ge(*ev.at("rsw", l, hd, ct, q))
                            x = rqk[:, ct, t0:t0 + size]
                            V.tensor_tensor(x, psg[:, n % RING, 0:size], roper[:, 0, t0:t0 + size], ALU.mult).then_inc(
                                *ev.mark("dve", "bank_free", n))
                            V.tensor_tensor(rtmp[:, t0:t0 + size], rtmp[:, t0:t0 + size],
                                               roper[:, 1, t0:t0 + size], ALU.mult).then_inc(
                                                   *ev.mark("dve", "r"))
                            dve.wait_ge(*ev.last("dve"))
                            V.tensor_tensor(x, x, rtmp[:, t0:t0 + size], ALU.add).then_inc(
                                *ev.mark("dve", "rqk", l, hd))
                        ev.now[("rtmp_done", l, hd, ct)] = {"dve": ev.count["dve"]}
                    dve.wait_ge(*ev.at("rdec", l, hd))
                    V.scalar_tensor_tensor(out=rd[:, 0, :], in0=rd[:, 0, :], scalar=R_SCALE, in1=c("upto"),
                                              op0=ALU.mult, op1=ALU.mult).then_inc(*ev.mark("dve", "r"))
                    V.scalar_tensor_tensor(out=rd[:, 1, :], in0=rd[:, 1, :], scalar=R_SCALE, in1=c("since"),
                                              op0=ALU.mult, op1=ALU.mult).then_inc(*ev.mark("dve", "r"))
                    dve.wait_ge(*ev.last("dve"))
                    V.tensor_tensor(rd[:, 0, :], rd[:, 0, :], rd[:, 1, :], ALU.add).then_inc(
                        *ev.mark("dve", "rdecD", l, hd))
                    dve.wait_ge(*ev.at("rcd", l, hd))
                    V.tensor_scalar(small[:, 116:118], small[:, 112:114], R_SCALE, None, ALU.mult).then_inc(
                        *ev.mark("dve", "rw", l, hd))
                elif kind == "rg":
                    for n, tt in banks_b(st):
                        dve.wait_ge(*ev.at("rgt", l, hd, tt[0]))
                        ps = psg[:, n % RING, :].rearrange("p (j c) -> p j c", j=2)
                        x = rg[:, tt[0]:tt[0] + 2, :]
                        V.scalar_tensor_tensor(out=x, in0=x, scalar=1.0, in1=ps, op0=ALU.add, op1=ALU.mult).then_inc(
                            *ev.mark("dve", "bank_free", n))
                        ev.now[("rg_sb", l, hd)] = {"dve": ev.count["dve"]}
                elif kind == "rtiles":
                    n = len(st["tiles"])
                    for i_ in st["ticks"]:
                        if i_ < n:
                            dve.wait_ge(*ev.at("rscore", l, hd, i_))
                            if i_ >= 2:
                                dve.wait_ge(*ev.at("rout", l, hd, i_ - 2))
                            V.tensor_tensor(rs[:, i_ % 2, 0, :], psm[:, 0, 0:P], rd[:, 0, :], ALU.mult).then_inc(
                                *ev.mark("dve", "rs", l, hd, i_))
                        if 2 <= i_ <= n + 1:
                            j = i_ - 2
                            o = psm[:, 2 + j % 3, 0:RV]
                            dve.wait_ge(*ev.at("rout", l, hd, j))
                            head_norm(dve, o, 16 + 24 * (j % 2), "rvar", l, hd, j)
                        if 3 <= i_ <= n + 2:
                            j = i_ - 3
                            t = st["tiles"][j]
                            cc = 16 + 24 * (j % 2)
                            o = psm[:, 2 + j % 3, 0:RV]
                            dve.wait_ge(*ev.at("rrstd", l, hd, j))
                            V.tensor_scalar(ry[:, j % 2, 0, :], o, small[:, cc + 8:cc + 9], small[:, cc + 11:cc + 12],
                                            ALU.subtract, ALU.mult).then_inc(
                                                *ev.mark("dve", "rnormed", l, hd, j))
                            dve.wait_ge(*ev.last("dve"))
                            dve.wait_ge(*ev.at("rg_sb", l, hd))
                            if j >= 2:
                                dve.wait_ge(*ev.at("ryT", l, hd, j - 2))
                            V.scalar_tensor_tensor(out=ry[:, j % 2, 1, :], in0=ry[:, j % 2, 0, :], scalar=0.5,
                                                   in1=rg[:, t, :], op0=ALU.mult, op1=ALU.mult).then_inc(
                                *ev.mark("dve", "ry", l, hd, j))
        @block.gpsimd
        def _(pool):
            G = nc.gpsimd

            pool.wait_ge(*ev.at("const"))
            for i, st in walk("pool"):
                kind, s = st["kind"], st["slot"]
                l, hd, t = st.get("l"), st.get("hd"), st.get("t")
                if kind == "region":
                    phase_end(pool, i)
                if kind == "split":
                    n = s["kt"] * s["cols"]
                    pool.wait_ge(*ev.at("head", s["n"]))
                    G.tensor_tensor(wl[:, s["sp"] % 2, 0:n], raw[:, s["n"] % 2, 0:n],
                                       wh[:, s["sp"] % 2, 0:n].bitcast(F32), ALU.subtract).then_inc(
                                           *ev.mark("pool", "rest", s["n"]))
                    ev.now[("raw_free", s["n"])] = {"pool": ev.count["pool"]}
                elif kind == "ysplit":
                    for t in st["tiles"]:
                        ts = slice(t * P, (t + 1) * P)
                        pool.wait_ge(*ev.at("yh", l, st["br"], t))
                        G.tensor_tensor(yl[:, 0:st["kt"], ts], yT[:, 0:st["kt"], ts],
                                        yh[:, 0:st["kt"], ts].bitcast(F32), ALU.subtract).then_inc(
                            *ev.mark("pool", "ysplit", l, st["br"], t))
                elif kind == "norms":
                    n = len(st["tiles"])
                    for k in st["ticks"]:
                        cc = 4 * (k % 2)
                        if k < n:
                            pool.wait_ge(*ev.at("ss", st["gen"], k))
                            G.tensor_scalar(small[:, cc + 1:cc + 2], small[:, cc:cc + 1], 1.0 / D, EPS, ALU.mult,
                                            ALU.add).then_inc(*ev.mark("pool", "ms", st["gen"], k))
                            pool.wait_ge(*ev.at("ms", st["gen"], k))
                            G.tensor_tensor(small[:, cc + 2:cc + 3], small[:, cc + 1:cc + 2], c("neg_half"),
                                            ALU.pow).then_inc(*ev.mark("pool", "rstd", st["gen"], k))
                        if k >= 2 and st["use"] != "last":
                            t = st["tiles"][k - 2]
                            ts = slice(t * P, (t + 1) * P)
                            pool.wait_ge(*ev.at("hh", st["gen"], k - 2))
                            G.tensor_tensor(hl[:, :, ts], hf[:, k % 2], hh[:, :, ts].bitcast(F32),
                                            ALU.subtract).then_inc(*ev.mark("pool", "h", st["gen"], t))
                elif kind == "up":
                    u = st["u"]
                    pool.wait_ge(*ev.at("uh", l, u))
                    t0 = 0 if st["ctx"] else CTX
                    G.tensor_tensor(ul[:, u % URING, t0:TOK], fu[:, t0:TOK],
                                       uh[:, u % URING, t0:TOK].bitcast(F32), ALU.subtract).then_inc(
                                           *ev.mark("pool", "u", l, u))
                elif kind == "mgates2":
                    pool.wait_ge(*ev.at("A", l))
                    G.partition_all_reduce(gm[:, 0, :], gm[:, 4, :], P, bass.bass_isa.ReduceOp.max).then_inc(
                        *ev.mark("pool", "cmax", l))
                elif kind in ("mstates", "rstates"):
                    r_ = kind[0]
                    for j in state_turns(st):
                        if j % 2 == 0:
                            weigh_values(pool, "pool", lambda o_, x_, w_: G.tensor_scalar(
                                o_, x_, w_, None, ALU.mult), st, j)
                    if r_ == "m" and 3 in st["ticks"]:
                        pool.wait_ge(*ev.at("mo", l, hd))
                        m0 = 0 if st["ctx"] else CT
                        G.tensor_scalar(mo[:, m0:, :], mo[:, m0:, :], 1.0, 0.5, ALU.add, ALU.mult).then_inc(
                            *ev.mark("pool", "mo_gate", l, hd))
                elif kind in ("mtiles", "rtiles"):
                    n = len(st["tiles"])
                    for i_ in st["ticks"]:
                        if i_ < n and kind == "rtiles":
                            t = st["tiles"][i_]
                            pool.wait_ge(*ev.at("rqk", l, hd))
                            pool.wait_ge(*ev.at("rrow", l, hd))
                            if i_ >= 2:
                                pool.wait_ge(*ev.at("rout", l, hd, i_ - 2))
                            for d in range(2):
                                G.tensor_tensor(rs[:, i_ % 2, 1 + d, :], rqk[:, 0, t * P:(t + 1) * P],
                                                rd[:, 1 + d, :], ALU.mult).then_inc(
                                                    *ev.mark("pool", "rq", l, hd, i_))
                        lag = 3 if kind == "mtiles" else 2
                        if lag <= i_ < n + lag:
                            j = i_ - lag
                            cc = 16 + 24 * (j % 2)
                            pool.wait_ge(*ev.at(kind[0] + "var", l, hd, j))
                            G.tensor_tensor(small[:, cc + 11:cc + 12], small[:, cc + 10:cc + 11], c("neg_half"),
                                            ALU.pow).then_inc(*ev.mark("pool", kind[0] + "rstd", l, hd, j))
                if kind == "branch" and st["br"] != "m":
                    cs = slice(st["n"] * COLS, (st["n"] + 1) * COLS)
                    for n, tt in banks_b(st):
                        pool.wait_ge(*ev.at("gated", l, st["br"], st["n"], tt[0]))
                        x = acc[:, tt[0]:tt[0] + 2, cs]
                        G.tensor_tensor(x, x, bt[:, n % 2, :].rearrange("p (j c) -> p j c", j=2), ALU.add).then_inc(
                            *ev.mark("pool", "summed", n))
        return ev.now


def arena_offset(nc, arena):
    return nc.sbuf_base - ARENA_BYTES


def build(bacc, args, shape):
    known = None
    for _ in range(2):
        nc = bacc.Bacc("TRN2", target_bir_lowering=False, num_devices=1)
        ins = {k: nc.dram_tensor(f"in_{k}", v.shape, F32, kind="ExternalInput").ap() for k, v in args.items()}
        out = nc.dram_tensor("out", shape, F32, kind="ExternalOutput").ap()
        known = backbone(nc, ins, out, known)
    return nc


def layout(inputs):
    consts, _, rope_a, rope_r = constants()
    PP, NPAR = param_places()
    plan, stream = make_plan()
    g = {k: np.ascontiguousarray(v) for k, v in inputs.items()}
    flat = np.empty(sum(s["kt"] * s["cols"] * P for s in stream), np.float32)
    off = 0
    for s in stream:
        name, row, cols = s["blocks"]
        w = g[name][s["l"], row:row + s["kt"] * P]
        w = np.concatenate([w[:, a:a + n] for a, n in cols], 1)
        n = w.size
        flat[off:off + n] = w.reshape(s["kt"], P, -1).transpose(1, 0, 2).ravel()
        off += n
    par = np.empty((P, DEPTH, NPAR), np.float32)
    for l in range(DEPTH):
        tap = g["m_conv_w"][l]
        rows = {
            "mod_b": g["mod_b"][l], "norm1": g["norm1_w"][l], "norm2": g["norm2_w"][l],
            "conv_q": tap[:, :MH * P].ravel(), "conv_k": tap[:, MH * P:].ravel(), "m_norm": g["m_norm_w"][l],
            "r_norm": g["ret_norm_w"][l], "f_conv": g["ffn_conv_w"][l].ravel(), "f_bias": g["ffn_conv_b"][l]}
        for k, v in rows.items():
            a, n = PP[k]
            par[:, l, a:a + n] = v.reshape(n, P).T
        for k, v in (("sink", g["a_sink"][l]), ("ret", g["ret_logit"][l].ravel()), ("gate", g["m_gate_bias"][l])):
            a, n = PP[k]
            par[:, l, a:a + n] = v[None, :]
    cvec = np.stack([g["c_ctx"].reshape(KD, P), g["c"][0].reshape(KD, P)], 0).transpose(2, 1, 0)
    return {"stream": flat, "consts": consts, "params": par, "cvec": np.ascontiguousarray(cvec),
            "rope_a": rope_a, "rope_r": rope_r, "mod_b": g["mod_b"], "final_w": g["final_norm_w"][None, :],
            "x": g["x"], "ctx": g["ctx"]}


def kernel(**inputs):
    from concourse.bass_utils import run_bass_kernel_spmd as run
    import concourse.bacc as bacc
    args = layout(inputs)
    nc = build(bacc, args, inputs["x"].shape)
    r = run(nc, [{f"in_{k}": v for k, v in args.items()}], core_ids=[0])
    return r.results[0]["out"]
```
